# Optimizing a Trainium2 kernel written in Bass

```python
import jax, jax.numpy as jnp
from jax import lax
import numpy as np

D_MODEL = 1024
BATCH = 1
SEQ = 512
DEPTH = 1

RWKV_HEADS = 8
RWKV_HEAD_DIM = 64
RWKV_WIDTH = RWKV_HEADS * RWKV_HEAD_DIM
DECAY_LORA = 32
ICLR_LORA = 32
VRES_LORA = 32
GATE_LORA = 96
SGU_GROUPS = 4
SGU_WIDTH = 256
SGU_CHUNK = 128
CONV_WIDTH = 256
CONV_KERNEL = 31
N_BRANCHES = 3

OFF_R = 0
OFF_K = OFF_R + RWKV_WIDTH
OFF_V = OFF_K + RWKV_WIDTH
OFF_WL = OFF_V + RWKV_WIDTH
OFF_AL = OFF_WL + DECAY_LORA
OFF_GL = OFF_AL + ICLR_LORA
RWKV_COLS = OFF_GL + GATE_LORA
OFF_SGU = RWKV_COLS
OFF_CONV = OFF_SGU + 2 * SGU_WIDTH
OFF_GATE = OFF_CONV + 2 * CONV_WIDTH
IN_COLS = OFF_GATE + N_BRANCHES * D_MODEL
OFF_VRES = IN_COLS

N_EXPERTS = 32
N_GROUPS = 4
EXPERTS_PER_GROUP = N_EXPERTS // N_GROUPS
TOP_K = 2
D_EXPERT = 512
EXPERT_BLOCK = 256

ALPHA = (2 * DEPTH) ** 0.25
BETA = (8 * DEPTH) ** -0.25
LN_EPS = 1e-5
GN_EPS = 64e-5

kernel_name = 'hybrid_rwkv7_sgu_conformer_grouped_moe'

def layer_norm(x, g, b):
    xf = x.astype(jnp.float32)
    mu = jnp.mean(xf, axis=-1, keepdims=True)
    var = jnp.mean(jnp.square(xf - mu), axis=-1, keepdims=True)
    return ((xf - mu) * lax.rsqrt(var + LN_EPS)).astype(x.dtype) * g + b

def token_shift_mix(p, mu):
    prev = jnp.pad(p, ((0, 0), (1, 0), (0, 0)))[:, :-1]
    return p + (prev - p) * mu

def wkv7_scan(r, decay, k, v, a, b):
    bsz, _, h, n = r.shape

    def step(state, inp):
        r_t, w_t, k_t, v_t, a_t, b_t = inp
        sa = jnp.einsum('bhvk,bhk->bhv', state, a_t)
        state = (state * w_t[:, :, None, :] + sa[..., None] * b_t[:, :, None, :]
                 + v_t[..., None] * k_t[:, :, None, :])
        return state, jnp.einsum('bhvk,bhk->bhv', state, r_t)

    xs = tuple(jnp.moveaxis(t, 1, 0) for t in (r, decay, k, v, a, b))
    _, y = lax.scan(step, jnp.zeros((bsz, h, n, n), jnp.float32), xs)
    return jnp.moveaxis(y, 0, 1)

def rwkv7_branch(r, k, v, wl, al, gl, w0, w_up, a0, a_up, g_up, k_k, k_a, r_k, gn_g, gn_b, w_o):
    f32 = jnp.float32
    bsz, seq, _ = r.shape

    def heads(t):
        return t.astype(f32).reshape(bsz, seq, RWKV_HEADS, RWKV_HEAD_DIM)

    w_log = -jax.nn.softplus(-(w0 + jnp.tanh(wl) @ w_up)) - 0.5
    decay = jnp.exp(-jnp.exp(heads(w_log)))
    iclr = jax.nn.sigmoid(a0 + al @ a_up)
    gate = jax.nn.sigmoid(gl) @ g_up
    kk = heads(k * k_k)
    kk = kk / jnp.maximum(jnp.sqrt(jnp.sum(kk * kk, axis=-1, keepdims=True)), 1e-12)
    kh = heads(k * (1 + (iclr - 1) * k_a))
    rh, vh, ah = heads(r), heads(v), heads(iclr)
    y = wkv7_scan(rh, decay, kh, vh, -kk, kk * ah)
    mu = jnp.mean(y, axis=-1, keepdims=True)
    var = jnp.mean(jnp.square(y - mu), axis=-1, keepdims=True)
    hn = (RWKV_HEADS, RWKV_HEAD_DIM)
    yn = (y - mu) * lax.rsqrt(var + GN_EPS) * gn_g.astype(f32).reshape(hn) + gn_b.astype(f32).reshape(hn)
    bonus = jnp.sum(rh * kh * r_k.astype(f32), axis=-1, keepdims=True) * vh
    out = (yn + bonus).reshape(bsz, seq, RWKV_WIDTH).astype(r.dtype) * gate
    return out @ w_o

def sgu_branch(pb, ln_g, ln_b, w_s, b_s, w_o):
    z = jax.nn.gelu(pb, approximate=False)
    u, v = z[..., :SGU_WIDTH], z[..., SGU_WIDTH:]
    v = layer_norm(v, ln_g, ln_b)
    bsz, seq, _ = v.shape
    vg = v.reshape(bsz, seq // SGU_CHUNK, SGU_CHUNK, SGU_GROUPS, SGU_WIDTH // SGU_GROUPS)
    causal = jnp.tril(jnp.ones((SGU_CHUNK, SGU_CHUNK), dtype=bool))
    w_c = jnp.where(causal, w_s, 0)
    mixed = jnp.einsum('gpq,bcqgd->bcpgd', w_c, vg) + jnp.transpose(b_s)[:, :, None]
    return (u * mixed.reshape(bsz, seq, SGU_WIDTH)) @ w_o

def conv_branch(pc, dw_kernel, dw_bias, ln_g, ln_b, w_o):
    h = pc[..., :CONV_WIDTH] * jax.nn.sigmoid(pc[..., CONV_WIDTH:])
    h = lax.conv_general_dilated(
        h, dw_kernel[:, None, :], window_strides=(1,), padding=[(CONV_KERNEL - 1, 0)],
        dimension_numbers=('NWC', 'WIO', 'NWC'), feature_group_count=CONV_WIDTH) + dw_bias
    h = jax.nn.silu(layer_norm(h, ln_g, ln_b))
    return h @ w_o

def grouped_moe(x, router_w, router_b, w_gate, w_up, w_down):
    bsz, seq, d = x.shape
    t = bsz * seq
    xf = x.reshape(t, d)
    scores = jax.nn.sigmoid((xf @ router_w).astype(jnp.float32))
    sel = (scores + router_b.astype(jnp.float32)).reshape(t, N_GROUPS, EXPERTS_PER_GROUP)
    group_score = jnp.sum(lax.top_k(sel, TOP_K)[0], axis=-1)
    grp = jnp.argmax(group_score, axis=-1)
    sel_in = jnp.take_along_axis(sel, grp[:, None, None], axis=1)[:, 0]
    _, local = lax.top_k(sel_in, TOP_K)
    expert = grp[:, None] * EXPERTS_PER_GROUP + local
    gate = jnp.take_along_axis(scores, expert, axis=1)
    gate = gate / jnp.sum(gate, axis=-1, keepdims=True)
    tk = t * TOP_K
    flat_e = expert.reshape(tk)
    flat_tok = jnp.repeat(jnp.arange(t, dtype=jnp.int32), TOP_K)
    flat_g = gate.reshape(tk)
    order = jnp.argsort(flat_e)
    e_sorted = flat_e[order]
    counts = jnp.bincount(flat_e, length=N_EXPERTS)
    padded = (counts + EXPERT_BLOCK - 1) // EXPERT_BLOCK * EXPERT_BLOCK
    pad_end = jnp.cumsum(padded)
    pad_start = pad_end - padded
    start = jnp.cumsum(counts) - counts
    dest = pad_start[e_sorted] + jnp.arange(tk, dtype=jnp.int32) - start[e_sorted]
    n_blocks = (tk + EXPERT_BLOCK - 1) // EXPERT_BLOCK + N_EXPERTS
    rows = n_blocks * EXPERT_BLOCK
    buf_tok = jnp.full((rows,), t, jnp.int32).at[dest].set(flat_tok[order])
    buf_gate = jnp.zeros((rows,), jnp.float32).at[dest].set(flat_g[order])
    block_expert = jnp.clip(
        jnp.searchsorted(pad_end, jnp.arange(n_blocks, dtype=jnp.int32) * EXPERT_BLOCK, side='right'),
        0, N_EXPERTS - 1)
    xb = jnp.take(xf, buf_tok, axis=0, mode='fill', fill_value=0).reshape(n_blocks, EXPERT_BLOCK, d)

    def expert_block(args):
        xblk, e = args
        h = jax.nn.silu(xblk @ w_gate[e]) * (xblk @ w_up[e])
        return h @ w_down[e]

    yb = lax.map(expert_block, (xb, block_expert)).reshape(rows, d)
    y = jnp.zeros((t, d), yb.dtype).at[buf_tok].add(yb * buf_gate[:, None].astype(yb.dtype), mode='drop')
    return y.reshape(bsz, seq, d)

def setup_inputs(seed: int = 0) -> dict:
    key = jax.random.key(seed)
    ks = iter(jax.random.split(key, 48))

    def nrm(shape, scale):
        return jax.random.normal(next(ks), shape, jnp.float32) * scale

    def uni(shape, lo, hi):
        return jax.random.uniform(next(ks), shape, jnp.float32, lo, hi)

    d, L = D_MODEL, DEPTH
    return {
        'x': nrm((BATCH, SEQ, d), 1.0),
        'w_in_first': nrm((d, IN_COLS), d ** -0.5),
        'w_in_rest': nrm((L - 1, d, IN_COLS + VRES_LORA), d ** -0.5),
        'rwkv_mu': uni((L, RWKV_COLS), 0.0, 1.0),
        'rwkv_mu_vres': uni((L - 1, VRES_LORA), 0.0, 1.0),
        'rwkv_w0': uni((L, RWKV_WIDTH), -5.0, 0.0),
        'rwkv_w_up': nrm((L, DECAY_LORA, RWKV_WIDTH), 0.5 * DECAY_LORA ** -0.5),
        'rwkv_a0': nrm((L, RWKV_WIDTH), 0.5),
        'rwkv_a_up': nrm((L, ICLR_LORA, RWKV_WIDTH), 0.5 * ICLR_LORA ** -0.5),
        'rwkv_g_up': nrm((L, GATE_LORA, RWKV_WIDTH), GATE_LORA ** -0.5),
        'rwkv_v0': nrm((L - 1, RWKV_WIDTH), 0.5),
        'rwkv_v_up': nrm((L - 1, VRES_LORA, RWKV_WIDTH), 0.5 * VRES_LORA ** -0.5),
        'rwkv_k_k': 0.85 + nrm((L, RWKV_WIDTH), 0.1),
        'rwkv_k_a': 1.0 + nrm((L, RWKV_WIDTH), 0.1),
        'rwkv_r_k': nrm((L, RWKV_HEADS, RWKV_HEAD_DIM), 0.1),
        'rwkv_gn_g': 1.0 + nrm((L, RWKV_WIDTH), 0.1),
        'rwkv_gn_b': nrm((L, RWKV_WIDTH), 0.01),
        'rwkv_w_o': nrm((L, RWKV_WIDTH, d), BETA * RWKV_WIDTH ** -0.5),
        'sgu_ln_g': 1.0 + nrm((L, SGU_WIDTH), 0.1),
        'sgu_ln_b': nrm((L, SGU_WIDTH), 0.01),
        'sgu_w': nrm((L, SGU_GROUPS, SGU_CHUNK, SGU_CHUNK), SGU_CHUNK ** -0.5),
        'sgu_b': 1.0 + nrm((L, SGU_GROUPS, SGU_CHUNK), 0.1),
        'sgu_w_o': nrm((L, SGU_WIDTH, d), BETA * SGU_WIDTH ** -0.5),
        'conv_dw': nrm((L, CONV_KERNEL, CONV_WIDTH), CONV_KERNEL ** -0.5),
        'conv_db': nrm((L, CONV_WIDTH), 0.01),
        'conv_ln_g': 1.0 + nrm((L, CONV_WIDTH), 0.1),
        'conv_ln_b': nrm((L, CONV_WIDTH), 0.01),
        'conv_w_o': nrm((L, CONV_WIDTH, d), BETA * CONV_WIDTH ** -0.5),
        'w_out': nrm((L, d, d), BETA * d ** -0.5),
        'ln1_g': 1.0 + nrm((L, d), 0.1),
        'ln1_b': nrm((L, d), 0.01),
        'router_w': nrm((d, N_EXPERTS), d ** -0.5),
        'router_b': nrm((N_EXPERTS,), 0.01),
        'moe_w_gate': nrm((L, N_EXPERTS, d, D_EXPERT), d ** -0.5),
        'moe_w_up': nrm((L, N_EXPERTS, d, D_EXPERT), d ** -0.5),
        'moe_w_down': nrm((L, N_EXPERTS, D_EXPERT, d), BETA * D_EXPERT ** -0.5),
        'ln2_g': 1.0 + nrm((L, d), 0.1),
        'ln2_b': nrm((L, d), 0.01),
    }

def reference(x, w_in_first, w_in_rest, rwkv_mu, rwkv_mu_vres, rwkv_w0, rwkv_w_up, rwkv_a0, rwkv_a_up,
              rwkv_g_up, rwkv_v0, rwkv_v_up, rwkv_k_k, rwkv_k_a, rwkv_r_k, rwkv_gn_g, rwkv_gn_b, rwkv_w_o,
              sgu_ln_g, sgu_ln_b, sgu_w, sgu_b, sgu_w_o, conv_dw, conv_db, conv_ln_g, conv_ln_b, conv_w_o,
              w_out, ln1_g, ln1_b, router_w, router_b, moe_w_gate, moe_w_up, moe_w_down, ln2_g, ln2_b):
    v_first = None
    for l in range(DEPTH):
        w_in = w_in_first if l == 0 else w_in_rest[l - 1]
        proj = x @ w_in
        pa = token_shift_mix(proj[..., :RWKV_COLS], rwkv_mu[l])
        r = pa[..., OFF_R:OFF_K]
        k = pa[..., OFF_K:OFF_V]
        v = pa[..., OFF_V:OFF_WL]
        wl = pa[..., OFF_WL:OFF_AL]
        al = pa[..., OFF_AL:OFF_GL]
        gl = pa[..., OFF_GL:RWKV_COLS]
        if l == 0:
            v_first = v
        else:
            vl = token_shift_mix(proj[..., OFF_VRES:], rwkv_mu_vres[l - 1])
            v = v + (v_first - v) * jax.nn.sigmoid(rwkv_v0[l - 1] + vl @ rwkv_v_up[l - 1])
        o_a = rwkv7_branch(r, k, v, wl, al, gl, rwkv_w0[l], rwkv_w_up[l], rwkv_a0[l], rwkv_a_up[l],
                           rwkv_g_up[l], rwkv_k_k[l], rwkv_k_a[l], rwkv_r_k[l], rwkv_gn_g[l], rwkv_gn_b[l],
                           rwkv_w_o[l])
        o_b = sgu_branch(proj[..., OFF_SGU:OFF_CONV], sgu_ln_g[l], sgu_ln_b[l], sgu_w[l], sgu_b[l], sgu_w_o[l])
        o_c = conv_branch(proj[..., OFF_CONV:OFF_GATE], conv_dw[l], conv_db[l], conv_ln_g[l], conv_ln_b[l],
                          conv_w_o[l])
        gates = jax.nn.sigmoid(proj[..., OFF_GATE:IN_COLS])
        merged = (gates[..., :D_MODEL] * o_a + gates[..., D_MODEL:2 * D_MODEL] * o_b
                  + gates[..., 2 * D_MODEL:] * o_c)
        x = layer_norm(ALPHA * x + merged @ w_out[l], ln1_g[l], ln1_b[l])
        moe_out = grouped_moe(x, router_w, router_b, moe_w_gate[l], moe_w_up[l], moe_w_down[l])
        x = layer_norm(ALPHA * x + moe_out, ln2_g[l], ln2_b[l])
    return x


_drawn_inputs = setup_inputs


def setup_inputs(seed=0):
    import zlib

    import numpy as np

    out = dict(_drawn_inputs(seed))
    spreads = {}
    factors = {'rwkv_w_up': 6.498,
     'rwkv_k_k': 3.744,
     'rwkv_gn_g': 2.758,
     'rwkv_gn_b': 24.944,
     'sgu_ln_g': 2.783,
     'sgu_ln_b': 22.682,
     'sgu_b': 2.94,
     'conv_db': 11.387,
     'conv_ln_b': 24.618,
     'ln2_b': 5.462,
     'conv_ln_g': 2.712}
    for name, (base, spread) in spreads.items():
        noise = np.random.default_rng([zlib.crc32(name.encode()), seed]).standard_normal(out[name].shape)
        drawn = base * np.exp(spread * noise) if base else spread * noise
        out[name] = __import__('jax').numpy.asarray(drawn.astype(out[name].dtype))
    for name, factor in factors.items():
        out[name] = (out[name] * factor).astype(out[name].dtype)
    return out
```

```python
from contextlib import ExitStack

import numpy as np

import concourse.bass as bass
from concourse import mybir

F32 = mybir.dt.float32
I32 = mybir.dt.int32
U32 = mybir.dt.uint32
ALU = mybir.AluOpType
ACT = mybir.ActivationFunctionType
AX_X = mybir.AxisListType.X
ADD, SUB, MUL, MAX = ALU.add, ALU.subtract, ALU.mult, ALU.max

P = 128
T, D = 512, 1024
KT = D // P
TT = T // P
HD = 64
RW = 512
HP = RW // P
LORA_W, LORA_A, LORA_G = 32, 32, 96
SGU = 256
CONV, TAPS = 256, 31
OFF_WL = 3 * RW
OFF_GL = OFF_WL + LORA_W + LORA_A
OFF_SGU = OFF_GL + LORA_G
OFF_CONV = OFF_SGU + 2 * SGU
OFF_GATE = OFF_CONV + 2 * CONV
ALPHA = 2 ** 0.25
LN_EPS, GN_EPS = 1e-5, 64e-5
DECAY_SCALE = float(np.exp(-0.5))

N_EXP, GROUPS, TOPK, FE = 32, 4, 2, 512
PER_GROUP = N_EXP // GROUPS
SLOTS = 64
MORE = T * TOPK // SLOTS - 1
PASSES = N_EXP + MORE + 1
GU = KT * 2 * FE
WD = FE // P * D
CHUNK = 2 * 2 * FE
NCH = (GU + WD) // CHUNK
BIG = 1e30

MU, W0, A0, KK_, KA_, RK_, GNG, GNB, CDB, CLG, CLB, CDW = 0, 14, 18, 22, 26, 30, 34, 38, 42, 44, 46, 48
N_PAR = CDW + 2 * TAPS

CONSTS = {}


def constant_table():
    i, j = np.arange(P)[:, None], np.arange(P)[None, :]
    same64, same16 = i // 64 == j // 64, i // 16 == j // 16
    blocks = {
        "ident": i == j,
        "within16": same16 & (j < i),
        "within16T": same16 & (i < j),
        "across16T": same64 & ~same16 & (i < j),
        "beforeT": same64 & (i < j),
        "uptoT": same64 & (i <= j),
        "head_ones": same64,
        "ident_twice": (i % 64) == np.arange(64)[None, :],
        "head0_down": (i == j) & (i < 64),
        "head1_down": (i - 64 == j),
        "ones": np.ones((P, P), bool),
        "earlier": i < j,
        "slot_iota": j % SLOTS + 0 * i,
        "iota": np.arange(64)[None, :] + np.zeros((P, 1)),
        "expert_left": N_EXP - np.arange(N_EXP)[None, :] + np.zeros((P, 1)),
        "group_left": GROUPS - np.arange(GROUPS)[None, :] + np.zeros((P, 1)),
        "token": np.arange(P)[:, None] + P * np.arange(TT)[None, :],
        "half": np.arange(P)[:, None] // SLOTS,
    }
    at, parts = 0, []
    for name, b in blocks.items():
        CONSTS[name] = (at, b.shape[1])
        at += b.shape[1]
        parts.append(b.astype(np.float32))
    return np.ascontiguousarray(np.concatenate(parts, 1))


TABLE = constant_table()

FILL = {"prep": 16, "turned": 2, "scores0": 4, "scores1": 4, "chain": 1, "y": 3, "mean": 3, "var": 0}
CHUNKS = T // HD
PER_PAIR = (3 * D // P // HP) * KT
FILL["var"] = PER_PAIR - sum(v * (CHUNKS - 1 if k == "chain" else 1) for k, v in FILL.items())
GATE_TILES = 3 * D // P
assert FILL["var"] >= 0


def column_tiles():
    tiles = [(OFF_CONV + P * i, P) for i in range(4)]
    tiles += [(OFF_SGU + SGU + P * i, P) for i in range(2)]
    tiles += [(OFF_SGU + P * i, P) for i in range(2)]
    tiles += [(OFF_WL, LORA_W + LORA_A), (OFF_GL, LORA_G)]
    g = 0
    for hp in range(HP):
        tiles += [(RW * n + P * hp, P) for n in range(3)]
        tiles += [(OFF_GATE + P * (g + i), P) for i in range(GATE_TILES // HP)]
        g += GATE_TILES // HP
    return tiles


TILES = column_tiles()
RING = 4
V_TILES = (4, 5)


def phase_after(tile):
    if tile < 4:
        return tile + 1
    if tile < 6:
        return 8
    return tile + 3



class Gates:

    def __init__(self):
        self.done = 0

    def step(self, n):
        first = self.done
        self.done += n
        return range(first, self.done)


def phase_of_gate(g):
    per = GATE_TILES // HP
    return 12 + (3 + per) * (g // per) + 3 + g % per


def tile_of_phase(ph):
    return ph if ph < 4 else (4 if ph < 8 else ph - 2)


def program(nc, x_tok, xT, w_in, par, table, lora, rows, sgu_b, sgu_wT, w_o, w_out, router_w, zeros, w_gu, w_down, out):
    with ExitStack() as ctx:
        def sb(name, shape, dt=F32):
            return ctx.enter_context(nc.sbuf_tensor(name, shape, dt))

        def sem(name):
            return ctx.enter_context(nc.semaphore(name))

        const = sb("const", [P, TABLE.shape[1]])
        par_sb = sb("par_sb", [P, N_PAR + 8])
        lora_sb = sb("lora_sb", [P, 2, RW])
        xT_sb = sb("xT_sb", [P, KT, T])
        ring = sb("ring", [P, RING, KT, P])
        gates = sb("gates", [P, GATE_TILES, T])
        sgu_out = sb("sgu_out", [P, 2, T])
        conv_out = sb("conv_out", [P, 2, T])
        rwkv_out = sb("rwkv_out", [P, HP, T])
        raw = sb("raw", [P, 2, T + 1])
        wl_al = sb("wl_al", [P, T])
        gl = sb("gl", [P, T])
        ARENA = 23700
        arena = sb("arena", [P, ARENA])
        proj = ctx.enter_context(nc.psum_tensor("proj", [P, 2, T], F32))
        bank = ctx.enter_context(nc.psum_tensor("bank", [P, 6, T], F32))

        def C(name):
            at, n = CONSTS[name]
            return const[:, at:at + n]

        def par_col(c):
            return par_sb[:, c:c + 1]

        CLG_S, GNG_S, EPS_CONV, EPS_GN = N_PAR, N_PAR + 2, N_PAR + 6, N_PAR + 7

        class Cut:
            def __init__(self, base):
                self.at = base

            def __call__(self, n, **split):
                v = arena[:, self.at:self.at + n]
                self.at += n
                assert self.at <= ARENA, self.at
                return v.rearrange(split["r"], **split["k"]) if split else v

        cut = Cut(0)
        conv_val = cut(2 * T, r="p (i t) -> p i t", k=dict(i=2))
        conv_gate = cut(2 * T, r="p (i t) -> p i t", k=dict(i=2))
        PADDED = T + TAPS - 1
        conv_in = cut(2 * PADDED, r="p (i t) -> p i t", k=dict(i=2))
        conv_acc = cut(2 * T, r="p (i t) -> p i t", k=dict(i=2))
        conv_sq = cut(2 * T, r="p (i t) -> p i t", k=dict(i=2))
        conv_rs = cut(T)
        sgu_u = cut(2 * T, r="p (i t) -> p i t", k=dict(i=2))
        sgu_v = cut(TT * SGU, r="p (c d) -> p c d", k=dict(c=TT))
        sgu_w = cut(4 * P, r="p (g q) -> p g q", k=dict(g=4))
        sgu_ln = cut(2 * SGU, r="p (i d) -> p i d", k=dict(i=2))
        sgu_bias = cut(2 * P, r="p (i q) -> p i q", k=dict(i=2))
        sgu_mix = cut(2 * T, r="p (i t) -> p i t", k=dict(i=2))
        sgu_stat = cut(TT * 6, r="p (c s) -> p c s", k=dict(c=TT))
        sgu_mv = cut(TT * 2, r="p (c s) -> p c s", k=dict(c=TT))
        sgu_rs = cut(TT)

        cut = Cut(0)
        r_, k_ = cut(T), cut(T)
        iclr, decay = cut(T), cut(T)
        kk, sq = cut(T), cut(T)
        v_, kh, cum, inv, norm, kkn = (cut(T) for _ in range(6))
        bT, kT, bH, kH, diag, bonus = (cut(T) for _ in range(6))
        arT = cut(2 * T, r="p (j n t) -> p j n t", k=dict(j=TT, n=2))
        X0 = cut(8 * P, r="p (h j n) -> p h j n", k=dict(h=2, j=TT))
        VZ = cut(8 * P, r="p (h j n) -> p h j n", k=dict(h=2, j=TT))
        BZ = cut(8 * P, r="p (h j c n) -> p h j c n", k=dict(h=2, j=TT, c=2))
        KZ = cut(8 * P, r="p (h j c n) -> p h j c n", k=dict(h=2, j=TT, c=2))
        rbT = cut(8 * P, r="p (h j n) -> p h j n", k=dict(h=2, j=TT))
        akrkT = cut(16 * P, r="p (h j n) -> p h j n", k=dict(h=2, j=TT))
        G = [[cut(4 * P, r="p (j n) -> p j n", k=dict(j=TT)) for _ in range(6)] for _ in range(2)]
        pair_end = cut.at
        out2 = arena[:, 0:2 * T].rearrange("p (h j n) -> p h j n", h=2, j=TT)
        gh = arena[:, 2 * T:4 * T].rearrange("p (h j n) -> p h j n", h=2, j=TT)
        state = arena[:, 4 * T:6 * T].rearrange("p (c h n) -> p c h n", c=CHUNKS, h=2)
        first_of_chunk = bT
        y_, yc, ysq, yrs, yn = bT, kT, bH, kH, cum

        cut = Cut(0)
        wout_sb = cut(KT * D, r="p (k n) -> p k n", k=dict(k=KT))
        merged = cut(KT * T, r="p (k t) -> p k t", k=dict(k=KT))
        wo_sb = cut(8 * D, r="p (k n) -> p k n", k=dict(k=8))
        mtmp = cut(3 * T, r="p (i t) -> p i t", k=dict(i=3))
        ln_stat = cut(TT * 12, r="p (c s) -> p c s", k=dict(c=TT))
        ln_mv = cut(TT * 2, r="p (c s) -> p c s", k=dict(c=TT))
        ln_rs = cut(TT)
        x1 = ring[:, :, :, :].rearrange("p s k c -> p s (k c)")
        ln_rows = xT_sb[:, :, :].rearrange("p k t -> p (k t)").rearrange("p (i d) -> p i d", i=4)

        small_end = cut.at
        w_set = [gates[:, :, :].rearrange("p g t -> p (g t)"), arena[:, 0:GU + WD]]
        assert KT * D + KT * T == GU + WD == GATE_TILES * T
        cut = Cut(KT * D + KT * T)
        x1T = cut(2 * KT * P, r="p (b k t) -> p b k t", k=dict(b=2, k=KT))
        slot_hot = cut(8 * P, r="p (n s) -> p n s", k=dict(n=8))
        pass_hot = cut(8 * 3 * PASSES, r="p (n i q) -> p n i q", k=dict(n=8, i=3))
        xe = cut(T)
        xeT = cut(T, r="p (c s) -> p c s", k=dict(c=4))
        h_silu, h_e = cut(FE // 2), cut(FE // 2)
        hT = cut(FE // 2, r="p (c s) -> p c s", k=dict(c=2))
        y_e = cut(T)
        assert cut.at <= KT * D + KT * T + 8 * D
        cut = Cut(small_end)
        rt = [cut(2 * TT * N_EXP) for _ in range(4)]
        assert cut.at <= ARENA
        pair_y = arena[:, 0:8 * D].rearrange("p (n d) -> p n d", n=8)
        lora_flat, raw_flat = lora_sb[:, :, :].rearrange("p i n -> p (i n)"), raw[:, :, :].rearrange("p i n -> p (i n)")
        place = {"lora": 0, "raw": 0}

        def late(where, flat, n):
            at = place[where]
            place[where] += n
            return flat[:, at:at + n]

        rw_sb = late("lora", lora_flat, KT * N_EXP).rearrange("p (k e) -> p k e", k=KT)
        rb_sb = late("lora", lora_flat, N_EXP)
        scores = late("lora", lora_flat, TT * N_EXP).rearrange("p (c e) -> p c e", c=TT)
        sel = late("lora", lora_flat, TT * N_EXP).rearrange("p (c e) -> p c e", c=TT)
        top8 = late("lora", lora_flat, TT * GROUPS * 8).rearrange("p (n e) -> p n e", e=8)
        grp = late("lora", lora_flat, 3 * TT * GROUPS).rearrange("p (i n) -> p i n", i=3)
        hot = late("lora", lora_flat, TOPK * TT * N_EXP).rearrange("p (k c e) -> p k c e", k=TOPK, c=TT)
        assert place["lora"] <= 2 * RW
        chosen = late("raw", raw_flat, TT * N_EXP).rearrange("p (c e) -> p c e", c=TT)
        small = late("raw", raw_flat, 12 * TOPK * TT).rearrange("p (i n) -> p i n", i=12)
        count = late("raw", raw_flat, 6 * N_EXP).rearrange("p (i n) -> p i n", i=6)
        gate_tab, idx_f, more_f = (late("raw", raw_flat, n) for n in (PASSES, PASSES, 16))
        idx_tab, idx_now, pos_i, more_i, more_exp = (late("raw", raw_flat, n).bitcast(I32) for n in (PASSES, 1, TOPK * TT, 1, 16))
        assert place["raw"] <= 2 * (T + 1)
        x1_dram = nc.dram_tensor("x1_rows", (T * 2, D // 2), F32).ap()
        y_dram = nc.dram_tensor("y_rows", (PASSES * SLOTS, D), F32).ap()

        s_const, s_par, s_x, s_small, s_lnrows, s_sgub = map(sem, ["const_in", "par_in", "xT_in", "sgu_par_in", "ln_rows_in", "sgu_bias_in"])
        s_win = [sem(f"ring_in{i}") for i in range(RING)]
        s_proj = sem("proj_done")
        s_projfree = sem("proj_read")
        s_rawfree = sem("raw_read")
        s_dve = sem("dve_seq")
        s_act = sem("act_seq")
        s_pool = sem("pool_seq")
        s_masked = sem("sgu_w_masked")
        s_convin, s_pads = sem("conv_in_ready"), sem("pads_zeroed")
        s_scaled = sem("gains_scaled")
        s_convacc, s_convsum, s_convsq, s_convvar, s_convn = map(sem, ["conv_acc", "conv_sum", "conv_sq", "conv_var", "conv_norm"])
        s_convout = sem("conv_out_ready")
        s_vln, s_mix, s_sguout = map(sem, ["v_normed", "mixed_in_psum", "sgu_out_ready"])
        s_early = sem("early_done")
        s_vstat, s_vroot, s_convroot = map(sem, ["v_variance", "v_deviation", "conv_deviation"])
        s_norm, s_yroot, s_lnvar, s_lnroot = map(sem, ["kk_norm", "y_deviation", "ln_variance", "ln_deviation"])
        s_lora, s_th = sem("lora_shifted"), sem("lora_activated")
        s_z, s_iclr, s_decay = map(sem, ["z_in_psum", "iclr_ready", "decay_ready"])
        s_sq, s_ss, s_pr, s_bs, s_ch = map(sem, ["kk_squared", "kk_norm_psum", "rk_product", "bonus_psum", "channels_ready"])
        s_v = sem("v_ready")
        s_tr, s_tma, s_tmd = map(sem, ["turned", "turned_out_act", "turned_out_dve"])
        s_sc, s_scev = sem("scores_psum"), sem("scores_out")
        s_dm, s_da, s_dd = sem("solve_psum"), sem("solve_out_act"), sem("solve_out_dve")
        s_init = sem("state_init")
        s_zero = sem("zeros_set")
        s_cm, s_ce = sem("chain_psum"), sem("chain_out")
        s_ymm, s_y, s_mu, s_yc, s_var, s_out = map(sem, ["y_psum", "y_out", "y_mean", "y_centred", "y_var", "pair_done"])
        s_wo, s_wout, s_xtok = map(sem, ["w_o_in", "w_out_in", "x_tok_in"])
        s_mm3, s_mread, s_m3, s_merged = map(sem, ["branches_psum", "branches_read", "products_ready", "merged_ready"])
        s_mx, s_pre = sem("mixed_psum"), sem("residual_added")
        s_x1, s_st = sem("x1_ready"), sem("stored")
        s_yfree = sem("ye_bank_free")
        s_begun, s_ypad = sem("gathers_begun"), sem("y_rows_zeroed")
        s_x1st, s_rw = sem("x1_stored"), sem("router_par_in")
        s_x1Tp, s_x1T, s_scp, s_score = map(sem, ["x1T_psum", "x1T_out", "scores_in_psum", "scores_ready"])
        s_chosen, s_rank, s_hot, s_tabp, s_tab, s_idxf = map(sem, ["chosen_ready", "rank_psum", "one_hots_ready", "table_psum", "tables_ready", "indices_float"])
        s_w = [[sem(f"w_in{b}_{c}") for c in range(NCH)] for b in range(2)]
        s_used = sem("w_used")
        s_idx, s_xe, s_xe0 = sem("index_ready"), sem("tokens_in"), sem("tokens_zeroed")
        s_xeTp, s_xeT, s_hp, s_silu, s_h, s_hTp, s_hT, s_yp, s_ye, s_yst = map(
            sem, ["xeT_psum", "xeT_out", "h_psum", "silu_ready", "h_ready", "hT_psum", "hT_out", "ye_psum", "ye_ready", "ye_stored"])
        s_pair, s_sum, s_sum2, s_x2 = [sem(f"pair_in{n}") for n in range(8)], sem("pairs_summed"), sem("residual2"), sem("x2_ready")
        s_lnvar2, s_lnroot2 = sem("ln2_variance"), sem("ln2_deviation")

        block = ctx.enter_context(nc.Block())

        @block.sync
        def _(sp):
            sp.dma_start(const[:, :], table).then_inc(s_const, 16)
            wv = w_in.rearrange("(k p) c -> p k c", p=P)
            for n, (c0, w) in enumerate(TILES):
                if n >= RING:
                    sp.wait_ge(s_proj, phase_after(n - RING))
                sp.dma_start(ring[:, n % RING, :, 0:w], wv[:, :, c0:c0 + w]).then_inc(s_win[n % RING], 16)
                if n == 0:
                    for k in range(0, KT, 4):
                        sp.dma_start(xT_sb[:, k:k + 4, :], xT[:, k:k + 4, :]).then_inc(s_x, 16)
            for q in range(N_EXP, PASSES):
                sp.dma_start(y_dram[q * SLOTS:(q + 1) * SLOTS, :], zeros).then_inc(s_ypad, 16)
            sp.wait_ge(s_proj, phase_after(len(TILES) - 1))
            sp.dma_start(x1, x_tok.rearrange("(c p) d -> p c d", p=P)).then_inc(s_xtok, 16)
            sp.dma_start(ln_rows, rows[:, 2 * SGU:2 * SGU + 4 * D].partition_broadcast(P).rearrange("p a (i d) -> p (a i) d", i=4)).then_inc(s_lnrows, 16)
            sp.wait_ge(s_dm, 24 * HP)
            sp.dma_start(wo_sb, w_o.rearrange("(k p) n -> p k n", p=P)).then_inc(s_wo, 16)
            sp.wait_ge(s_out, HP)
            sp.dma_start(rw_sb[:, :, :], router_w.rearrange("(k p) e -> p k e", p=P)).then_inc(s_rw, 16)
            sp.dma_start(rb_sb[:, :], rows[:, 2 * SGU + 4 * D:].partition_broadcast(P).rearrange("p a e -> p (a e)")).then_inc(s_rw, 16)
            sp.dma_start(wout_sb, w_out.rearrange("(k p) n -> p k n", p=P)).then_inc(s_wout, 16)
            def chunk_src(e, c):
                n = c * CHUNK
                return w_gu[e, :, n:n + CHUNK] if n < GU else w_down[e, :, n - GU:n - GU + CHUNK]

            def load(b, c, e):
                sp.dma_start(w_set[b][:, c * CHUNK:(c + 1) * CHUNK], chunk_src(e, c)).then_inc(s_w[b][c], 16)

            sp.wait_ge(s_m3, KT)
            for c in range(NCH):
                load(0, c, 0)
            for c in range(TT):
                sp.wait_ge(s_x1, c + 1)
                sp.dma_start(x1_dram.rearrange("(t h) d -> t (h d)", h=2)[c * P:(c + 1) * P, :], x1[:, c, :]).then_inc(s_x1st, 16)
            sp.wait_ge(s_mx, 2 * TT)
            for c in range(NCH):
                load(1, c, 1)
            with sp.Fori(1, N_EXP // 2) as i:
                for b in range(2):
                    for c in range(NCH):
                        sp.wait_ge(s_used, i * (2 * NCH) + (b - 2) * NCH + c + 1)
                        e = sp.snap(i * 2 + b, min_val=0, max_val=N_EXP - 1)
                        n = c * CHUNK
                        src = w_gu[bass.ds(e, 1), :, n:n + CHUNK] if n < GU else w_down[bass.ds(e, 1), :, n - GU:n - GU + CHUNK]
                        sp.dma_start(w_set[b][:, n:n + CHUNK], src.rearrange("a p n -> (a p) n")).then_inc(s_w[b][c], 16)
            sp.wait_ge(s_tab, 3)
            more = sp.value_load(more_i[0:1, 0:1], min_val=0, max_val=MORE)
            with sp.If(more > 0):
                with sp.Fori(0, more) as i:
                    e = sp.value_load(more_exp[0:1, bass.ds(i, 1)], min_val=0, max_val=N_EXP - 1)
                    for c in range(NCH):
                        sp.wait_ge(s_used, i * NCH + (N_EXP - 1) * NCH + c + 1)
                        n = c * CHUNK
                        src = w_gu[bass.ds(e, 1), :, n:n + CHUNK] if n < GU else w_down[bass.ds(e, 1), :, n - GU:n - GU + CHUNK]
                        sp.dma_start(w_set[0][:, n:n + CHUNK], src.rearrange("a p n -> (a p) n")).then_inc(s_w[0][c], 16)
            for c in range(TT):
                sp.wait_ge(s_x2, c + 1)
                sp.dma_start(out[c * P:(c + 1) * P, :], x1[:, c, :]).then_inc(s_st, 16)
            sp.wait_ge(s_st, 16 * TT)

        @block.gpsimd
        def _(pool):
            pool.dma_start(sgu_w, sgu_wT).then_inc(s_small, 16)
            pool.dma_start(sgu_ln, rows[:, 0:2 * SGU].partition_broadcast(P).rearrange("p a (i d) -> p (a i) d", i=2)).then_inc(s_small, 16)
            for g in range(4):
                pool.dma_start(sgu_bias[HD * (g % 2):HD * (g % 2) + HD, g // 2, :],
                               sgu_b[g:g + 1, :].partition_broadcast(HD).rearrange("p a q -> p (a q)")).then_inc(s_sgub, 16)
            pool.memset(conv_in[:, :, 0:TAPS - 1], 0.0).then_inc(s_pads, 1)
            pool.memset(raw[:, :, 0:1], 0.0).then_inc(s_pads, 1)
            pool.wait_ge(s_small, 32)
            pool.affine_select(out=sgu_w, in_=sgu_w, compare_op=ALU.is_ge, fill=0.0, base=0,
                               pattern=[[0, 4], [1, P]], channel_multiplier=-1).then_inc(s_masked, 1)
            pool.wait_ge(s_early, 1)
            pool.wait_ge(s_convout, 2)
            for z in (VZ, BZ, KZ):
                pool.memset(z, 0.0).then_inc(s_zero, 1)
            for hp in range(HP):
                pool.wait_ge(s_ch, hp + 1)
                if hp:
                    pool.wait_ge(s_out, hp)
                if hp == 0:
                    pool.wait_ge(s_zero, 3)
                    pool.wait_ge(s_const, 16)
                pool.memset(state[0:HD, 0, :, :], 0.0).then_inc(s_init, 1)
                pool.wait_ge(s_init, 2 * hp + 1)
                pool.tensor_copy(state[HD:P, :, :, :].rearrange("p c h n -> p (c h) n"),
                                 C("ident_twice")[HD:P, :].unsqueeze(1).broadcast_to([HD, 2 * CHUNKS, HD])).then_inc(s_init, 1)
            pool.wait_ge(s_init, 2 * HP)
            for m in range(KT):
                pool.wait_ge(s_m3, m + 1)
                pool.tensor_tensor(mtmp[:, 0, :], mtmp[:, 0, :], mtmp[:, 1, :], ADD).then_inc(s_pool, 1)
                pool.wait_ge(s_pool, m + 1)
                pool.tensor_tensor(merged[:, m, :], mtmp[:, 0, :], mtmp[:, 2, :], ADD).then_inc(s_merged, 1)
            pool.wait_ge(s_ypad, 16 * (PASSES - N_EXP))
            pool.wait_ge(s_mm3, KT)
            pool.wait_ge(s_merged, KT)
            pool.memset(xe, 0.0).then_inc(s_xe0, 1)
            pool.wait_ge(s_tab, 3)
            pool.wait_ge(s_xe0, 1)
            pool.wait_ge(s_x1st, 16 * TT)

            last_half_row, last_row = pool.to_reg(2 * T - 1), pool.to_reg(PASSES * SLOTS - 1)

            def gather(p):
                pool.tensor_copy(idx_now[:, 0:1], idx_tab[:, bass.ds(p, 1)]).then_inc(s_idx, 1)
                pool.wait_ge(s_idx, p + 1)
                pool.sem_inc(s_begun, 1)
                pool.indirect_dma_start(xe, None, x1_dram, bass.IndirectOffsetOnAxis(ap=idx_now[:, 0:1], axis=0),
                                        bounds_check=last_half_row, oob_is_err=False).then_inc(s_xe, 16)

            gather(0)
            with pool.Fori(0, N_EXP) as i:
                pool.wait_ge(s_xe, i * 16 + 16)
                pool.wait_ge(s_xeTp, i + 1)
                gather(i + 1)
            more = pool.value_load(more_i[0:1, 0:1], min_val=0, max_val=MORE)
            with pool.If(more > 0):
                with pool.Fori(0, more) as i:
                    pool.wait_ge(s_xe, i * 16 + 16 * (N_EXP + 1))
                    pool.wait_ge(s_xeTp, i + N_EXP + 1)
                    gather(i + N_EXP + 1)
            pool.wait_ge(s_xe, more * 16 + 16 * (N_EXP + 1))
            pool.wait_ge(s_yst, more * 32 + 32 * N_EXP)
            pool.sem_inc(s_begun, 1)
            for c in range(TT):
                for k in range(TOPK):
                    n = TOPK * c + k
                    pool.indirect_dma_start(pair_y[:, n, :], None, y_dram,
                                            bass.IndirectOffsetOnAxis(ap=pos_i[:, k * TT + c:k * TT + c + 1], axis=0),
                                            bounds_check=last_row, oob_is_err=False).then_inc(s_pair[n], 16)

        @block.scalar
        def _(act):
            act.dma_start(par_sb[:, 0:N_PAR], par).then_inc(s_par, 16)
            act.dma_start(lora_sb[:, :, :], lora).then_inc(s_par, 16)
            state_ = {"phase": 0, "raw": 0, "seq": 0}

            def take(out, func, rows_=P, **kw):
                ph = state_["phase"]
                act.wait_ge(s_proj, ph + 1)
                n = SGU if 4 <= ph < 8 else T
                act.activation(out, proj[0:rows_, ph % 2, 0:n], func, **kw).then_inc(s_projfree, 1)
                state_["phase"] += 1

            def take_raw(rows_=P):
                n = state_["raw"]
                if n == 0:
                    act.wait_ge(s_pads, 2)
                if n >= 2:
                    act.wait_ge(s_rawfree, n - 1)
                ph = state_["phase"]
                act.wait_ge(s_proj, ph + 1)
                act.activation(raw[0:rows_, n % 2, 1:T + 1], proj[0:rows_, ph % 2, :], ACT.Copy).then_inc(s_projfree, 1)
                state_["phase"] += 1
                state_["raw"] += 1

            for i in range(2):
                take(conv_val[:, i, :], ACT.Copy)
            for i in range(2):
                take(conv_gate[:, i, :], ACT.Sigmoid)
            for c in range(TT):
                take(sgu_v[:, c, :], ACT.Gelu)
            for i in range(2):
                take(sgu_u[:, i, :], ACT.Gelu)
            take_raw(LORA_W + LORA_A)
            take_raw(LORA_G)
            act.wait_ge(s_vstat, 1)
            act.activation(sgu_rs, sgu_rs, ACT.Sqrt).then_inc(s_vroot, 1)
            act.wait_ge(s_lora, 2)
            act.activation(wl_al[0:LORA_W, :], wl_al[0:LORA_W, :], ACT.Tanh).then_inc(s_th, 1)
            act.activation(gl[0:LORA_G, :], gl[0:LORA_G, :], ACT.Sigmoid).then_inc(s_th, 1)
            act.wait_ge(s_scaled, 1)
            act.wait_ge(s_convvar, 1)
            act.activation(conv_rs, bank[:, 1, :], ACT.Sqrt, bias=par_col(EPS_CONV)).then_inc(s_convroot, 1)
            for i in range(2):
                act.wait_ge(s_convn, i + 1)
                act.wait_ge(s_scaled, 1)
                act.activation(conv_out[:, i, :], conv_sq[:, i, :], ACT.Silu, bias=par_col(CLB + i),
                               scale=par_col(CLG_S + i)).then_inc(s_convout, 1)
            act.wait_ge(s_early, 1)

            gate = Gates()

            def evac_gates(n):
                for mm in gate.step(n):
                    if mm % KT == KT - 1:
                        g = mm // KT
                        assert state_["phase"] == phase_of_gate(g)
                        take(gates[:, g, :], ACT.Sigmoid)

            for hp in range(HP):
                act.wait_ge(s_z, hp + 1)
                act.activation(decay, bank[:, 0, :], ACT.Sigmoid, bias=par_col(W0 + hp)).then_inc(s_act, 1)
                act.activation(iclr, bank[:, 1, :], ACT.Sigmoid, bias=par_col(A0 + hp)).then_inc(s_iclr, 1)
                act.wait_ge(s_act, hp + 1)
                act.activation(decay, decay, ACT.Exp, scale=-DECAY_SCALE).then_inc(s_decay, 1)
                for _ in range(3):
                    take_raw()
                act.wait_ge(s_ss, hp + 1)
                act.activation(norm, bank[:, 2, :], ACT.Sqrt).then_inc(s_norm, 1)
                evac_gates(FILL["prep"])
                act.wait_ge(s_tr, 4 * hp + 1)
                if hp == 0:
                    act.wait_ge(s_zero, 3)
                for h in range(2):
                    act.activation(X0[:, h, :, 0:HD],
                                   bank[:, 2, :].rearrange("p (j c) -> p j c", j=TT)[:, :, h * HD:(h + 1) * HD],
                                   ACT.Copy).then_inc(s_tma, 1)
                act.wait_ge(s_tr, 4 * hp + 2)
                for h in range(2):
                    act.activation(VZ[:, h, :, HD:P],
                                   bank[:, 5, :].rearrange("p (j c) -> p j c", j=TT)[:, :, h * HD:(h + 1) * HD],
                                   ACT.Copy).then_inc(s_tma, 1)
                evac_gates(FILL["turned"])
                evac_gates(FILL["scores0"])
                evac_gates(FILL["scores1"])

                def out(stage, dst, b, inc=True):
                    for g in range(2):
                        act.wait_ge(s_dm, 24 * hp + 2 * (stage - 1) + g + 1)
                        src = bank[:, 3 * g + b, :].rearrange("p (j n) -> p j n", j=TT)
                        for d, part in dst:
                            ins = act.activation(d(g), src[:, :, 0:part], ACT.Copy)
                        ins.then_inc(s_da, 1)

                out(1, [(lambda g: G[g][2], P)], 0)
                out(2, [(lambda g: G[g][0], P)], 0)
                for g in range(2):
                    act.wait_ge(s_dm, 24 * hp + 2 * 2 + g + 1)
                    act.activation(G[g][2], bank[:, 3 * g, :].rearrange("p (j n) -> p j n", j=TT), ACT.Copy)
                    act.activation(X0[:, g, :, HD:P], bank[:, 3 * g + 1, 0:TT * HD].rearrange("p (j n) -> p j n", j=TT),
                                   ACT.Copy).then_inc(s_da, 1)
                out(5, [(lambda g: G[g][1], P)], 0)
                for st in (6, 8, 10):
                    out(st, [(lambda g: G[g][2], P)], 1)
                out(12, [(lambda g: out2[:, g, :, :], P)], 1)
                evac_gates(FILL["chain"] * (CHUNKS - 1))
                evac_gates(FILL["y"])
                act.wait_ge(s_ymm, hp + 1)
                act.activation(y_, bank[:, 3, :], ACT.Copy).then_inc(s_y, 1)
                evac_gates(FILL["mean"])
                act.wait_ge(s_var, hp + 1)
                act.activation(yrs, bank[:, 1, :], ACT.Sqrt, bias=par_col(EPS_GN)).then_inc(s_yroot, 1)
                evac_gates(FILL["var"])
            for c in range(TT):
                act.wait_ge(s_lnvar, c + 1)
                act.activation(ln_rs[:, c:c + 1], ln_rs[:, c:c + 1], ACT.Sqrt).then_inc(s_lnroot, 1)
                act.wait_ge(s_x1Tp, c + 1)
                b = 2 * (c % 2)
                act.activation(x1T[:, c % 2, :, :], bank[:, b:b + 2, :].rearrange("p b (k t) -> p (b k) t", k=4), ACT.Copy).then_inc(s_x1T, 1)
            act.wait_ge(s_scp, 1)
            act.activation(scores[:, :, :], bank[:, 4, 0:TT * N_EXP].rearrange("p (c e) -> p c e", c=TT), ACT.Sigmoid).then_inc(s_score, 1)

            act.wait_ge(s_tab, 3)
            act.sem_inc(s_yfree, 1)

            def one_pass(p):
                act.wait_ge(s_hp, p + 1)
                act.activation(h_silu, bank[:, 0, 0:FE // 2], ACT.Silu).then_inc(s_silu, 1)
                act.wait_ge(s_yp, p + 1)
                act.activation(y_e, bank[:, 1, :], ACT.Copy, scale=gate_tab[:, bass.ds(p, 1)]).then_inc(s_ye, 1)
                act.wait_ge(s_ye, p + 1)
                act.sem_inc(s_yfree, 1)
                dst = y_dram.rearrange("(q s) (h d) -> q h s d", s=SLOTS, h=2)
                for h in range(2):
                    act.dma_start(dst[bass.ds(p, 1), h, :, :].rearrange("q s d -> (q s) d"), y_e[SLOTS * h:SLOTS * h + SLOTS, :]).then_inc(s_yst, 16)
                act.wait_ge(s_yst, p * 32 + 32)

            with act.Fori(0, N_EXP) as i:
                one_pass(i)
            more = act.value_load(more_i[0:1, 0:1], min_val=0, max_val=MORE)
            with act.If(more > 0):
                with act.Fori(0, more) as i:
                    one_pass(i + N_EXP)
            for c in range(TT):
                act.wait_ge(s_lnvar2, c + 1)
                act.activation(ln_rs[:, c:c + 1], ln_rs[:, c:c + 1], ACT.Sqrt).then_inc(s_lnroot2, 1)

        @block.vector
        def _(dve):
            seq = {"n": 0, "raw": 0}

            def then(ins):
                seq["n"] += 1
                ins.then_inc(s_dve, 1)
                dve.wait_ge(s_dve, seq["n"])

            dve.wait_ge(s_par, 32)
            dve.tensor_scalar(par_sb[:, CLG_S:CLG_S + 2], par_sb[:, CLG:CLG + 2], CONV ** 0.5, None, MUL)
            dve.memset(par_sb[:, EPS_CONV:EPS_CONV + 1], CONV * LN_EPS)
            dve.memset(par_sb[:, EPS_GN:EPS_GN + 1], HD * GN_EPS)
            dve.tensor_scalar(par_sb[:, GNG_S:GNG_S + 4], par_sb[:, GNG:GNG + 4], HD ** 0.5, None, MUL).then_inc(s_scaled, 1)
            dve.wait_ge(s_scaled, 1)

            dve.wait_ge(s_projfree, 4)
            dve.wait_ge(s_pads, 2)
            for i in range(2):
                dve.tensor_tensor(conv_in[:, i, TAPS - 1:PADDED], conv_val[:, i, :], conv_gate[:, i, :], MUL).then_inc(s_convin, 1)
            dve.wait_ge(s_convin, 2)
            for tap in range(TAPS):
                for i in range(2):
                    src, w = conv_in[:, i, tap:tap + T], par_col(CDW + TAPS * i + tap)
                    if tap >= 1:
                        dve.wait_ge(s_convacc, 2 * tap + i - 1)
                    if tap == 0:
                        ins = dve.tensor_scalar(conv_acc[:, i, :], src, w, par_col(CDB + i), MUL, ADD)
                    else:
                        ins = dve.scalar_tensor_tensor(conv_acc[:, i, :], src, w, conv_acc[:, i, :], MUL, ADD)
                    ins.then_inc(s_convacc, 1)

            def shift(dst, mu, rows_=P, done=None):
                n = seq["raw"]
                seq["raw"] += 1
                ph = 10 + n if n < 2 else 12 + (3 + GATE_TILES // HP) * ((n - 2) // 3) + (n - 2) % 3
                dve.wait_ge(s_projfree, ph + 1)
                now, before = raw[0:rows_, n % 2, 1:T + 1], raw[0:rows_, n % 2, 0:T]
                then(dve.tensor_tensor(dst, before, now, SUB))
                dve.scalar_tensor_tensor(dst, dst, par_sb[0:rows_, MU + mu:MU + mu + 1], now, MUL, ADD).then_inc(s_rawfree, 1)

            dve.wait_ge(s_projfree, 8)
            for c in range(TT):
                ins = dve.bn_stats(sgu_stat[:, c, :], sgu_v[:, c, :])
            then(ins)
            for c in range(TT):
                ins = dve.bn_aggr(sgu_mv[:, c, :], sgu_stat[:, c, :])
            then(ins)
            dve.tensor_scalar(sgu_rs, sgu_mv[:, :, 1], LN_EPS, None, ADD).then_inc(s_vstat, 1)
            dve.wait_ge(s_vroot, 1)
            then(dve.reciprocal(sgu_rs, sgu_rs))
            for c in range(TT):
                ins = dve.tensor_scalar(sgu_v[:, c, :], sgu_v[:, c, :], sgu_mv[:, c, 0:1], sgu_rs[:, c:c + 1], SUB, MUL)
            then(ins)
            dve.wait_ge(s_small, 32)
            then(dve.tensor_tensor(sgu_v, sgu_v, sgu_ln[:, 0:1, :].broadcast_to([P, TT, SGU]), MUL))
            dve.tensor_tensor(sgu_v, sgu_v, sgu_ln[:, 1:2, :].broadcast_to([P, TT, SGU]), ADD).then_inc(s_vln, 1)

            shift(wl_al[0:LORA_W + LORA_A, :], 12, LORA_W + LORA_A)
            shift(gl[0:LORA_G, :], 13, LORA_G)
            dve.wait_ge(s_rawfree, 2)
            dve.sem_inc(s_lora, 2)

            dve.wait_ge(s_convsum, 1)
            for i in range(2):
                ins = dve.scalar_tensor_tensor(conv_acc[:, i, :], bank[:, 0, :], -1.0 / CONV, conv_acc[:, i, :], MUL, ADD)
            then(ins)
            for i in range(2):
                dve.tensor_tensor(conv_sq[:, i, :], conv_acc[:, i, :], conv_acc[:, i, :], MUL).then_inc(s_convsq, 1)
            dve.wait_ge(s_convroot, 1)
            then(dve.reciprocal(conv_rs, conv_rs))
            for i in range(2):
                dve.tensor_tensor(conv_sq[:, i, :], conv_acc[:, i, :], conv_rs, MUL).then_inc(s_convn, 1)

            dve.wait_ge(s_mix, 1)
            dve.wait_ge(s_sgub, 64)
            dve.wait_ge(s_projfree, 10)
            for i in range(2):
                ins = dve.tensor_tensor(sgu_mix[:, i, :].rearrange("p (c q) -> p c q", c=TT),
                                        bank[:, 2 + i, :].rearrange("p (c q) -> p c q", c=TT),
                                        sgu_bias[:, i:i + 1, :].broadcast_to([P, TT, P]), ADD)
            then(ins)
            dve.tensor_tensor(sgu_out[:, :, :], sgu_mix, sgu_u, MUL).then_inc(s_early, 1)
            dve.wait_ge(s_early, 1)
            dve.wait_ge(s_convout, 2)

            dve.wait_ge(s_const, 16)
            chunked = "p (c n) -> p c n"
            for hp in range(HP):
                shift(r_, 0 + hp)
                shift(k_, 4 + hp)
                shift(v_, 8 + hp)
                dve.wait_ge(s_rawfree, 2 + 3 * hp + 3)
                then(dve.tensor_scalar(kk, k_, par_col(KK_ + hp), None, MUL))
                dve.tensor_tensor(sq, kk, kk, MUL).then_inc(s_sq, 1)
                dve.wait_ge(s_iclr, hp + 1)
                then(dve.tensor_scalar(kh, iclr, 1.0, par_col(KA_ + hp), SUB, MUL))
                then(dve.scalar_tensor_tensor(kh, kh, 1.0, k_, ADD, MUL))
                dve.scalar_tensor_tensor(kkn, r_, par_col(RK_ + hp), kh, MUL, MUL).then_inc(s_pr, 1)
                dve.wait_ge(s_decay, hp + 1)
                then(dve.memset(first_of_chunk, 0.0))
                then(dve.tensor_copy(first_of_chunk[:, ::HD], decay[:, ::HD]))
                then(dve.memset(decay[:, ::HD], 0.0))
                then(dve.tensor_tensor_scan(cum, decay, first_of_chunk, 0.0, MUL, ADD))
                dve.reciprocal(inv, cum)
                dve.wait_ge(s_norm, hp + 1)
                then(dve.tensor_scalar(norm, norm, 1e-12, None, MAX))
                then(dve.reciprocal(norm, norm))
                dve.wait_ge(s_bs, hp + 1)
                then(dve.scalar_tensor_tensor(kkn, kk, -1.0, norm, MUL, MUL))
                ar = arT.rearrange("p j n (c t) -> p j n c t", c=2)
                k5, c5 = (v.rearrange("p (j c t) -> p j c t", j=TT, c=2) for v in (kkn, cum))
                dve.tensor_tensor(ar[:, :, 0, :, 1:HD], k5[:, :, :, 1:HD], c5[:, :, :, 0:HD - 1], MUL)
                dve.tensor_copy(ar[:, :, 0, :, 0:1], k5[:, :, :, 0:1])
                dve.tensor_tensor(arT[:, :, 1, :], r_.rearrange("p (j t) -> p j t", j=TT), cum.rearrange("p (j t) -> p j t", j=TT), MUL)
                then(dve.tensor_tensor(norm, iclr, inv, MUL))
                dve.scalar_tensor_tensor(bT, kkn, -1.0, norm, MUL, MUL)
                then(dve.tensor_tensor(kT, kh, inv, MUL))
                end = cum.rearrange(chunked, c=CHUNKS)[:, :, HD - 1:HD].broadcast_to([P, CHUNKS, HD])
                dve.tensor_tensor(bH.rearrange(chunked, c=CHUNKS), bT.rearrange(chunked, c=CHUNKS), end, MUL)
                dve.tensor_tensor(kH.rearrange(chunked, c=CHUNKS), kT.rearrange(chunked, c=CHUNKS), end, MUL)
                dve.tensor_tensor(diag.rearrange(chunked, c=CHUNKS),
                                  C("ident_twice").unsqueeze(1).broadcast_to([P, CHUNKS, HD]), end, MUL)
                dve.tensor_tensor(bonus, bank[:, 3, :], v_, MUL).then_inc(s_ch, 1)

                if hp == 0:
                    dve.wait_ge(s_zero, 3)
                for n, (z, b) in enumerate(((BZ, 3), (KZ, 4))):
                    dve.wait_ge(s_tr, 4 * hp + 3 + n)
                    src = bank[:, b, :].rearrange("p (j h n) -> p h j n", j=TT, h=2)
                    for c in range(2):
                        rows_ = slice(HD * c, HD * c + HD)
                        ins = dve.tensor_copy(z[rows_, :, :, c, :], src[rows_])
                    ins.then_inc(s_tmd, 1)

                for g in range(2):
                    dve.wait_ge(s_sc, 2 * hp + g + 1)
                    ab = bank[:, 0:2, :].rearrange("p b (u n) -> p (b u) n", u=2)
                    ak = bank[:, 2:4, :].rearrange("p b (u n) -> p (b u) n", u=2)

                    def mask(name, n=P):
                        at = CONSTS[name][0]
                        return const[:, at:at + n].unsqueeze(1).broadcast_to([P, TT, n])

                    dve.tensor_tensor(G[g][1], ab[:, :, 0:P], mask("within16T"), MUL)
                    dve.tensor_tensor(G[g][4], ab[:, :, 0:P], mask("across16T"), MUL)
                    dve.tensor_tensor(rbT[:, g, :, :], ab[:, :, P:2 * P], mask("uptoT"), MUL)
                    dve.tensor_tensor(akrkT[:, g, :, :], ak, mask("beforeT", 2 * P), MUL)
                    dve.tensor_tensor(G[g][0], bank[:, 4, :].rearrange("p (j n) -> p j n", j=TT), mask("within16"), MUL).then_inc(s_scev, 1)
                dve.wait_ge(s_scev, 2 * hp + 2)
                for g in range(2):
                    ins = dve.tensor_tensor(G[g][5], G[g][1], mask("ident"), ADD)
                then(ins)

                def stage(n, f):
                    for g in range(2):
                        dve.wait_ge(s_dm, 24 * hp + 2 * (n - 1) + g + 1)
                        f(g, lambda b: bank[:, 3 * g + b, :].rearrange("p (j n) -> p j n", j=TT)).then_inc(s_dd, 1)

                def grow(g, b):
                    return dve.tensor_tensor(G[g][5], G[g][5], b(2), ADD)

                def grow_and_keep(g, b):
                    grow(g, b)
                    return dve.tensor_copy(G[g][1], b(1))

                stage(1, lambda g, b: dve.tensor_copy(G[g][3], b(1)))
                stage(2, grow_and_keep)
                dve.wait_ge(s_dd, 16 * hp + 4)
                stage(3, grow)
                dve.wait_ge(s_dd, 16 * hp + 6)
                stage(4, grow)
                for n in (7, 9, 11):
                    stage(n, lambda g, b: dve.tensor_tensor(G[g][0], b(0), G[g][1], ADD))
                stage(12, lambda g, b: dve.tensor_copy(gh[:, g, :, :], b(2)))

                for c in range(CHUNKS - 1):
                    dve.wait_ge(s_cm, (CHUNKS - 1) * hp + c + 1)
                    dve.wait_ge(s_init, 2 * hp + 2)
                    dve.tensor_copy(state[0:HD, c + 1, :, :],
                                    bank[0:HD, 0, P * (c % 2):P * (c % 2) + P].rearrange("p (h n) -> p h n", h=2)).then_inc(s_ce, 1)
                dve.wait_ge(s_mu, hp + 1)
                dve.wait_ge(s_y, hp + 1)
                then(dve.scalar_tensor_tensor(yc, bank[:, 4, :], -1.0 / HD, y_, MUL, ADD))
                dve.tensor_tensor(ysq, yc, yc, MUL).then_inc(s_yc, 1)
                dve.wait_ge(s_yroot, hp + 1)
                then(dve.reciprocal(yrs, yrs))
                then(dve.tensor_tensor(yn, yc, yrs, MUL))
                then(dve.tensor_scalar(yn, yn, par_col(GNG_S + hp), par_col(GNB + hp), MUL, ADD))
                then(dve.tensor_tensor(yn, yn, bonus, ADD))
                dve.tensor_tensor(rwkv_out[:, hp, :], yn, bank[:, 5, :], MUL).then_inc(s_out, 1)
                dve.wait_ge(s_out, hp + 1)

            for m in range(KT):
                dve.wait_ge(s_mm3, m + 1)
                if m == 0:
                    dve.wait_ge(s_projfree, phase_of_gate(GATE_TILES - 1) + 1)
                if m:
                    dve.wait_ge(s_merged, m)
                for n in range(3):
                    ins = dve.tensor_tensor(mtmp[:, n, :], bank[:, 3 * (m % 2) + n, :], gates[:, KT * n + m, :], MUL)
                ins.then_inc(s_m3, 1)
            dve.wait_ge(s_xtok, 16)
            for c in range(TT):
                for i in range(2):
                    n = 2 * c + i
                    dve.wait_ge(s_mx, n + 1)
                    part = x1[:, c, T * i:T * i + T]
                    dve.scalar_tensor_tensor(part, part, ALPHA, proj[:, n % 2, :], MUL, ADD).then_inc(s_pre, 1)
                dve.wait_ge(s_pre, 2 * c + 2)
                for i in range(2):
                    ins = dve.bn_stats(ln_stat[:, c, 6 * i:6 * i + 6], x1[:, c, T * i:T * i + T])
                then(ins)
                then(dve.bn_aggr(ln_mv[:, c, :], ln_stat[:, c, :]))
                dve.tensor_scalar(ln_rs[:, c:c + 1], ln_mv[:, c, 1:2], LN_EPS, None, ADD).then_inc(s_lnvar, 1)
                dve.wait_ge(s_lnroot, c + 1)
                then(dve.reciprocal(ln_rs[:, c:c + 1], ln_rs[:, c:c + 1]))
                then(dve.tensor_scalar(x1[:, c, :], x1[:, c, :], ln_mv[:, c, 0:1], ln_rs[:, c:c + 1], SUB, MUL))
                if c == 0:
                    dve.wait_ge(s_lnrows, 16)
                then(dve.tensor_tensor(x1[:, c, :], x1[:, c, :], ln_rows[:, 0, :], MUL))
                dve.tensor_tensor(x1[:, c, :], x1[:, c, :], ln_rows[:, 1, :], ADD).then_inc(s_x1, 1)

            def bc(name, shape, n=None):
                v = C(name) if n is None else C(name)[:, 0:n]
                return v.unsqueeze(1).broadcast_to([P, shape, n or CONSTS[name][1]])

            NG = TT * GROUPS
            dve.wait_ge(s_score, 1)
            dve.wait_ge(s_rw, 32)
            then(dve.tensor_tensor(sel[:, :, :], scores[:, :, :], rb_sb[:, :].unsqueeze(1).broadcast_to([P, TT, N_EXP]), ADD))
            sel_g = sel[:, :, :].rearrange("p c (g e) -> p (c g) e", g=GROUPS)
            for n in range(NG):
                ins = dve.max(top8[:, n, :], sel_g[:, n, :])
            then(ins)
            then(dve.tensor_tensor(grp[:, 0, :], top8[:, :, 0], top8[:, :, 1], ADD))
            g4 = [grp[:, n, :].rearrange("p (c g) -> p c g", c=TT) for n in range(3)]
            then(dve.tensor_reduce(small[:, 0, 0:TT], g4[0], AX_X, MAX))
            then(dve.tensor_tensor(g4[1], g4[0], small[:, 0, 0:TT].unsqueeze(2).broadcast_to([P, TT, GROUPS]), ALU.is_equal))
            then(dve.tensor_tensor(g4[1], g4[1], bc("group_left", TT), MUL))
            then(dve.tensor_reduce(small[:, 0, 0:TT], g4[1], AX_X, MAX))
            then(dve.tensor_tensor(g4[2], g4[1], small[:, 0, 0:TT].unsqueeze(2).broadcast_to([P, TT, GROUPS]), ALU.is_equal))
            then(dve.tensor_tensor(sel_g, sel_g, grp[:, 2, :].unsqueeze(2).broadcast_to([P, NG, PER_GROUP]), MUL))
            then(dve.tensor_scalar(grp[:, 1, :], grp[:, 2, :], 1.0, BIG, SUB, MUL))
            then(dve.tensor_tensor(sel_g, sel_g, grp[:, 1, :].unsqueeze(2).broadcast_to([P, NG, PER_GROUP]), ADD))
            best = small[:, 1, 0:TT]
            for k in range(TOPK):
                pick = hot[:, k, :, :]
                then(dve.tensor_reduce(best, sel[:, :, :], AX_X, MAX))
                then(dve.tensor_tensor(pick, sel[:, :, :], best.unsqueeze(2).broadcast_to([P, TT, N_EXP]), ALU.is_equal))
                then(dve.tensor_tensor(pick, pick, bc("expert_left", TT), MUL))
                then(dve.tensor_reduce(best, pick, AX_X, MAX))
                then(dve.tensor_tensor(pick, pick, best.unsqueeze(2).broadcast_to([P, TT, N_EXP]), ALU.is_equal))
                if k == 0:
                    then(dve.scalar_tensor_tensor(sel[:, :, :], pick, -3 * BIG, sel[:, :, :], MUL, ADD))
            dve.tensor_tensor(chosen[:, :, :], hot[:, 0, :, :], hot[:, 1, :, :], ADD).then_inc(s_chosen, 1)

            KC = TOPK * TT
            hot_f = hot[:, :, :, :].rearrange("p k c e -> p (k c) e")
            work = rt[0].rearrange("p (n e) -> p n e", n=KC)
            GATE_, RANK, QUOT, EXP_, BASE, PASS_, POS, TMP, FLAG = range(2, 11)

            def picked(dst, row):
                then(dve.tensor_tensor(work, hot_f, row, MUL))
                then(dve.tensor_reduce(small[:, dst, :], work, AX_X, ADD))

            work4 = work.rearrange("p (k c) e -> p k c e", k=TOPK)
            for k in range(TOPK):
                ins = dve.tensor_tensor(work4[:, k, :, :], hot[:, k, :, :], scores[:, :, :], MUL)
            then(ins)
            then(dve.tensor_reduce(small[:, GATE_, :], work, AX_X, ADD))
            then(dve.tensor_tensor(small[:, TMP, 0:TT], small[:, GATE_, 0:TT], small[:, GATE_, TT:KC], ADD))
            then(dve.reciprocal(small[:, TMP, 0:TT], small[:, TMP, 0:TT]))
            for k in range(TOPK):
                ins = dve.tensor_tensor(small[:, GATE_, k * TT:(k + 1) * TT], small[:, GATE_, k * TT:(k + 1) * TT], small[:, TMP, 0:TT], MUL)
            then(ins)
            dve.wait_ge(s_rank, 1)
            rank_ps = bank[:, 5, 0:TT * N_EXP].rearrange("p (c e) -> p c e", c=TT)
            for k in range(TOPK):
                ins = dve.tensor_tensor(work4[:, k, :, :], hot[:, k, :, :], rank_ps, MUL)
            then(ins)
            dve.tensor_reduce(small[:, RANK, :], work, AX_X, ADD)
            EXTRA, INCL, FIRST, ZERO = range(4)
            then(dve.tensor_scalar(count[:, EXTRA, :], bank[:, 5, TT * N_EXP:(TT + 1) * N_EXP], float(SLOTS), None, ALU.is_gt))
            then(dve.tensor_scalar(small[:, QUOT, :], small[:, RANK, :], float(SLOTS), None, ALU.is_ge))
            dve.memset(count[:, ZERO, :], 0.0)
            for n in range(2, T // SLOTS):
                dve.scalar_tensor_tensor(count[:, EXTRA, :], bank[:, 5, TT * N_EXP:(TT + 1) * N_EXP], float(SLOTS * n), count[:, EXTRA, :], ALU.is_gt, ADD).then_inc(s_dve, 1)
                dve.scalar_tensor_tensor(small[:, QUOT, :], small[:, RANK, :], float(SLOTS * n), small[:, QUOT, :], ALU.is_ge, ADD).then_inc(s_dve, 1)
                seq["n"] += 2
                dve.wait_ge(s_dve, seq["n"])
            then(dve.tensor_tensor_scan(count[:, INCL, :], count[:, EXTRA, :], count[:, ZERO, :], 0.0, ADD, ADD))
            then(dve.tensor_tensor(count[:, FIRST, :], count[:, INCL, :], count[:, EXTRA, :], SUB))
            then(dve.scalar_tensor_tensor(count[:, FIRST, :], count[:, FIRST, :], float(N_EXP - 1), C("iota")[:, 0:N_EXP], ADD, SUB))
            grid = rt[1][:, 0:128].rearrange("p (n e) -> p n e", n=4)
            for q in range(0, 16, 4):
                then(dve.tensor_tensor(grid, count[:, INCL, :].unsqueeze(1).broadcast_to([P, 4, N_EXP]),
                                       C("iota")[:, q:q + 4].unsqueeze(2).broadcast_to([P, 4, N_EXP]), ALU.is_le))
                then(dve.tensor_reduce(more_f[:, q:q + 4], grid, AX_X, ADD))
            dve.tensor_scalar(more_exp[:, :], more_f[:, :], float(N_EXP - 1), None, ALU.min).then_inc(s_tab, 1)
            dve.tensor_copy(more_i[:, :], count[:, INCL, N_EXP - 1:N_EXP]).then_inc(s_tab, 1)
            picked(EXP_, bc("iota", KC, N_EXP))
            picked(BASE, count[:, FIRST, :].unsqueeze(1).broadcast_to([P, KC, N_EXP]))
            then(dve.tensor_scalar(small[:, FLAG, :], small[:, QUOT, :], 0.0, None, ALU.is_gt))
            then(dve.tensor_tensor(small[:, TMP, :], small[:, BASE, :], small[:, QUOT, :], ADD))
            then(dve.tensor_tensor(small[:, TMP, :], small[:, TMP, :], small[:, FLAG, :], MUL))
            then(dve.tensor_tensor(small[:, PASS_, :], small[:, TMP, :], small[:, EXP_, :], ADD))
            then(dve.scalar_tensor_tensor(small[:, RANK, :], small[:, QUOT, :], -float(SLOTS), small[:, RANK, :], MUL, ADD))
            then(dve.scalar_tensor_tensor(small[:, POS, :], small[:, PASS_, :], float(SLOTS), small[:, RANK, :], MUL, ADD))
            dve.tensor_copy(pos_i[:, :], small[:, POS, :])
            for n in range(KC):
                c = n % TT
                dve.tensor_scalar(slot_hot[:, n, :], C("slot_iota"), small[:, RANK, n:n + 1], None, ALU.is_equal)
                of_pass, io = small[:, PASS_, n:n + 1], C("iota")[:, 0:PASSES]
                dve.tensor_scalar(pass_hot[:, n, 0, :], io, of_pass, None, ALU.is_equal)
                dve.tensor_scalar(pass_hot[:, n, 1, :], io, of_pass, C("token")[:, c:c + 1], ALU.is_equal, MUL)
                dve.tensor_scalar(pass_hot[:, n, 2, :], io, of_pass, small[:, GATE_, n:n + 1], ALU.is_equal, MUL).then_inc(s_hot, 1)
            dve.wait_ge(s_tabp, 1)
            tab = bank[:, 4, 0:3 * PASSES].rearrange("p (i q) -> p i q", i=3)
            dve.tensor_copy(gate_tab[:, :], tab[:, 2, :])
            then(dve.tensor_scalar(idx_f[:, :], tab[:, 0, :], 1.0, -4.0 * T, SUB, MUL))
            then(dve.scalar_tensor_tensor(idx_f[:, :], tab[:, 1, :], 2.0, idx_f[:, :], MUL, ADD))
            dve.tensor_scalar(idx_tab[:, :], idx_f[:, :], C("half"), None, ADD).then_inc(s_tab, 1)

            def one_pass(p, tokens_only=False):
                dve.wait_ge(s_hp, p + 1)
                dve.wait_ge(s_silu, p + 1)
                dve.tensor_tensor(h_e, h_silu, bank[:, 0, FE // 2:FE], MUL).then_inc(s_h, 1)
                turned(p + 1)
                dve.wait_ge(s_hTp, p + 1)
                dve.tensor_copy(hT, bank[:, 3, 0:FE // 2].rearrange("p (c s) -> p c s", c=2)).then_inc(s_hT, 1)

            def turned(p):
                dve.wait_ge(s_xeTp, p + 1)
                dve.tensor_copy(xeT, bank[:, 2, :].rearrange("p (c s) -> p c s", c=4)).then_inc(s_xeT, 1)

            turned(0)
            with dve.Fori(0, N_EXP) as i:
                one_pass(i)
            more = dve.value_load(more_i[0:1, 0:1], min_val=0, max_val=MORE)
            with dve.If(more > 0):
                with dve.Fori(0, more) as i:
                    one_pass(i + N_EXP)
            for c in range(TT):
                for k in range(TOPK):
                    dve.wait_ge(s_pair[TOPK * c + k], 16)
                dve.tensor_tensor(pair_y[:, 2 * c, :], pair_y[:, 2 * c, :], pair_y[:, 2 * c + 1, :], ADD).then_inc(s_sum, 1)
                dve.wait_ge(s_sum, c + 1)
                then(dve.scalar_tensor_tensor(x1[:, c, :], x1[:, c, :], ALPHA, pair_y[:, 2 * c, :], MUL, ADD))
                for i in range(2):
                    ins = dve.bn_stats(ln_stat[:, c, 6 * i:6 * i + 6], x1[:, c, T * i:T * i + T])
                then(ins)
                then(dve.bn_aggr(ln_mv[:, c, :], ln_stat[:, c, :]))
                dve.tensor_scalar(ln_rs[:, c:c + 1], ln_mv[:, c, 1:2], LN_EPS, None, ADD).then_inc(s_lnvar2, 1)
                dve.wait_ge(s_lnroot2, c + 1)
                then(dve.reciprocal(ln_rs[:, c:c + 1], ln_rs[:, c:c + 1]))
                then(dve.tensor_scalar(x1[:, c, :], x1[:, c, :], ln_mv[:, c, 0:1], ln_rs[:, c:c + 1], SUB, MUL))
                then(dve.tensor_tensor(x1[:, c, :], x1[:, c, :], ln_rows[:, 2, :], MUL))
                dve.tensor_tensor(x1[:, c, :], x1[:, c, :], ln_rows[:, 3, :], ADD).then_inc(s_x2, 1)

        @block.tensor
        def _(pe):
            st = {"phase": 0, "tile": 0}

            def open_phase():
                ph = st["phase"]
                st["phase"] += 1
                if ph >= 2:
                    pe.wait_ge(s_projfree, ph - 1)
                return ph % 2

            def tile_in():
                n = st["tile"]
                st["tile"] += 1
                pe.wait_ge(s_win[n % RING], 16 * (n // RING + 1))
                return n % RING

            def channels(w=P):
                slot, b = tile_in(), open_phase()
                for k in range(KT):
                    ins = pe.matmul(proj[0:w, b, :], ring[:, slot, k, 0:w], xT_sb[:, k, :], start=(k == 0), stop=(k == KT - 1))
                ins.then_inc(s_proj, 1)

            pe.wait_ge(s_x, 32)
            for _ in range(4):
                channels()
            slot = tile_in()
            tile_in()
            for c in range(TT):
                b = open_phase()
                for k in range(KT):
                    ins = pe.matmul(proj[:, b, 0:SGU], xT_sb[:, k, c * P:(c + 1) * P],
                                    ring[:, slot:slot + 2, k, :], start=(k == 0), stop=(k == KT - 1))
                ins.then_inc(s_proj, 1)
            for _ in range(2):
                channels()
            channels(LORA_W + LORA_A)
            channels(LORA_G)

            pe.wait_ge(s_vln, 1)
            pe.wait_ge(s_masked, 1)
            for g in range(4):
                for c in range(TT):
                    at = HD * (g % 2)
                    ins = pe.matmul(bank[at:at + HD, 2 + g // 2, c * P:(c + 1) * P], sgu_v[:, c, g * HD:(g + 1) * HD],
                                    sgu_w[:, g, :], start=True, stop=True)
            ins.then_inc(s_mix, 1)
            pe.wait_ge(s_const, 16)
            pe.wait_ge(s_convacc, 2 * TAPS)
            for i in range(2):
                ins = pe.matmul(bank[:, 0, :], C("ones"), conv_acc[:, i, :], start=(i == 0), stop=(i == 1))
            ins.then_inc(s_convsum, 1)
            pe.wait_ge(s_convsq, 2)
            for i in range(2):
                ins = pe.matmul(bank[:, 1, :], C("ones"), conv_sq[:, i, :], start=(i == 0), stop=(i == 1))
            ins.then_inc(s_convvar, 1)
            pe.wait_ge(s_early, 1)
            pe.wait_ge(s_convn, 2)

            gate = Gates()
            gate_at = {}

            def fill(n):
                for mm in gate.step(n):
                    k = mm % KT
                    if k == 0:
                        gate_at["slot"], gate_at["bank"] = tile_in(), open_phase()
                    ins = pe.matmul(proj[:, gate_at["bank"], :], ring[:, gate_at["slot"], k, :], xT_sb[:, k, :],
                                    start=(k == 0), stop=(k == KT - 1))
                    if k == KT - 1:
                        ins.then_inc(s_proj, 1)

            for hp in range(HP):
                ch = slice(P * hp, P * hp + P)
                if hp == 0:
                    pe.wait_ge(s_th, 2)
                    pe.wait_ge(s_par, 32)
                else:
                    pe.wait_ge(s_out, hp)
                pe.matmul(bank[:, 0, :], lora_sb[0:LORA_W, 0, ch], wl_al[0:LORA_W, :], start=True, stop=True)
                pe.matmul(bank[:, 1, :], lora_sb[LORA_W:LORA_W + LORA_A, 0, ch], wl_al[LORA_W:LORA_W + LORA_A, :],
                          start=True, stop=True).then_inc(s_z, 1)
                for _ in range(3):
                    channels()
                pe.wait_ge(s_sq, hp + 1)
                pe.matmul(bank[:, 2, :], C("head_ones"), sq, start=True, stop=True).then_inc(s_ss, 1)
                pe.wait_ge(s_pr, hp + 1)
                pe.matmul(bank[:, 3, :], C("head_ones"), kkn, start=True, stop=True).then_inc(s_bs, 1)
                fill(FILL["prep"])
                pe.wait_ge(s_ch, hp + 1)
                for b, src in ((2, arT[:, :, 0, :]), (5, v_.rearrange("p (j t) -> p j t", j=TT)),
                               (3, bH.rearrange("p (j t) -> p j t", j=TT)), (4, kH.rearrange("p (j t) -> p j t", j=TT))):
                    for j in range(TT):
                        ins = pe.transpose(bank[:, b, j * P:(j + 1) * P], src[:, j, :], C("ident"))
                    ins.then_inc(s_tr, 1)
                fill(FILL["turned"])
                for g in range(2):
                    h = slice(HD * g, HD * g + HD)
                    if g == 0:
                        pe.wait_ge(s_tma, 4 * hp + 4)
                        pe.wait_ge(s_tmd, 2 * hp + 2)
                    else:
                        pe.wait_ge(s_scev, 2 * hp + 1)
                    for j in range(TT):
                        t = slice(j * P, (j + 1) * P)
                        at = slice(2 * P * (j % 2), 2 * P * (j % 2) + 2 * P)
                        pe.matmul(bank[:, j // 2, at], bT[h, t], arT[h, j, :, :], start=True, stop=True)
                        pe.matmul(bank[:, 2 + j // 2, at], kT[h, t], arT[h, j, :, :], start=True, stop=True)
                        ins = pe.matmul(bank[:, 4, t], arT[h, j, 0, :], bT[h, t], start=True, stop=True)
                    ins.then_inc(s_sc, 1)
                    fill(FILL[f"scores{g}"])

                def stage(acts, dves, products):
                    for g in range(2):
                        if acts:
                            pe.wait_ge(s_da, 16 * hp + 2 * (acts - 1) + g + 1)
                        if dves:
                            pe.wait_ge(s_dd, 16 * hp + 2 * (dves - 1) + g + 1)
                        for b, terms, n in products(*G[g], g):
                            for j in range(TT):
                                for i, (lhsT, rhs) in enumerate(terms):
                                    ins = pe.matmul(bank[:, 3 * g + b, j * n:j * n + n], lhsT(j), rhs(j),
                                                    start=(i == 0), stop=(i == len(terms) - 1))
                        ins.then_inc(s_dm, 1)

                def of(t):
                    return lambda j: t[:, j, :]

                pe.wait_ge(s_scev, 2 * hp + 2)
                stage(0, 0, lambda d, dT, e, eT, nT, z, g: [(0, [(of(dT), of(d))], P), (1, [(of(d), of(dT))], P)])
                stage(1, 1, lambda d, dT, e, eT, nT, z, g: [(0, [(of(eT), of(e))], P), (1, [(of(e), of(eT))], P),
                                                          (2, [(of(e), of(z))], P)])
                stage(2, 2, lambda d, dT, e, eT, nT, z, g: [(0, [(of(dT), of(d))], P),
                                                          (1, [(lambda j: akrkT[:, g, j, 0:P], lambda j: VZ[:, g, j, HD:P])], HD),
                                                          (2, [(of(d), of(z))], P)])
                stage(3, 3, lambda d, dT, e, eT, nT, z, g: [(2, [(of(e), of(z))], P)])
                stage(0, 4, lambda d, dT, e, eT, nT, z, g: [(0, [(of(z), lambda j: X0[:, g, j, :])], P)])
                y = 1
                for it in range(3):
                    stage(4 + it, 4 + it if it else 0,
                          lambda d, dT, e, eT, nT, z, g: [(1, [(of(nT), of(d if it else dT))], P)])
                    stage(5 + it, 0, lambda d, dT, e, eT, nT, z, g: [(0, [(of(z), of(e))], P)])
                down = (C("head0_down"), C("head1_down"))
                stage(7, 7, lambda d, dT, e, eT, nT, z, g: [
                    (1, [(of(d), lambda j: rbT[:, g, j, :]), (lambda j: VZ[:, g, j, :], lambda j: akrkT[:, g, j, P:2 * P]),
                         (lambda j: down[g], lambda j: arT[:, j, 1, :])], P),
                    (2, [(of(d), lambda j: BZ[:, g, j, :, :]), (lambda j: VZ[:, g, j, :], lambda j: KZ[:, g, j, :, :]),
                         (lambda j: down[g], lambda j: diag[:, j * P:(j + 1) * P])], P)])
                pe.wait_ge(s_dd, 16 * hp + 16)
                pe.wait_ge(s_init, 2 * hp + 2)
                for c in range(CHUNKS - 1):
                    if c:
                        pe.wait_ge(s_ce, (CHUNKS - 1) * hp + c)
                    for h in range(2):
                        at = P * (c % 2) + HD * h
                        ins = pe.matmul(bank[0:HD, 0, at:at + HD], gh[:, h, c // 2, HD * (c % 2):HD * (c % 2) + HD],
                                        state[:, c, h, :], start=True, stop=True)
                    ins.then_inc(s_cm, 1)
                    fill(FILL["chain"])
                pe.wait_ge(s_ce, (CHUNKS - 1) * (hp + 1))
                pe.wait_ge(s_da, 16 * hp + 16)
                for h in range(2):
                    for c in range(CHUNKS):
                        ins = pe.matmul(bank[HD * h:HD * h + HD, 3, HD * c:HD * c + HD], state[:, c, h, :],
                                        out2[:, h, c // 2, HD * (c % 2):HD * (c % 2) + HD], start=True, stop=True)
                ins.then_inc(s_ymm, 1)
                fill(FILL["y"])
                pe.wait_ge(s_y, hp + 1)
                pe.matmul(bank[:, 5, :], lora_sb[0:LORA_G, 1, ch], gl[0:LORA_G, :], start=True, stop=True)
                pe.matmul(bank[:, 4, :], C("head_ones"), y_, start=True, stop=True).then_inc(s_mu, 1)
                fill(FILL["mean"])
                pe.wait_ge(s_yc, hp + 1)
                pe.matmul(bank[:, 1, :], C("head_ones"), ysq, start=True, stop=True).then_inc(s_var, 1)
                fill(FILL["var"])

            pe.wait_ge(s_out, HP)
            pe.wait_ge(s_wo, 16)
            for m in range(KT):
                if m >= 2:
                    pe.wait_ge(s_m3, m - 1)
                parts = [(0, rwkv_out, 0, 4), (1, sgu_out, 4, 2), (2, conv_out, 6, 2)]
                for n, src, k0, nk in parts:
                    for k in range(nk):
                        ins = pe.matmul(bank[:, 3 * (m % 2) + n, :], wo_sb[:, k0 + k, m * P:(m + 1) * P], src[:, k, :],
                                        start=(k == 0), stop=(k == nk - 1))
                ins.then_inc(s_mm3, 1)
            def mix(c):
                for i in range(2):
                    n = 2 * c + i
                    if n >= 2:
                        pe.wait_ge(s_pre, n - 1)
                    for k in range(KT):
                        if n == 0:
                            pe.wait_ge(s_merged, k + 1)
                        ins = pe.matmul(proj[:, n % 2, :], merged[:, k, c * P:(c + 1) * P], wout_sb[:, k, T * i:T * i + T],
                                        start=(k == 0), stop=(k == KT - 1))
                    ins.then_inc(s_mx, 1)

            def turn_x1(c):
                pe.wait_ge(s_x1, c + 1)
                if c >= 2:
                    pe.wait_ge(s_x1T, c - 1)
                for k in range(KT):
                    ins = pe.transpose(bank[:, 2 * (c % 2) + k // 4, P * (k % 4):P * (k % 4) + P], x1[:, c, k * P:(k + 1) * P], C("ident"))
                ins.then_inc(s_x1Tp, 1)

            def router(c):
                pe.wait_ge(s_x1T, c + 1)
                for k in range(KT):
                    ins = pe.matmul(bank[:, 4, c * N_EXP:(c + 1) * N_EXP], x1T[:, c % 2, k, :], rw_sb[:, k, :],
                                    start=(k == 0), stop=(k == KT - 1))
                if c == TT - 1:
                    ins.then_inc(s_scp, 1)

            pe.wait_ge(s_wout, 16)
            pe.wait_ge(s_projfree, st["phase"])
            mix(0)
            pe.wait_ge(s_m3, KT)
            pe.wait_ge(s_rw, 32)
            for c in range(TT):
                if c + 1 < TT:
                    mix(c + 1)
                turn_x1(c)
                if c:
                    router(c - 1)
            router(TT - 1)
            pe.wait_ge(s_chosen, 1)
            for c in range(TT):
                for n in range(c + 1):
                    pe.matmul(bank[:, 5, c * N_EXP:(c + 1) * N_EXP], C("earlier") if n == c else C("ones"), chosen[:, n, :],
                              start=(n == 0), stop=(n == c))
            for n in range(TT):
                ins = pe.matmul(bank[:, 5, TT * N_EXP:(TT + 1) * N_EXP], C("ones"), chosen[:, n, :], start=(n == 0), stop=(n == TT - 1))
            ins.then_inc(s_rank, 1)
            for n in range(TOPK * TT):
                pe.wait_ge(s_hot, n + 1)
                if n == 0:
                    pe.wait_ge(s_score, 1)
                ins = pe.matmul(bank[:, 4, 0:3 * PASSES], slot_hot[:, n, :], pass_hot[:, n, :, :], start=(n == 0), stop=(n == TOPK * TT - 1))
            ins.then_inc(s_tabp, 1)
            pe.wait_ge(s_tab, 3)

            def turn(p):
                pe.wait_ge(s_xe, p * 16 + 16)
                pe.wait_ge(s_xeT, p)
                for c in range(4):
                    ins = pe.transpose(bank[:, 2, c * P:(c + 1) * P], xe[:, c * P:(c + 1) * P], C("ident"))
                ins.then_inc(s_xeTp, 1)

            def one_pass(p, b, loads):
                pe.wait_ge(s_xeT, p + 1)
                gu = w_set[b][:, 0:GU].rearrange("p (k h i n) -> p k h i n", k=KT, h=2, i=2)
                for k in range(KT):
                    if k % 2 == 0:
                        pe.wait_ge(s_w[b][k // 2], loads)
                    for h in range(2):
                        ins = pe.matmul(bank[SLOTS * h:SLOTS * h + SLOTS, 0, :], xeT[:, k % 4, SLOTS * (k // 4):SLOTS * (k // 4) + SLOTS],
                                        gu[:, k, h, :, :], start=(k == 0), stop=(k == KT - 1))
                    if k == KT - 1:
                        ins.then_inc(s_hp, 1)
                    elif k % 2 == 1:
                        ins.then_inc(s_used, 1)
                turn(p + 1)
                pe.wait_ge(s_h, p + 1)
                for c in range(2):
                    ins = pe.transpose(bank[:, 3, c * P:(c + 1) * P], h_e[:, c * P:(c + 1) * P], C("ident"))
                ins.then_inc(s_hTp, 1)
                pe.sem_inc(s_used, 1)
                pe.wait_ge(s_hT, p + 1)
                pe.wait_ge(s_yfree, p + 1)
                wd = w_set[b][:, GU:].rearrange("p (f h n) -> p f h n", f=4, h=2)
                for f in range(4):
                    if f % 2 == 0:
                        pe.wait_ge(s_w[b][4 + f // 2], loads)
                    for h in range(2):
                        ins = pe.matmul(bank[SLOTS * h:SLOTS * h + SLOTS, 1, :], hT[:, f % 2, SLOTS * (f // 2):SLOTS * (f // 2) + SLOTS],
                                        wd[:, f, h, :], start=(f == 0), stop=(f == 3))
                    if f == 1:
                        ins.then_inc(s_used, 1)
                ins.then_inc(s_yp, 1)
                pe.wait_ge(s_yp, p + 1)
                pe.sem_inc(s_used, 1)

            turn(0)
            with pe.Fori(0, N_EXP // 2) as i:
                for b in range(2):
                    one_pass(i * 2 + b, b, i * 16 + 16)
            more = pe.value_load(more_i[0:1, 0:1], min_val=0, max_val=MORE)
            with pe.If(more > 0):
                with pe.Fori(0, more) as i:
                    one_pass(i + N_EXP, 0, i * 16 + 16 * (N_EXP // 2 + 1))


def tiles_of(v):
    return v.reshape(-1, P).T


def kernel(**inputs):
    import concourse.bacc as bacc
    from concourse.bass_utils import run_bass_kernel_spmd

    a = {k: np.asarray(v) for k, v in inputs.items()}
    mu = a["rwkv_mu"][0]
    cols = [tiles_of(mu[0:3 * RW])]
    for at, n in ((OFF_WL, LORA_W + LORA_A), (OFF_GL, LORA_G)):
        col = np.zeros((P, 1), np.float32)
        col[:n, 0] = mu[at:at + n]
        cols.append(col)
    for name in ("rwkv_w0", "rwkv_a0", "rwkv_k_k", "rwkv_k_a", "rwkv_r_k", "rwkv_gn_g", "rwkv_gn_b", "conv_db", "conv_ln_g", "conv_ln_b"):
        cols.append(tiles_of(a[name][0].reshape(-1)))
    dw = a["conv_dw"][0]
    cols += [dw[:, P * i:P * i + P].T for i in range(2)]
    lora = np.zeros((P, 2, RW), np.float32)
    lora[0:LORA_W, 0] = a["rwkv_w_up"][0]
    lora[LORA_W:LORA_W + LORA_A, 0] = a["rwkv_a_up"][0]
    lora[0:LORA_G, 1] = a["rwkv_g_up"][0]
    arrays = {
        "x_tok": a["x"][0],
        "xT": a["x"][0].T.reshape(KT, P, T).transpose(1, 0, 2),
        "w_in": a["w_in_first"],
        "par": np.concatenate(cols, 1),
        "table": TABLE,
        "lora": lora,
        "rows": np.concatenate([a[n].reshape(-1) for n in ("sgu_ln_g", "sgu_ln_b", "ln1_g", "ln1_b", "ln2_g", "ln2_b", "router_b")])[None],
        "sgu_b": a["sgu_b"][0],
        "sgu_wT": a["sgu_w"][0].transpose(2, 0, 1),
        "w_o": np.concatenate([a["rwkv_w_o"][0], a["sgu_w_o"][0], a["conv_w_o"][0]], 0),
        "w_out": a["w_out"][0],
        "router_w": a["router_w"],
        "zeros": np.zeros((SLOTS, D), np.float32),
        "w_gu": np.stack([a[n][0].reshape(N_EXP, KT, P, 2, FE // 2) for n in ("moe_w_gate", "moe_w_up")], 4)
                  .transpose(0, 2, 1, 3, 4, 5).reshape(N_EXP, P, GU),
        "w_down": a["moe_w_down"][0].reshape(N_EXP, FE // P, P, D).transpose(0, 2, 1, 3).reshape(N_EXP, P, WD),
    }
    nc = bacc.Bacc("TRN2", target_bir_lowering=False, num_devices=1)
    aps = []
    for name, v in arrays.items():
        arrays[name] = v = np.ascontiguousarray(v)
        aps.append(nc.dram_tensor(name, v.shape, mybir.dt.from_np(v.dtype), kind="ExternalInput").ap())
    out = nc.dram_tensor("out", (T, D), F32, kind="ExternalOutput").ap()
    program(nc, *aps, out)
    r = run_bass_kernel_spmd(nc, [arrays], core_ids=[0])
    return r.results[0]["out"].reshape(1, T, D)
```

```python
from contextlib import ExitStack

import numpy as np

import concourse.bass as bass
from concourse import mybir

F32 = mybir.dt.float32
I32 = mybir.dt.int32
U32 = mybir.dt.uint32
ALU = mybir.AluOpType
ACT = mybir.ActivationFunctionType
AX_X = mybir.AxisListType.X
ADD, SUB, MUL, MAX = ALU.add, ALU.subtract, ALU.mult, ALU.max

P = 128
T, D = 512, 1024
KT = D // P
TT = T // P
HD = 64
RW = 512
HP = RW // P
LORA_W, LORA_A, LORA_G = 32, 32, 96
SGU = 256
CONV, TAPS = 256, 31
OFF_WL = 3 * RW
OFF_GL = OFF_WL + LORA_W + LORA_A
OFF_SGU = OFF_GL + LORA_G
OFF_CONV = OFF_SGU + 2 * SGU
OFF_GATE = OFF_CONV + 2 * CONV
ALPHA = 2 ** 0.25
LN_EPS, GN_EPS = 1e-5, 64e-5
DECAY_SCALE = float(np.exp(-0.5))

N_EXP, GROUPS, TOPK, FE = 32, 4, 2, 512
PER_GROUP = N_EXP // GROUPS
SLOTS = 64
MORE = T * TOPK // SLOTS - 1
PASSES = N_EXP + MORE + 1
GU = KT * 2 * FE
WD = FE // P * D
CHUNK = 2 * 2 * FE
NCH = (GU + WD) // CHUNK
BIG = 1e30

MU, W0, A0, KK_, KA_, RK_, GNG, GNB, CDB, CLG, CLB, CDW = 0, 14, 18, 22, 26, 30, 34, 38, 42, 44, 46, 48
N_PAR = CDW + 2 * TAPS

CONSTS = {}


def constant_table():
    i, j = np.arange(P)[:, None], np.arange(P)[None, :]
    same64, same16 = i // 64 == j // 64, i // 16 == j // 16
    ic, jc = i % HD, np.arange(HD)[None, :]
    blocks = {
        "ident": i == j,
        "within16": same16 & (j < i),
        "within16T": same16 & (i < j),
        "across16": same64 & ~same16 & (j < i),
        "beforeT": ic < jc,
        "uptoT": ic <= jc,
        "head_ones": same64,
        "ident_twice": (i % 64) == np.arange(64)[None, :],
        "ones": np.ones((P, P), bool),
        "earlier": i < j,
        "slot_iota": j % SLOTS + 0 * i,
        "iota": np.arange(64)[None, :] + np.zeros((P, 1)),
        "expert_left": N_EXP - np.arange(N_EXP)[None, :] + np.zeros((P, 1)),
        "group_left": GROUPS - np.arange(GROUPS)[None, :] + np.zeros((P, 1)),
        "token": np.arange(P)[:, None] + P * np.arange(TT)[None, :],
        "half": np.arange(P)[:, None] // SLOTS,
    }
    at, parts = 0, []
    for name, b in blocks.items():
        CONSTS[name] = (at, b.shape[1])
        at += b.shape[1]
        parts.append(b.astype(np.float32))
    return np.ascontiguousarray(np.concatenate(parts, 1))


TABLE = constant_table()

FILL = {"prep": 14, "turned": 2, "scores": 4, "solve": 1, "chain": 1, "y": 3, "mean": 3, "var": 0}
CHUNKS = T // HD
PER_PAIR = (3 * D // P // HP) * KT
FILL["var"] = PER_PAIR - sum(v * {"chain": CHUNKS - 1, "solve": 6}.get(k, 1) for k, v in FILL.items())
GATE_TILES = 3 * D // P
assert FILL["var"] >= 0


def column_tiles():
    tiles = [(OFF_CONV + P * i, P) for i in range(4)]
    tiles += [(OFF_SGU + SGU + P * i, P) for i in range(2)]
    tiles += [(OFF_SGU + P * i, P) for i in range(2)]
    tiles += [(OFF_WL, LORA_W + LORA_A), (OFF_GL, LORA_G)]
    g = 0
    for hp in range(HP):
        tiles += [(RW * n + P * hp, P) for n in range(3)]
        tiles += [(OFF_GATE + P * (g + i), P) for i in range(GATE_TILES // HP)]
        g += GATE_TILES // HP
    return tiles


TILES = column_tiles()
RING = 4
V_TILES = (4, 5)


def phase_after(tile):
    if tile < 4:
        return tile + 1
    if tile < 6:
        return 8
    return tile + 3



class Gates:

    def __init__(self):
        self.done = 0

    def step(self, n):
        first = self.done
        self.done += n
        return range(first, self.done)


def phase_of_gate(g):
    per = GATE_TILES // HP
    return 12 + (3 + per) * (g // per) + 3 + g % per


def tile_of_phase(ph):
    return ph if ph < 4 else (4 if ph < 8 else ph - 2)


def program(nc, x_tok, xT, w_in, par, table, lora, rows, sgu_b, sgu_wT, w_o, w_out, router_w, zeros, w_gu, w_down, out):
    with ExitStack() as ctx:
        def sb(name, shape, dt=F32):
            return ctx.enter_context(nc.sbuf_tensor(name, shape, dt))

        def sem(name):
            return ctx.enter_context(nc.semaphore(name))

        const = sb("const", [P, TABLE.shape[1]])
        par_sb = sb("par_sb", [P, N_PAR + 8])
        lora_sb = sb("lora_sb", [P, 2, RW])
        xT_sb = sb("xT_sb", [P, KT, T])
        ring = sb("ring", [P, RING, KT, P])
        gates = sb("gates", [P, GATE_TILES, T])
        sgu_out = sb("sgu_out", [P, 2, T])
        conv_out = sb("conv_out", [P, 2, T])
        rwkv_out = sb("rwkv_out", [P, HP, T])
        raw = sb("raw", [P, 2, T + 1])
        wl_al = sb("wl_al", [P, T])
        gl = sb("gl", [P, T])
        ARENA = 23700
        arena = sb("arena", [P, ARENA])
        proj = ctx.enter_context(nc.psum_tensor("proj", [P, 2, T], F32))
        bank = ctx.enter_context(nc.psum_tensor("bank", [P, 6, T], F32))

        def C(name):
            at, n = CONSTS[name]
            return const[:, at:at + n]

        def par_col(c):
            return par_sb[:, c:c + 1]

        CLG_S, GNG_S, EPS_CONV, EPS_GN = N_PAR, N_PAR + 2, N_PAR + 6, N_PAR + 7

        class Cut:
            def __init__(self, base):
                self.at = base

            def __call__(self, n, **split):
                v = arena[:, self.at:self.at + n]
                self.at += n
                assert self.at <= ARENA, self.at
                return v.rearrange(split["r"], **split["k"]) if split else v

        cut = Cut(0)
        conv_val = cut(2 * T, r="p (i t) -> p i t", k=dict(i=2))
        conv_gate = cut(2 * T, r="p (i t) -> p i t", k=dict(i=2))
        PADDED = T + TAPS - 1
        conv_in = cut(2 * PADDED, r="p (i t) -> p i t", k=dict(i=2))
        conv_acc = cut(2 * T, r="p (i t) -> p i t", k=dict(i=2))
        conv_sq = cut(2 * T, r="p (i t) -> p i t", k=dict(i=2))
        conv_rs = cut(T)
        sgu_u = cut(2 * T, r="p (i t) -> p i t", k=dict(i=2))
        sgu_v = cut(TT * SGU, r="p (c d) -> p c d", k=dict(c=TT))
        sgu_w = cut(4 * P, r="p (g q) -> p g q", k=dict(g=4))
        sgu_ln = cut(2 * SGU, r="p (i d) -> p i d", k=dict(i=2))
        sgu_bias = cut(2 * P, r="p (i q) -> p i q", k=dict(i=2))
        sgu_mix = cut(2 * T, r="p (i t) -> p i t", k=dict(i=2))
        sgu_stat = cut(TT * 6, r="p (c s) -> p c s", k=dict(c=TT))
        sgu_mv = cut(TT * 2, r="p (c s) -> p c s", k=dict(c=TT))
        sgu_rs = cut(TT)

        cut = Cut(0)
        r_, k_ = cut(T), cut(T)
        iclr, decay = cut(T), cut(T)
        kk, sq = cut(T), cut(T)
        v_, cum, kh, inv, norm, kkn = (cut(T) for _ in range(6))
        bT, kT, bH, kH, bonus = (cut(T) for _ in range(5))
        ar = cut(3 * T, r="p (n t) -> p n t", k=dict(n=3))
        diag = [cut(T) for _ in range(2)]
        carry = cut(T)
        KS, VS = (slice(0, HD), slice(HD, P)), (slice(HD, P), slice(0, HD))

        def per_chunk(n):
            return cut(8 * n, r="p (h j n) -> p h j n", k=dict(h=2, j=TT))

        X0, Y0, Y1, Y2 = (per_chunk(P) for _ in range(4))
        V, AK = (per_chunk(HD) for _ in range(2))
        BR, KR = (per_chunk(P) for _ in range(2))
        L16, L16T, LX, ZT = (per_chunk(P) for _ in range(4))
        E, ET = (arena[:, at:at + 2 * T].rearrange("p (h j n) -> p h j n", h=2, j=TT) for at in (8 * T, 10 * T))
        out2 = arena[:, 0:2 * T].rearrange("p (h j n) -> p h j n", h=2, j=TT)
        gh = arena[:, 2 * T:4 * T].rearrange("p (h j n) -> p h j n", h=2, j=TT)
        state = arena[:, 4 * T:6 * T].rearrange("p (c h n) -> p c h n", c=CHUNKS, h=2)
        y_, yc, ysq, yrs, yn = bT, kT, bH, kH, cum

        cut = Cut(0)
        wout_sb = cut(KT * D, r="p (k n) -> p k n", k=dict(k=KT))
        merged = cut(KT * T, r="p (k t) -> p k t", k=dict(k=KT))
        wo_sb = cut(8 * D, r="p (k n) -> p k n", k=dict(k=8))
        mtmp = cut(3 * T, r="p (i t) -> p i t", k=dict(i=3))
        ln_stat = cut(TT * 12, r="p (c s) -> p c s", k=dict(c=TT))
        ln_mv = cut(TT * 2, r="p (c s) -> p c s", k=dict(c=TT))
        ln_rs = cut(TT)
        x1 = ring[:, :, :, :].rearrange("p s k c -> p s (k c)")
        ln_rows = xT_sb[:, :, :].rearrange("p k t -> p (k t)").rearrange("p (i d) -> p i d", i=4)

        small_end = cut.at
        w_set = [gates[:, :, :].rearrange("p g t -> p (g t)"), arena[:, 0:GU + WD]]
        assert KT * D + KT * T == GU + WD == GATE_TILES * T
        cut = Cut(KT * D + KT * T)
        x1T = cut(2 * KT * P, r="p (b k t) -> p b k t", k=dict(b=2, k=KT))
        slot_hot = cut(8 * P, r="p (n s) -> p n s", k=dict(n=8))
        pass_hot = cut(8 * 3 * PASSES, r="p (n i q) -> p n i q", k=dict(n=8, i=3))
        xe = cut(T)
        xeT = cut(T, r="p (c s) -> p c s", k=dict(c=4))
        h_silu, h_e = cut(FE // 2), cut(FE // 2)
        hT = cut(FE // 2, r="p (c s) -> p c s", k=dict(c=2))
        y_e = cut(T)
        assert cut.at <= KT * D + KT * T + 8 * D
        cut = Cut(small_end)
        rt = [cut(2 * TT * N_EXP) for _ in range(4)]
        assert cut.at <= ARENA
        pair_y = arena[:, 0:8 * D].rearrange("p (n d) -> p n d", n=8)
        lora_flat, raw_flat = lora_sb[:, :, :].rearrange("p i n -> p (i n)"), raw[:, :, :].rearrange("p i n -> p (i n)")
        place = {"lora": 0, "raw": 0}

        def late(where, flat, n):
            at = place[where]
            place[where] += n
            return flat[:, at:at + n]

        rw_sb = late("lora", lora_flat, KT * N_EXP).rearrange("p (k e) -> p k e", k=KT)
        rb_sb = late("lora", lora_flat, N_EXP)
        scores = late("lora", lora_flat, TT * N_EXP).rearrange("p (c e) -> p c e", c=TT)
        sel = late("lora", lora_flat, TT * N_EXP).rearrange("p (c e) -> p c e", c=TT)
        top8 = late("lora", lora_flat, TT * GROUPS * 8).rearrange("p (n e) -> p n e", e=8)
        grp = late("lora", lora_flat, 3 * TT * GROUPS).rearrange("p (i n) -> p i n", i=3)
        hot = late("lora", lora_flat, TOPK * TT * N_EXP).rearrange("p (k c e) -> p k c e", k=TOPK, c=TT)
        assert place["lora"] <= 2 * RW
        chosen = late("raw", raw_flat, TT * N_EXP).rearrange("p (c e) -> p c e", c=TT)
        small = late("raw", raw_flat, 12 * TOPK * TT).rearrange("p (i n) -> p i n", i=12)
        count = late("raw", raw_flat, 6 * N_EXP).rearrange("p (i n) -> p i n", i=6)
        gate_tab, idx_f, more_f = (late("raw", raw_flat, n) for n in (PASSES, PASSES, 16))
        idx_tab, idx_now, pos_i, more_i, more_exp = (late("raw", raw_flat, n).bitcast(I32) for n in (PASSES, 1, TOPK * TT, 1, 16))
        assert place["raw"] <= 2 * (T + 1)
        x1_dram = nc.dram_tensor("x1_rows", (T * 2, D // 2), F32).ap()
        y_dram = nc.dram_tensor("y_rows", (PASSES * SLOTS, D), F32).ap()

        s_const, s_par, s_x, s_small, s_lnrows, s_sgub = map(sem, ["const_in", "par_in", "xT_in", "sgu_par_in", "ln_rows_in", "sgu_bias_in"])
        s_win = [sem(f"ring_in{i}") for i in range(RING)]
        s_proj = sem("proj_done")
        s_projfree = sem("proj_read")
        s_rawfree = sem("raw_read")
        s_dve = sem("dve_seq")
        s_pool = sem("pool_seq")
        s_masked = sem("sgu_w_masked")
        s_convin, s_pads = sem("conv_in_ready"), sem("pads_zeroed")
        s_scaled = sem("gains_scaled")
        s_convacc, s_convsum, s_convsq, s_convvar, s_convn = map(sem, ["conv_acc", "conv_sum", "conv_sq", "conv_var", "conv_norm"])
        s_convout = sem("conv_out_ready")
        s_vln, s_mix, s_sguout = map(sem, ["v_normed", "mixed_in_psum", "sgu_out_ready"])
        s_early = sem("early_done")
        s_vstat, s_vroot, s_convroot = map(sem, ["v_variance", "v_deviation", "conv_deviation"])
        s_norm, s_yroot, s_lnvar, s_lnroot = map(sem, ["kk_norm", "y_deviation", "ln_variance", "ln_deviation"])
        s_lora, s_th = sem("lora_shifted"), sem("lora_activated")
        s_z, s_iclr, s_decay = map(sem, ["z_in_psum", "iclr_ready", "decay_ready"])
        s_sq, s_ss, s_pr, s_bs, s_ch = map(sem, ["kk_squared", "kk_norm_psum", "rk_product", "bonus_psum", "channels_ready"])
        s_v = sem("v_ready")
        s_tr, s_tma, s_tmd = map(sem, ["turned", "turned_out_act", "turned_out_dve"])
        s_sc, s_scev = sem("scores_psum"), sem("scores_out")
        s_dm, s_da, s_dd = sem("solve_psum"), sem("solve_out_act"), sem("solve_out_dve")
        s_init, s_diag, s_out2 = sem("state_init"), sem("chunk_products_ready"), sem("output_maps_ready")
        s_zero, s_cumlog, s_cum = sem("zeros_set"), sem("decay_logs_summed"), sem("decay_products_ready")
        s_cm, s_ce = sem("chain_psum"), sem("chain_out")
        s_ymm, s_y, s_mu, s_yc, s_var, s_out = map(sem, ["y_psum", "y_out", "y_mean", "y_centred", "y_var", "pair_done"])
        s_wo, s_wout, s_xtok = map(sem, ["w_o_in", "w_out_in", "x_tok_in"])
        s_mm3, s_mread, s_m3, s_merged = map(sem, ["branches_psum", "branches_read", "products_ready", "merged_ready"])
        s_mx, s_pre = sem("mixed_psum"), sem("residual_added")
        s_x1, s_st = sem("x1_ready"), sem("stored")
        s_yfree = sem("ye_bank_free")
        s_begun, s_ypad = sem("gathers_begun"), sem("y_rows_zeroed")
        s_x1st, s_rw = sem("x1_stored"), sem("router_par_in")
        s_x1Tp, s_x1T, s_scp, s_score = map(sem, ["x1T_psum", "x1T_out", "scores_in_psum", "scores_ready"])
        s_chosen, s_rank, s_hot, s_tabp, s_tab, s_idxf = map(sem, ["chosen_ready", "rank_psum", "one_hots_ready", "table_psum", "tables_ready", "indices_float"])
        s_w = [[sem(f"w_in{b}_{c}") for c in range(NCH)] for b in range(2)]
        s_used = sem("w_used")
        s_idx, s_xe, s_xe0 = sem("index_ready"), sem("tokens_in"), sem("tokens_zeroed")
        s_xeTp, s_xeT, s_hp, s_silu, s_h, s_hTp, s_hT, s_yp, s_ye, s_yst = map(
            sem, ["xeT_psum", "xeT_out", "h_psum", "silu_ready", "h_ready", "hT_psum", "hT_out", "ye_psum", "ye_ready", "ye_stored"])
        s_pair, s_sum, s_sum2, s_x2 = [sem(f"pair_in{n}") for n in range(8)], sem("pairs_summed"), sem("residual2"), sem("x2_ready")
        s_lnvar2, s_lnroot2 = sem("ln2_variance"), sem("ln2_deviation")

        block = ctx.enter_context(nc.Block())

        @block.sync
        def _(sp):
            sp.dma_start(const[:, :], table).then_inc(s_const, 16)
            wv = w_in.rearrange("(k p) c -> p k c", p=P)
            for n, (c0, w) in enumerate(TILES):
                if n >= RING:
                    sp.wait_ge(s_proj, phase_after(n - RING))
                sp.dma_start(ring[:, n % RING, :, 0:w], wv[:, :, c0:c0 + w]).then_inc(s_win[n % RING], 16)
                if n == 0:
                    for k in range(0, KT, 4):
                        sp.dma_start(xT_sb[:, k:k + 4, :], xT[:, k:k + 4, :]).then_inc(s_x, 16)
            for q in range(N_EXP, PASSES):
                sp.dma_start(y_dram[q * SLOTS:(q + 1) * SLOTS, :], zeros).then_inc(s_ypad, 16)
            sp.wait_ge(s_proj, phase_after(len(TILES) - 1))
            sp.dma_start(x1, x_tok.rearrange("(c p) d -> p c d", p=P)).then_inc(s_xtok, 16)
            sp.dma_start(ln_rows, rows[:, 2 * SGU:2 * SGU + 4 * D].partition_broadcast(P).rearrange("p a (i d) -> p (a i) d", i=4)).then_inc(s_lnrows, 16)
            sp.wait_ge(s_dm, 18 * HP)
            sp.dma_start(wo_sb, w_o.rearrange("(k p) n -> p k n", p=P)).then_inc(s_wo, 16)
            sp.wait_ge(s_out, HP)
            sp.dma_start(rw_sb[:, :, :], router_w.rearrange("(k p) e -> p k e", p=P)).then_inc(s_rw, 16)
            sp.dma_start(rb_sb[:, :], rows[:, 2 * SGU + 4 * D:].partition_broadcast(P).rearrange("p a e -> p (a e)")).then_inc(s_rw, 16)
            sp.dma_start(wout_sb, w_out.rearrange("(k p) n -> p k n", p=P)).then_inc(s_wout, 16)
            def chunk_src(e, c):
                n = c * CHUNK
                return w_gu[e, :, n:n + CHUNK] if n < GU else w_down[e, :, n - GU:n - GU + CHUNK]

            def load(b, c, e):
                sp.dma_start(w_set[b][:, c * CHUNK:(c + 1) * CHUNK], chunk_src(e, c)).then_inc(s_w[b][c], 16)

            sp.wait_ge(s_m3, KT)
            for c in range(NCH):
                load(0, c, 0)
            for c in range(TT):
                sp.wait_ge(s_x1, c + 1)
                sp.dma_start(x1_dram.rearrange("(t h) d -> t (h d)", h=2)[c * P:(c + 1) * P, :], x1[:, c, :]).then_inc(s_x1st, 16)
            sp.wait_ge(s_mx, 2 * TT)
            for c in range(NCH):
                load(1, c, 1)
            with sp.Fori(1, N_EXP // 2) as i:
                for b in range(2):
                    for c in range(NCH):
                        sp.wait_ge(s_used, i * (2 * NCH) + (b - 2) * NCH + c + 1)
                        e = sp.snap(i * 2 + b, min_val=0, max_val=N_EXP - 1)
                        n = c * CHUNK
                        src = w_gu[bass.ds(e, 1), :, n:n + CHUNK] if n < GU else w_down[bass.ds(e, 1), :, n - GU:n - GU + CHUNK]
                        sp.dma_start(w_set[b][:, n:n + CHUNK], src.rearrange("a p n -> (a p) n")).then_inc(s_w[b][c], 16)
            sp.wait_ge(s_tab, 3)
            more = sp.value_load(more_i[0:1, 0:1], min_val=0, max_val=MORE)
            with sp.If(more > 0):
                with sp.Fori(0, more) as i:
                    e = sp.value_load(more_exp[0:1, bass.ds(i, 1)], min_val=0, max_val=N_EXP - 1)
                    for c in range(NCH):
                        sp.wait_ge(s_used, i * NCH + (N_EXP - 1) * NCH + c + 1)
                        n = c * CHUNK
                        src = w_gu[bass.ds(e, 1), :, n:n + CHUNK] if n < GU else w_down[bass.ds(e, 1), :, n - GU:n - GU + CHUNK]
                        sp.dma_start(w_set[0][:, n:n + CHUNK], src.rearrange("a p n -> (a p) n")).then_inc(s_w[0][c], 16)
            for c in range(TT):
                sp.wait_ge(s_x2, c + 1)
                sp.dma_start(out[c * P:(c + 1) * P, :], x1[:, c, :]).then_inc(s_st, 16)
            sp.wait_ge(s_st, 16 * TT)

        @block.gpsimd
        def _(pool):
            pool.dma_start(sgu_w, sgu_wT).then_inc(s_small, 16)
            pool.dma_start(sgu_ln, rows[:, 0:2 * SGU].partition_broadcast(P).rearrange("p a (i d) -> p (a i) d", i=2)).then_inc(s_small, 16)
            for g in range(4):
                pool.dma_start(sgu_bias[HD * (g % 2):HD * (g % 2) + HD, g // 2, :],
                               sgu_b[g:g + 1, :].partition_broadcast(HD).rearrange("p a q -> p (a q)")).then_inc(s_sgub, 16)
            pool.memset(conv_in[:, :, 0:TAPS - 1], 0.0).then_inc(s_pads, 1)
            pool.memset(raw[:, :, 0:1], 0.0).then_inc(s_pads, 1)
            pool.wait_ge(s_small, 32)
            pool.affine_select(out=sgu_w, in_=sgu_w, compare_op=ALU.is_ge, fill=0.0, base=0,
                               pattern=[[0, 4], [1, P]], channel_multiplier=-1).then_inc(s_masked, 1)
            pool.wait_ge(s_early, 1)
            pool.wait_ge(s_convout, 2)
            for n, z in enumerate((ar[VS[0], 1, :], ar[VS[1], 2, :], diag[0][VS[0], :], diag[1][VS[1], :])):
                pool.memset(z, 0.0).then_inc(s_zero, 1)
                pool.wait_ge(s_zero, n + 1)
            for hp in range(HP):
                pool.wait_ge(s_ch, hp + 1)
                if hp:
                    pool.wait_ge(s_out, hp)
                else:
                    pool.wait_ge(s_const, 16)
                for h in range(2):
                    pool.memset(state[KS[h], 0, h, :], 0.0).then_inc(s_init, 1)
                    pool.wait_ge(s_init, 4 * hp + 2 * h + 1)
                    pool.tensor_copy(state[VS[h], :, h, :],
                                     C("ident_twice")[VS[h], :].unsqueeze(1).broadcast_to([HD, CHUNKS, HD])).then_inc(s_init, 1)
                    pool.wait_ge(s_init, 4 * hp + 2 * h + 2)
                for h in range(2):
                    end = cum[KS[h], :].rearrange("p (c n) -> p c n", c=CHUNKS)[:, :, HD - 1:HD].broadcast_to([HD, CHUNKS, HD])
                    pool.tensor_tensor(diag[h][KS[h], :].rearrange("p (c n) -> p c n", c=CHUNKS),
                                       C("ident_twice")[KS[h], :].unsqueeze(1).broadcast_to([HD, CHUNKS, HD]), end, MUL).then_inc(s_diag, 1)
                    pool.wait_ge(s_diag, 2 * hp + h + 1)
            pool.wait_ge(s_init, 4 * HP)
            for m in range(KT):
                pool.wait_ge(s_m3, m + 1)
                pool.tensor_tensor(mtmp[:, 0, :], mtmp[:, 0, :], mtmp[:, 1, :], ADD).then_inc(s_pool, 1)
                pool.wait_ge(s_pool, m + 1)
                pool.tensor_tensor(merged[:, m, :], mtmp[:, 0, :], mtmp[:, 2, :], ADD).then_inc(s_merged, 1)
            pool.wait_ge(s_ypad, 16 * (PASSES - N_EXP))
            pool.wait_ge(s_mm3, KT)
            pool.wait_ge(s_merged, KT)
            pool.memset(xe, 0.0).then_inc(s_xe0, 1)
            pool.wait_ge(s_tab, 3)
            pool.wait_ge(s_xe0, 1)
            pool.wait_ge(s_x1st, 16 * TT)

            last_half_row, last_row = pool.to_reg(2 * T - 1), pool.to_reg(PASSES * SLOTS - 1)

            def gather(p):
                pool.tensor_copy(idx_now[:, 0:1], idx_tab[:, bass.ds(p, 1)]).then_inc(s_idx, 1)
                pool.wait_ge(s_idx, p + 1)
                pool.sem_inc(s_begun, 1)
                pool.indirect_dma_start(xe, None, x1_dram, bass.IndirectOffsetOnAxis(ap=idx_now[:, 0:1], axis=0),
                                        bounds_check=last_half_row, oob_is_err=False).then_inc(s_xe, 16)

            gather(0)
            with pool.Fori(0, N_EXP) as i:
                pool.wait_ge(s_xe, i * 16 + 16)
                pool.wait_ge(s_xeTp, i + 1)
                gather(i + 1)
            more = pool.value_load(more_i[0:1, 0:1], min_val=0, max_val=MORE)
            with pool.If(more > 0):
                with pool.Fori(0, more) as i:
                    pool.wait_ge(s_xe, i * 16 + 16 * (N_EXP + 1))
                    pool.wait_ge(s_xeTp, i + N_EXP + 1)
                    gather(i + N_EXP + 1)
            pool.wait_ge(s_xe, more * 16 + 16 * (N_EXP + 1))
            pool.wait_ge(s_yst, more * 32 + 32 * N_EXP)
            pool.sem_inc(s_begun, 1)
            for c in range(TT):
                for k in range(TOPK):
                    n = TOPK * c + k
                    pool.indirect_dma_start(pair_y[:, n, :], None, y_dram,
                                            bass.IndirectOffsetOnAxis(ap=pos_i[:, k * TT + c:k * TT + c + 1], axis=0),
                                            bounds_check=last_row, oob_is_err=False).then_inc(s_pair[n], 16)

        @block.scalar
        def _(act):
            act.dma_start(par_sb[:, 0:N_PAR], par).then_inc(s_par, 16)
            act.dma_start(lora_sb[:, :, :], lora).then_inc(s_par, 16)
            state_ = {"phase": 0, "raw": 0, "seq": 0}

            def take(out, func, rows_=P, **kw):
                ph = state_["phase"]
                act.wait_ge(s_proj, ph + 1)
                n = SGU if 4 <= ph < 8 else T
                act.activation(out, proj[0:rows_, ph % 2, 0:n], func, **kw).then_inc(s_projfree, 1)
                state_["phase"] += 1

            def take_raw(rows_=P):
                n = state_["raw"]
                if n == 0:
                    act.wait_ge(s_pads, 2)
                if n >= 2:
                    act.wait_ge(s_rawfree, n - 1)
                ph = state_["phase"]
                act.wait_ge(s_proj, ph + 1)
                act.activation(raw[0:rows_, n % 2, 1:T + 1], proj[0:rows_, ph % 2, :], ACT.Copy).then_inc(s_projfree, 1)
                state_["phase"] += 1
                state_["raw"] += 1

            for i in range(2):
                take(conv_val[:, i, :], ACT.Copy)
            for i in range(2):
                take(conv_gate[:, i, :], ACT.Sigmoid)
            for c in range(TT):
                take(sgu_v[:, c, :], ACT.Gelu)
            for i in range(2):
                take(sgu_u[:, i, :], ACT.Gelu)
            take_raw(LORA_W + LORA_A)
            take_raw(LORA_G)
            act.wait_ge(s_vstat, 1)
            act.activation(sgu_rs, sgu_rs, ACT.Sqrt).then_inc(s_vroot, 1)
            act.wait_ge(s_lora, 2)
            act.activation(wl_al[0:LORA_W, :], wl_al[0:LORA_W, :], ACT.Tanh).then_inc(s_th, 1)
            act.activation(gl[0:LORA_G, :], gl[0:LORA_G, :], ACT.Sigmoid).then_inc(s_th, 1)
            act.wait_ge(s_scaled, 1)
            act.wait_ge(s_convvar, 1)
            act.activation(conv_rs, bank[:, 1, :], ACT.Sqrt, bias=par_col(EPS_CONV)).then_inc(s_convroot, 1)
            for i in range(2):
                act.wait_ge(s_convn, i + 1)
                act.wait_ge(s_scaled, 1)
                act.activation(conv_out[:, i, :], conv_sq[:, i, :], ACT.Silu, bias=par_col(CLB + i),
                               scale=par_col(CLG_S + i)).then_inc(s_convout, 1)
            act.wait_ge(s_early, 1)

            gate = Gates()

            def evac_gates(n):
                for mm in gate.step(n):
                    if mm % KT == KT - 1:
                        g = mm // KT
                        assert state_["phase"] == phase_of_gate(g)
                        take(gates[:, g, :], ACT.Sigmoid)

            for hp in range(HP):
                act.wait_ge(s_z, hp + 1)
                act.activation(decay, bank[:, 0, :], ACT.Sigmoid, bias=par_col(W0 + hp)).then_inc(s_decay, 1)
                act.activation(iclr, bank[:, 1, :], ACT.Sigmoid, bias=par_col(A0 + hp)).then_inc(s_iclr, 1)
                take_raw()
                act.wait_ge(s_cumlog, hp + 1)
                act.activation(cum, inv, ACT.Exp, scale=-DECAY_SCALE)
                act.activation(inv, inv, ACT.Exp, scale=DECAY_SCALE).then_inc(s_cum, 1)
                take_raw()
                take_raw()
                act.wait_ge(s_ss, hp + 1)
                act.activation(norm, bank[:, 2, :], ACT.Sqrt).then_inc(s_norm, 1)
                evac_gates(FILL["prep"])
                act.wait_ge(s_tr, 4 * hp + 1)
                for h in range(2):
                    act.activation(X0[:, h, :, KS[h]],
                                   bank[:, 2, :].rearrange("p (j c) -> p j c", j=TT)[:, :, h * HD:(h + 1) * HD],
                                   ACT.Copy).then_inc(s_tma, 1)
                act.wait_ge(s_tr, 4 * hp + 2)
                act.activation(V, bank[:, 5, :].rearrange("p (j h n) -> p h j n", j=TT, h=2), ACT.Copy).then_inc(s_tma, 1)
                evac_gates(FILL["turned"])
                evac_gates(FILL["scores"])

                def out(stage, *copies):
                    for g in range(2):
                        act.wait_ge(s_dm, 18 * hp + 2 * (stage - 1) + g + 1)
                        for dst, b in copies:
                            d = dst(g)
                            n = d.shape[-1]
                            ins = act.activation(d, bank[:, 3 * g + b, 0:TT * n].rearrange("p (j n) -> p j n", j=TT), ACT.Copy)
                        ins.then_inc(s_da, 1)

                out(1, (lambda g: E[:, g], 0))
                out(2, (lambda g: L16[:, g], 0))
                out(3, (lambda g: E[:, g], 0), (lambda g: X0[:, g, :, VS[g]], 1))
                for n in (3, 4):
                    evac_gates(FILL["solve"])
                out(5, (lambda g: Y0[:, g], 0))
                for n in (5, 6, 7, 8):
                    evac_gates(FILL["solve"])
                evac_gates(FILL["chain"] * (CHUNKS - 1))
                evac_gates(FILL["y"])
                act.wait_ge(s_ymm, hp + 1)
                act.activation(y_, bank[:, 3, :], ACT.Copy).then_inc(s_y, 1)
                evac_gates(FILL["mean"])
                act.wait_ge(s_var, hp + 1)
                act.activation(yrs, bank[:, 1, :], ACT.Sqrt, bias=par_col(EPS_GN)).then_inc(s_yroot, 1)
                evac_gates(FILL["var"])
            for c in range(TT):
                act.wait_ge(s_lnvar, c + 1)
                act.activation(ln_rs[:, c:c + 1], ln_rs[:, c:c + 1], ACT.Sqrt).then_inc(s_lnroot, 1)
                act.wait_ge(s_x1Tp, c + 1)
                b = 2 * (c % 2)
                act.activation(x1T[:, c % 2, :, :], bank[:, b:b + 2, :].rearrange("p b (k t) -> p (b k) t", k=4), ACT.Copy).then_inc(s_x1T, 1)
            act.wait_ge(s_scp, 1)
            act.activation(scores[:, :, :], bank[:, 4, 0:TT * N_EXP].rearrange("p (c e) -> p c e", c=TT), ACT.Sigmoid).then_inc(s_score, 1)

            act.wait_ge(s_tab, 3)
            act.sem_inc(s_yfree, 1)

            def one_pass(p):
                act.wait_ge(s_hp, p + 1)
                act.activation(h_silu, bank[:, 0, 0:FE // 2], ACT.Silu).then_inc(s_silu, 1)
                act.wait_ge(s_yp, p + 1)
                act.activation(y_e, bank[:, 1, :], ACT.Copy, scale=gate_tab[:, bass.ds(p, 1)]).then_inc(s_ye, 1)
                act.wait_ge(s_ye, p + 1)
                act.sem_inc(s_yfree, 1)
                dst = y_dram.rearrange("(q s) (h d) -> q h s d", s=SLOTS, h=2)
                for h in range(2):
                    act.dma_start(dst[bass.ds(p, 1), h, :, :].rearrange("q s d -> (q s) d"), y_e[SLOTS * h:SLOTS * h + SLOTS, :]).then_inc(s_yst, 16)
                act.wait_ge(s_yst, p * 32 + 32)

            with act.Fori(0, N_EXP) as i:
                one_pass(i)
            more = act.value_load(more_i[0:1, 0:1], min_val=0, max_val=MORE)
            with act.If(more > 0):
                with act.Fori(0, more) as i:
                    one_pass(i + N_EXP)
            for c in range(TT):
                act.wait_ge(s_lnvar2, c + 1)
                act.activation(ln_rs[:, c:c + 1], ln_rs[:, c:c + 1], ACT.Sqrt).then_inc(s_lnroot2, 1)

        @block.vector
        def _(dve):
            seq = {"n": 0, "raw": 0}

            def then(ins):
                seq["n"] += 1
                ins.then_inc(s_dve, 1)
                dve.wait_ge(s_dve, seq["n"])

            dve.wait_ge(s_par, 32)
            dve.tensor_scalar(par_sb[:, CLG_S:CLG_S + 2], par_sb[:, CLG:CLG + 2], CONV ** 0.5, None, MUL)
            dve.memset(par_sb[:, EPS_CONV:EPS_CONV + 1], CONV * LN_EPS)
            dve.memset(par_sb[:, EPS_GN:EPS_GN + 1], HD * GN_EPS)
            dve.tensor_scalar(par_sb[:, GNG_S:GNG_S + 4], par_sb[:, GNG:GNG + 4], HD ** 0.5, None, MUL).then_inc(s_scaled, 1)
            dve.wait_ge(s_scaled, 1)

            dve.wait_ge(s_projfree, 4)
            dve.wait_ge(s_pads, 2)
            for i in range(2):
                dve.tensor_tensor(conv_in[:, i, TAPS - 1:PADDED], conv_val[:, i, :], conv_gate[:, i, :], MUL).then_inc(s_convin, 1)
            dve.wait_ge(s_convin, 2)
            for tap in range(TAPS):
                for i in range(2):
                    src, w = conv_in[:, i, tap:tap + T], par_col(CDW + TAPS * i + tap)
                    if tap >= 1:
                        dve.wait_ge(s_convacc, 2 * tap + i - 1)
                    if tap == 0:
                        ins = dve.tensor_scalar(conv_acc[:, i, :], src, w, par_col(CDB + i), MUL, ADD)
                    else:
                        ins = dve.scalar_tensor_tensor(conv_acc[:, i, :], src, w, conv_acc[:, i, :], MUL, ADD)
                    ins.then_inc(s_convacc, 1)

            def shift(dst, mu, rows_=P, done=None):
                n = seq["raw"]
                seq["raw"] += 1
                ph = 10 + n if n < 2 else 12 + (3 + GATE_TILES // HP) * ((n - 2) // 3) + (n - 2) % 3
                dve.wait_ge(s_projfree, ph + 1)
                now, before = raw[0:rows_, n % 2, 1:T + 1], raw[0:rows_, n % 2, 0:T]
                then(dve.tensor_tensor(dst, before, now, SUB))
                dve.scalar_tensor_tensor(dst, dst, par_sb[0:rows_, MU + mu:MU + mu + 1], now, MUL, ADD).then_inc(s_rawfree, 1)

            dve.wait_ge(s_projfree, 8)
            for c in range(TT):
                ins = dve.bn_stats(sgu_stat[:, c, :], sgu_v[:, c, :])
            then(ins)
            for c in range(TT):
                ins = dve.bn_aggr(sgu_mv[:, c, :], sgu_stat[:, c, :])
            then(ins)
            dve.tensor_scalar(sgu_rs, sgu_mv[:, :, 1], LN_EPS, None, ADD).then_inc(s_vstat, 1)
            dve.wait_ge(s_vroot, 1)
            then(dve.reciprocal(sgu_rs, sgu_rs))
            for c in range(TT):
                ins = dve.tensor_scalar(sgu_v[:, c, :], sgu_v[:, c, :], sgu_mv[:, c, 0:1], sgu_rs[:, c:c + 1], SUB, MUL)
            then(ins)
            dve.wait_ge(s_small, 32)
            then(dve.tensor_tensor(sgu_v, sgu_v, sgu_ln[:, 0:1, :].broadcast_to([P, TT, SGU]), MUL))
            dve.tensor_tensor(sgu_v, sgu_v, sgu_ln[:, 1:2, :].broadcast_to([P, TT, SGU]), ADD).then_inc(s_vln, 1)

            shift(wl_al[0:LORA_W + LORA_A, :], 12, LORA_W + LORA_A)
            shift(gl[0:LORA_G, :], 13, LORA_G)
            dve.wait_ge(s_rawfree, 2)
            dve.sem_inc(s_lora, 2)

            dve.wait_ge(s_convsum, 1)
            for i in range(2):
                ins = dve.scalar_tensor_tensor(conv_acc[:, i, :], bank[:, 0, :], -1.0 / CONV, conv_acc[:, i, :], MUL, ADD)
            then(ins)
            for i in range(2):
                dve.tensor_tensor(conv_sq[:, i, :], conv_acc[:, i, :], conv_acc[:, i, :], MUL).then_inc(s_convsq, 1)
            dve.wait_ge(s_convroot, 1)
            then(dve.reciprocal(conv_rs, conv_rs))
            for i in range(2):
                dve.tensor_tensor(conv_sq[:, i, :], conv_acc[:, i, :], conv_rs, MUL).then_inc(s_convn, 1)

            dve.wait_ge(s_mix, 1)
            dve.wait_ge(s_sgub, 64)
            dve.wait_ge(s_projfree, 10)
            for i in range(2):
                ins = dve.tensor_tensor(sgu_mix[:, i, :].rearrange("p (c q) -> p c q", c=TT),
                                        bank[:, 2 + i, :].rearrange("p (c q) -> p c q", c=TT),
                                        sgu_bias[:, i:i + 1, :].broadcast_to([P, TT, P]), ADD)
            then(ins)
            dve.tensor_tensor(sgu_out[:, :, :], sgu_mix, sgu_u, MUL).then_inc(s_early, 1)
            dve.wait_ge(s_early, 1)
            dve.wait_ge(s_convout, 2)

            dve.wait_ge(s_const, 16)
            chunked = "p (c n) -> p c n"
            then(dve.memset(carry, 1.0))
            then(dve.memset(carry[:, ::HD], 0.0))
            for hp in range(HP):
                dve.wait_ge(s_decay, hp + 1)
                dve.tensor_tensor_scan(inv, carry, decay, 0.0, MUL, ADD).then_inc(s_cumlog, 1)
                shift(r_, 0 + hp)
                shift(k_, 4 + hp)
                dve.wait_ge(s_rawfree, 2 + 3 * hp + 2)
                then(dve.tensor_scalar(kk, k_, par_col(KK_ + hp), None, MUL))
                dve.tensor_tensor(sq, kk, kk, MUL).then_inc(s_sq, 1)
                dve.wait_ge(s_iclr, hp + 1)
                then(dve.tensor_scalar(kh, iclr, 1.0, par_col(KA_ + hp), SUB, MUL))
                then(dve.scalar_tensor_tensor(kh, kh, 1.0, k_, ADD, MUL))
                dve.scalar_tensor_tensor(kkn, r_, par_col(RK_ + hp), kh, MUL, MUL).then_inc(s_pr, 1)
                shift(v_, 8 + hp)
                dve.wait_ge(s_norm, hp + 1)
                then(dve.tensor_scalar(norm, norm, 1e-12, None, MAX))
                then(dve.reciprocal(norm, norm))
                dve.wait_ge(s_cum, hp + 1)
                dve.wait_ge(s_bs, hp + 1)
                then(dve.scalar_tensor_tensor(kkn, kk, -1.0, norm, MUL, MUL))
                k3, c3, a3 = (v.rearrange(chunked, c=CHUNKS) for v in (kkn, cum, ar[:, 0, :]))
                dve.tensor_tensor(a3[:, :, 1:HD], k3[:, :, 1:HD], c3[:, :, 0:HD - 1], MUL)
                dve.tensor_copy(a3[:, :, 0:1], k3[:, :, 0:1])
                for h in range(2):
                    dve.tensor_tensor(ar[KS[h], 1 + h, :], r_[KS[h], :], cum[KS[h], :], MUL)
                then(dve.tensor_tensor(norm, iclr, inv, MUL))
                dve.scalar_tensor_tensor(bT, kkn, -1.0, norm, MUL, MUL)
                then(dve.tensor_tensor(kT, kh, inv, MUL))
                end = cum.rearrange(chunked, c=CHUNKS)[:, :, HD - 1:HD].broadcast_to([P, CHUNKS, HD])
                dve.tensor_tensor(bH.rearrange(chunked, c=CHUNKS), bT.rearrange(chunked, c=CHUNKS), end, MUL)
                dve.tensor_tensor(kH.rearrange(chunked, c=CHUNKS), kT.rearrange(chunked, c=CHUNKS), end, MUL)
                dve.wait_ge(s_rawfree, 2 + 3 * hp + 3)
                dve.tensor_tensor(bonus, bank[:, 3, :], v_, MUL).then_inc(s_ch, 1)

                for n, dst in enumerate((BR, KR)):
                    dve.wait_ge(s_tr, 4 * hp + 3 + n)
                    dve.tensor_copy(dst[:, :, :, 0:HD], bank[:, 3 + n, :].rearrange("p (j h n) -> p h j n", j=TT, h=2)).then_inc(s_tmd, 1)

                dve.wait_ge(s_sc, hp + 1)

                def mask(name, n=P):
                    at = CONSTS[name][0]
                    return const[:, at:at + n].unsqueeze(1).broadcast_to([P, 2 * TT, n])

                def both(t):
                    return t.rearrange("p h j n -> p (h j) n")

                def spread(src, name, dst):
                    return dve.tensor_tensor(both(dst).rearrange("p u (c n) -> p u c n", c=2), src.unsqueeze(2).broadcast_to([P, 2 * TT, 2, HD]),
                                             mask(name).rearrange("p u (c n) -> p u c n", c=2), MUL)

                ab, back = (bank[:, b:b + 2, :].rearrange("p h (j n) -> p (h j) n", j=TT) for b in (0, 3))
                spread(ab[:, :, 0:HD], "within16T", L16T)
                spread(back[:, :, 0:HD], "within16", L16)
                spread(back[:, :, 0:HD], "across16", LX)
                dve.tensor_tensor(both(BR)[:, :, HD:P], ab[:, :, HD:P], mask("uptoT", HD), MUL).then_inc(s_scev, 1)
                dve.wait_ge(s_scev, 3 * hp + 1)
                dve.tensor_tensor(both(ZT), both(L16T), mask("ident"), ADD).then_inc(s_scev, 1)
                for h in range(2):
                    ak = bank[:, 2 + 3 * h, :].rearrange("p (j n) -> p j n", j=TT)
                    dve.tensor_tensor(AK[:, h], ak[:, :, 0:HD], mask("beforeT", HD)[:, 0:TT, :], MUL)
                    ins = dve.tensor_tensor(KR[:, h, :, HD:P], ak[:, :, HD:P], mask("uptoT", HD)[:, 0:TT, :], MUL)
                ins.then_inc(s_scev, 1)
                dve.wait_ge(s_scev, 3 * hp + 2)

                def stage(n, f):
                    for g in range(2):
                        dve.wait_ge(s_dm, 18 * hp + 2 * (n - 1) + g + 1)
                        f(g, lambda b, n=P: bank[:, 3 * g + b, 0:TT * n].rearrange("p (j n) -> p j n", j=TT)).then_inc(s_dd, 1)

                def grow(g, b):
                    return dve.tensor_tensor(ZT[:, g], ZT[:, g], b(2), ADD)

                def grow_and_keep(g, b):
                    grow(g, b)
                    return dve.tensor_copy(L16T[:, g], b(1))

                stage(1, lambda g, b: dve.tensor_copy(ET[:, g], b(1)))
                stage(2, grow_and_keep)
                dve.wait_ge(s_dd, 18 * hp + 4)
                stage(3, grow)
                dve.wait_ge(s_dd, 18 * hp + 6)
                stage(4, grow)
                stage(5, lambda g, b: dve.tensor_copy(ET[:, g], b(2)))
                stage(6, lambda g, b: dve.tensor_tensor(Y1[:, g], b(1, P), Y0[:, g], ADD))
                stage(7, lambda g, b: dve.tensor_tensor(Y2[:, g], b(0, P), Y0[:, g], ADD))
                stage(8, lambda g, b: dve.tensor_tensor(Y1[:, g], b(1, P), Y0[:, g], ADD))
                dve.wait_ge(s_diag, 2 * hp + 2)
                def maps(n, g, dst, own):
                    src = bank[:, 3 * g + 1:3 * g + 3, :].rearrange("p c (j w n) -> p w j c n", j=TT, w=2)[:, n]
                    return dve.tensor_tensor(dst[:, g].rearrange("p j (c n) -> p j c n", c=2), src, own.rearrange("p (j c n) -> p j c n", j=TT, c=2), ADD)

                stage(9, lambda g, b: maps(0, g, gh, diag[g]))

                dve.wait_ge(s_init, 4 * hp + 4)
                for c in range(CHUNKS - 1):
                    for h in range(2):
                        dve.wait_ge(s_cm, 2 * (CHUNKS - 1) * hp + 2 * c + h + 1)
                        dve.tensor_copy(state[KS[h], c + 1, h, :], bank[KS[h], 0, HD * (c % 2):HD * (c % 2) + HD]).then_inc(s_ce, 1)
                    if c in (1, 3):
                        g = c // 2
                        maps(1, g, out2, ar[:, 1 + g, :]).then_inc(s_out2, 1)
                dve.wait_ge(s_mu, hp + 1)
                dve.wait_ge(s_y, hp + 1)
                then(dve.scalar_tensor_tensor(yc, bank[:, 4, :], -1.0 / HD, y_, MUL, ADD))
                dve.tensor_tensor(ysq, yc, yc, MUL).then_inc(s_yc, 1)
                dve.wait_ge(s_yroot, hp + 1)
                then(dve.reciprocal(yrs, yrs))
                then(dve.tensor_tensor(yn, yc, yrs, MUL))
                then(dve.tensor_scalar(yn, yn, par_col(GNG_S + hp), par_col(GNB + hp), MUL, ADD))
                then(dve.tensor_tensor(yn, yn, bonus, ADD))
                dve.tensor_tensor(rwkv_out[:, hp, :], yn, bank[:, 5, :], MUL).then_inc(s_out, 1)
                dve.wait_ge(s_out, hp + 1)

            for m in range(KT):
                dve.wait_ge(s_mm3, m + 1)
                if m == 0:
                    dve.wait_ge(s_projfree, phase_of_gate(GATE_TILES - 1) + 1)
                if m:
                    dve.wait_ge(s_merged, m)
                for n in range(3):
                    ins = dve.tensor_tensor(mtmp[:, n, :], bank[:, 3 * (m % 2) + n, :], gates[:, KT * n + m, :], MUL)
                ins.then_inc(s_m3, 1)
            dve.wait_ge(s_xtok, 16)
            for c in range(TT):
                for i in range(2):
                    n = 2 * c + i
                    dve.wait_ge(s_mx, n + 1)
                    part = x1[:, c, T * i:T * i + T]
                    dve.scalar_tensor_tensor(part, part, ALPHA, proj[:, n % 2, :], MUL, ADD).then_inc(s_pre, 1)
                dve.wait_ge(s_pre, 2 * c + 2)
                for i in range(2):
                    ins = dve.bn_stats(ln_stat[:, c, 6 * i:6 * i + 6], x1[:, c, T * i:T * i + T])
                then(ins)
                then(dve.bn_aggr(ln_mv[:, c, :], ln_stat[:, c, :]))
                dve.tensor_scalar(ln_rs[:, c:c + 1], ln_mv[:, c, 1:2], LN_EPS, None, ADD).then_inc(s_lnvar, 1)
                dve.wait_ge(s_lnroot, c + 1)
                then(dve.reciprocal(ln_rs[:, c:c + 1], ln_rs[:, c:c + 1]))
                then(dve.tensor_scalar(x1[:, c, :], x1[:, c, :], ln_mv[:, c, 0:1], ln_rs[:, c:c + 1], SUB, MUL))
                if c == 0:
                    dve.wait_ge(s_lnrows, 16)
                then(dve.tensor_tensor(x1[:, c, :], x1[:, c, :], ln_rows[:, 0, :], MUL))
                dve.tensor_tensor(x1[:, c, :], x1[:, c, :], ln_rows[:, 1, :], ADD).then_inc(s_x1, 1)

            def bc(name, shape, n=None):
                v = C(name) if n is None else C(name)[:, 0:n]
                return v.unsqueeze(1).broadcast_to([P, shape, n or CONSTS[name][1]])

            NG = TT * GROUPS
            dve.wait_ge(s_score, 1)
            dve.wait_ge(s_rw, 32)
            then(dve.tensor_tensor(sel[:, :, :], scores[:, :, :], rb_sb[:, :].unsqueeze(1).broadcast_to([P, TT, N_EXP]), ADD))
            sel_g = sel[:, :, :].rearrange("p c (g e) -> p (c g) e", g=GROUPS)
            for n in range(NG):
                ins = dve.max(top8[:, n, :], sel_g[:, n, :])
            then(ins)
            then(dve.tensor_tensor(grp[:, 0, :], top8[:, :, 0], top8[:, :, 1], ADD))
            g4 = [grp[:, n, :].rearrange("p (c g) -> p c g", c=TT) for n in range(3)]
            then(dve.tensor_reduce(small[:, 0, 0:TT], g4[0], AX_X, MAX))
            then(dve.tensor_tensor(g4[1], g4[0], small[:, 0, 0:TT].unsqueeze(2).broadcast_to([P, TT, GROUPS]), ALU.is_equal))
            then(dve.tensor_tensor(g4[1], g4[1], bc("group_left", TT), MUL))
            then(dve.tensor_reduce(small[:, 0, 0:TT], g4[1], AX_X, MAX))
            then(dve.tensor_tensor(g4[2], g4[1], small[:, 0, 0:TT].unsqueeze(2).broadcast_to([P, TT, GROUPS]), ALU.is_equal))
            then(dve.tensor_tensor(sel_g, sel_g, grp[:, 2, :].unsqueeze(2).broadcast_to([P, NG, PER_GROUP]), MUL))
            then(dve.tensor_scalar(grp[:, 1, :], grp[:, 2, :], 1.0, BIG, SUB, MUL))
            then(dve.tensor_tensor(sel_g, sel_g, grp[:, 1, :].unsqueeze(2).broadcast_to([P, NG, PER_GROUP]), ADD))
            best = small[:, 1, 0:TT]
            for k in range(TOPK):
                pick = hot[:, k, :, :]
                then(dve.tensor_reduce(best, sel[:, :, :], AX_X, MAX))
                then(dve.tensor_tensor(pick, sel[:, :, :], best.unsqueeze(2).broadcast_to([P, TT, N_EXP]), ALU.is_equal))
                then(dve.tensor_tensor(pick, pick, bc("expert_left", TT), MUL))
                then(dve.tensor_reduce(best, pick, AX_X, MAX))
                then(dve.tensor_tensor(pick, pick, best.unsqueeze(2).broadcast_to([P, TT, N_EXP]), ALU.is_equal))
                if k == 0:
                    then(dve.scalar_tensor_tensor(sel[:, :, :], pick, -3 * BIG, sel[:, :, :], MUL, ADD))
            dve.tensor_tensor(chosen[:, :, :], hot[:, 0, :, :], hot[:, 1, :, :], ADD).then_inc(s_chosen, 1)

            KC = TOPK * TT
            hot_f = hot[:, :, :, :].rearrange("p k c e -> p (k c) e")
            work = rt[0].rearrange("p (n e) -> p n e", n=KC)
            GATE_, RANK, QUOT, EXP_, BASE, PASS_, POS, TMP, FLAG = range(2, 11)

            def picked(dst, row):
                then(dve.tensor_tensor(work, hot_f, row, MUL))
                then(dve.tensor_reduce(small[:, dst, :], work, AX_X, ADD))

            work4 = work.rearrange("p (k c) e -> p k c e", k=TOPK)
            for k in range(TOPK):
                ins = dve.tensor_tensor(work4[:, k, :, :], hot[:, k, :, :], scores[:, :, :], MUL)
            then(ins)
            then(dve.tensor_reduce(small[:, GATE_, :], work, AX_X, ADD))
            then(dve.tensor_tensor(small[:, TMP, 0:TT], small[:, GATE_, 0:TT], small[:, GATE_, TT:KC], ADD))
            then(dve.reciprocal(small[:, TMP, 0:TT], small[:, TMP, 0:TT]))
            for k in range(TOPK):
                ins = dve.tensor_tensor(small[:, GATE_, k * TT:(k + 1) * TT], small[:, GATE_, k * TT:(k + 1) * TT], small[:, TMP, 0:TT], MUL)
            then(ins)
            dve.wait_ge(s_rank, 1)
            rank_ps = bank[:, 5, 0:TT * N_EXP].rearrange("p (c e) -> p c e", c=TT)
            for k in range(TOPK):
                ins = dve.tensor_tensor(work4[:, k, :, :], hot[:, k, :, :], rank_ps, MUL)
            then(ins)
            dve.tensor_reduce(small[:, RANK, :], work, AX_X, ADD)
            EXTRA, INCL, FIRST, ZERO = range(4)
            then(dve.tensor_scalar(count[:, EXTRA, :], bank[:, 5, TT * N_EXP:(TT + 1) * N_EXP], float(SLOTS), None, ALU.is_gt))
            then(dve.tensor_scalar(small[:, QUOT, :], small[:, RANK, :], float(SLOTS), None, ALU.is_ge))
            dve.memset(count[:, ZERO, :], 0.0)
            for n in range(2, T // SLOTS):
                dve.scalar_tensor_tensor(count[:, EXTRA, :], bank[:, 5, TT * N_EXP:(TT + 1) * N_EXP], float(SLOTS * n), count[:, EXTRA, :], ALU.is_gt, ADD).then_inc(s_dve, 1)
                dve.scalar_tensor_tensor(small[:, QUOT, :], small[:, RANK, :], float(SLOTS * n), small[:, QUOT, :], ALU.is_ge, ADD).then_inc(s_dve, 1)
                seq["n"] += 2
                dve.wait_ge(s_dve, seq["n"])
            then(dve.tensor_tensor_scan(count[:, INCL, :], count[:, EXTRA, :], count[:, ZERO, :], 0.0, ADD, ADD))
            then(dve.tensor_tensor(count[:, FIRST, :], count[:, INCL, :], count[:, EXTRA, :], SUB))
            then(dve.scalar_tensor_tensor(count[:, FIRST, :], count[:, FIRST, :], float(N_EXP - 1), C("iota")[:, 0:N_EXP], ADD, SUB))
            grid = rt[1][:, 0:128].rearrange("p (n e) -> p n e", n=4)
            for q in range(0, 16, 4):
                then(dve.tensor_tensor(grid, count[:, INCL, :].unsqueeze(1).broadcast_to([P, 4, N_EXP]),
                                       C("iota")[:, q:q + 4].unsqueeze(2).broadcast_to([P, 4, N_EXP]), ALU.is_le))
                then(dve.tensor_reduce(more_f[:, q:q + 4], grid, AX_X, ADD))
            dve.tensor_scalar(more_exp[:, :], more_f[:, :], float(N_EXP - 1), None, ALU.min).then_inc(s_tab, 1)
            dve.tensor_copy(more_i[:, :], count[:, INCL, N_EXP - 1:N_EXP]).then_inc(s_tab, 1)
            picked(EXP_, bc("iota", KC, N_EXP))
            picked(BASE, count[:, FIRST, :].unsqueeze(1).broadcast_to([P, KC, N_EXP]))
            then(dve.tensor_scalar(small[:, FLAG, :], small[:, QUOT, :], 0.0, None, ALU.is_gt))
            then(dve.tensor_tensor(small[:, TMP, :], small[:, BASE, :], small[:, QUOT, :], ADD))
            then(dve.tensor_tensor(small[:, TMP, :], small[:, TMP, :], small[:, FLAG, :], MUL))
            then(dve.tensor_tensor(small[:, PASS_, :], small[:, TMP, :], small[:, EXP_, :], ADD))
            then(dve.scalar_tensor_tensor(small[:, RANK, :], small[:, QUOT, :], -float(SLOTS), small[:, RANK, :], MUL, ADD))
            then(dve.scalar_tensor_tensor(small[:, POS, :], small[:, PASS_, :], float(SLOTS), small[:, RANK, :], MUL, ADD))
            dve.tensor_copy(pos_i[:, :], small[:, POS, :])
            for n in range(KC):
                c = n % TT
                dve.tensor_scalar(slot_hot[:, n, :], C("slot_iota"), small[:, RANK, n:n + 1], None, ALU.is_equal)
                of_pass, io = small[:, PASS_, n:n + 1], C("iota")[:, 0:PASSES]
                dve.tensor_scalar(pass_hot[:, n, 0, :], io, of_pass, None, ALU.is_equal)
                dve.tensor_scalar(pass_hot[:, n, 1, :], io, of_pass, C("token")[:, c:c + 1], ALU.is_equal, MUL)
                dve.tensor_scalar(pass_hot[:, n, 2, :], io, of_pass, small[:, GATE_, n:n + 1], ALU.is_equal, MUL).then_inc(s_hot, 1)
            dve.wait_ge(s_tabp, 1)
            tab = bank[:, 4, 0:3 * PASSES].rearrange("p (i q) -> p i q", i=3)
            dve.tensor_copy(gate_tab[:, :], tab[:, 2, :])
            then(dve.tensor_scalar(idx_f[:, :], tab[:, 0, :], 1.0, -4.0 * T, SUB, MUL))
            then(dve.scalar_tensor_tensor(idx_f[:, :], tab[:, 1, :], 2.0, idx_f[:, :], MUL, ADD))
            dve.tensor_scalar(idx_tab[:, :], idx_f[:, :], C("half"), None, ADD).then_inc(s_tab, 1)

            def one_pass(p, tokens_only=False):
                dve.wait_ge(s_hp, p + 1)
                dve.wait_ge(s_silu, p + 1)
                dve.tensor_tensor(h_e, h_silu, bank[:, 0, FE // 2:FE], MUL).then_inc(s_h, 1)
                turned(p + 1)
                dve.wait_ge(s_hTp, p + 1)
                dve.tensor_copy(hT, bank[:, 3, 0:FE // 2].rearrange("p (c s) -> p c s", c=2)).then_inc(s_hT, 1)

            def turned(p):
                dve.wait_ge(s_xeTp, p + 1)
                dve.tensor_copy(xeT, bank[:, 2, :].rearrange("p (c s) -> p c s", c=4)).then_inc(s_xeT, 1)

            turned(0)
            with dve.Fori(0, N_EXP) as i:
                one_pass(i)
            more = dve.value_load(more_i[0:1, 0:1], min_val=0, max_val=MORE)
            with dve.If(more > 0):
                with dve.Fori(0, more) as i:
                    one_pass(i + N_EXP)
            for c in range(TT):
                for k in range(TOPK):
                    dve.wait_ge(s_pair[TOPK * c + k], 16)
                dve.tensor_tensor(pair_y[:, 2 * c, :], pair_y[:, 2 * c, :], pair_y[:, 2 * c + 1, :], ADD).then_inc(s_sum, 1)
                dve.wait_ge(s_sum, c + 1)
                then(dve.scalar_tensor_tensor(x1[:, c, :], x1[:, c, :], ALPHA, pair_y[:, 2 * c, :], MUL, ADD))
                for i in range(2):
                    ins = dve.bn_stats(ln_stat[:, c, 6 * i:6 * i + 6], x1[:, c, T * i:T * i + T])
                then(ins)
                then(dve.bn_aggr(ln_mv[:, c, :], ln_stat[:, c, :]))
                dve.tensor_scalar(ln_rs[:, c:c + 1], ln_mv[:, c, 1:2], LN_EPS, None, ADD).then_inc(s_lnvar2, 1)
                dve.wait_ge(s_lnroot2, c + 1)
                then(dve.reciprocal(ln_rs[:, c:c + 1], ln_rs[:, c:c + 1]))
                then(dve.tensor_scalar(x1[:, c, :], x1[:, c, :], ln_mv[:, c, 0:1], ln_rs[:, c:c + 1], SUB, MUL))
                then(dve.tensor_tensor(x1[:, c, :], x1[:, c, :], ln_rows[:, 2, :], MUL))
                dve.tensor_tensor(x1[:, c, :], x1[:, c, :], ln_rows[:, 3, :], ADD).then_inc(s_x2, 1)

        @block.tensor
        def _(pe):
            st = {"phase": 0, "tile": 0}

            def open_phase():
                ph = st["phase"]
                st["phase"] += 1
                if ph >= 2:
                    pe.wait_ge(s_projfree, ph - 1)
                return ph % 2

            def tile_in():
                n = st["tile"]
                st["tile"] += 1
                pe.wait_ge(s_win[n % RING], 16 * (n // RING + 1))
                return n % RING

            def channels(w=P):
                slot, b = tile_in(), open_phase()
                for k in range(KT):
                    ins = pe.matmul(proj[0:w, b, :], ring[:, slot, k, 0:w], xT_sb[:, k, :], start=(k == 0), stop=(k == KT - 1))
                ins.then_inc(s_proj, 1)

            pe.wait_ge(s_x, 32)
            for _ in range(4):
                channels()
            slot = tile_in()
            tile_in()
            for c in range(TT):
                b = open_phase()
                for k in range(KT):
                    ins = pe.matmul(proj[:, b, 0:SGU], xT_sb[:, k, c * P:(c + 1) * P],
                                    ring[:, slot:slot + 2, k, :], start=(k == 0), stop=(k == KT - 1))
                ins.then_inc(s_proj, 1)
            for _ in range(2):
                channels()
            channels(LORA_W + LORA_A)
            channels(LORA_G)

            pe.wait_ge(s_vln, 1)
            pe.wait_ge(s_masked, 1)
            for g in range(4):
                for c in range(TT):
                    at = HD * (g % 2)
                    ins = pe.matmul(bank[at:at + HD, 2 + g // 2, c * P:(c + 1) * P], sgu_v[:, c, g * HD:(g + 1) * HD],
                                    sgu_w[:, g, :], start=True, stop=True)
            ins.then_inc(s_mix, 1)
            pe.wait_ge(s_const, 16)
            pe.wait_ge(s_convacc, 2 * TAPS)
            for i in range(2):
                ins = pe.matmul(bank[:, 0, :], C("ones"), conv_acc[:, i, :], start=(i == 0), stop=(i == 1))
            ins.then_inc(s_convsum, 1)
            pe.wait_ge(s_convsq, 2)
            for i in range(2):
                ins = pe.matmul(bank[:, 1, :], C("ones"), conv_sq[:, i, :], start=(i == 0), stop=(i == 1))
            ins.then_inc(s_convvar, 1)
            pe.wait_ge(s_early, 1)
            pe.wait_ge(s_convn, 2)

            gate = Gates()
            gate_at = {}

            def fill(n):
                for mm in gate.step(n):
                    k = mm % KT
                    if k == 0:
                        gate_at["slot"], gate_at["bank"] = tile_in(), open_phase()
                    ins = pe.matmul(proj[:, gate_at["bank"], :], ring[:, gate_at["slot"], k, :], xT_sb[:, k, :],
                                    start=(k == 0), stop=(k == KT - 1))
                    if k == KT - 1:
                        ins.then_inc(s_proj, 1)

            for hp in range(HP):
                ch = slice(P * hp, P * hp + P)
                if hp == 0:
                    pe.wait_ge(s_th, 2)
                    pe.wait_ge(s_par, 32)
                else:
                    pe.wait_ge(s_out, hp)
                pe.matmul(bank[:, 0, :], lora_sb[0:LORA_W, 0, ch], wl_al[0:LORA_W, :], start=True, stop=True)
                pe.matmul(bank[:, 1, :], lora_sb[LORA_W:LORA_W + LORA_A, 0, ch], wl_al[LORA_W:LORA_W + LORA_A, :],
                          start=True, stop=True).then_inc(s_z, 1)
                for _ in range(3):
                    channels()
                pe.wait_ge(s_sq, hp + 1)
                pe.matmul(bank[:, 2, :], C("head_ones"), sq, start=True, stop=True).then_inc(s_ss, 1)
                pe.wait_ge(s_pr, hp + 1)
                pe.matmul(bank[:, 3, :], C("head_ones"), kkn, start=True, stop=True).then_inc(s_bs, 1)
                fill(FILL["prep"])
                pe.wait_ge(s_ch, hp + 1)
                for b, src in ((2, ar[:, 0, :]), (5, v_), (3, bH), (4, kH)):
                    for j in range(TT):
                        ins = pe.transpose(bank[:, b, j * P:(j + 1) * P], src[:, j * P:(j + 1) * P], C("ident"))
                    ins.then_inc(s_tr, 1)
                fill(FILL["turned"])
                pe.wait_ge(s_tma, 3 * hp + 3)
                pe.wait_ge(s_tmd, 2 * hp + 2)
                quarters = [(h, c) for h in range(2) for c in range(2)]
                for j in range(TT):
                    for banks, lhs in (((0, 1), bT), ((2, 5), kT)):
                        for h, c in quarters:
                            t = slice(j * P + HD * c, j * P + HD * c + HD)
                            pe.matmul(bank[HD * c:HD * c + HD, banks[h], j * P:(j + 1) * P], lhs[KS[h], t],
                                      ar[KS[h], 0:2 + h:1 + h, t], start=True, stop=True)
                    for h, c in quarters:
                        t = slice(j * P + HD * c, j * P + HD * c + HD)
                        ins = pe.matmul(bank[HD * c:HD * c + HD, 3 + h, j * P:j * P + HD], ar[KS[h], 0, t], bT[KS[h], t], start=True, stop=True)
                ins.then_inc(s_sc, 1)
                fill(FILL["scores"])

                def stage(acts, dves, products, more=0):
                    for g in range(2):
                        if acts:
                            pe.wait_ge(s_da, 8 * hp + 2 * (acts - 1) + g + 1)
                        if dves:
                            pe.wait_ge(s_dd, 18 * hp + 2 * (dves - 1) + g + 1)
                        for b, lhsT, rhs in products(g):
                            for j in range(TT):
                                ins = pe.matmul(bank[:, 3 * g + b, j * P:j * P + P], lhsT[:, j, :], rhs[:, j, :], start=True, stop=True)
                        ins.then_inc(s_dm, 1)
                    fill(more)

                more = FILL["solve"]
                pe.wait_ge(s_scev, 3 * hp + 1)
                stage(0, 0, lambda g: [(0, L16T[:, g], L16[:, g]), (1, L16[:, g], L16T[:, g])])
                pe.wait_ge(s_scev, 3 * hp + 3)
                stage(1, 1, lambda g: [(0, ET[:, g], E[:, g]), (1, E[:, g], ET[:, g]), (2, E[:, g], ZT[:, g])])
                for g in range(2):
                    pe.wait_ge(s_da, 8 * hp + 2 + g + 1)
                    pe.wait_ge(s_dd, 18 * hp + 2 + g + 1)
                    for j in range(TT):
                        for c in range(2):
                            t = slice(HD * c, HD * c + HD)
                            pe.matmul(bank[t, 3 * g + 1, j * HD:j * HD + HD], AK[t, g, j, :], V[t, g, j, :], start=True, stop=True)
                    for b, lhsT, rhs in ((0, L16T, L16), (2, L16, ZT)):
                        for j in range(TT):
                            ins = pe.matmul(bank[:, 3 * g + b, j * P:j * P + P], lhsT[:, g, j, :], rhs[:, g, j, :], start=True, stop=True)
                    ins.then_inc(s_dm, 1)
                fill(more)
                stage(3, 3, lambda g: [(2, E[:, g], ZT[:, g])], more)
                stage(0, 4, lambda g: [(0, ZT[:, g], X0[:, g]), (2, LX[:, g], ZT[:, g])], more)
                stage(4, 5, lambda g: [(1, ET[:, g], Y0[:, g])], more)
                stage(0, 6, lambda g: [(0, ET[:, g], Y1[:, g])], more)
                stage(0, 7, lambda g: [(1, ET[:, g], Y2[:, g])], more)
                for g in range(2):
                    pe.wait_ge(s_dd, 18 * hp + 14 + g + 1)
                    for j in range(TT):
                        at, t = slice(j * P, (j + 1) * P), [slice(HD * c, HD * c + HD) for c in range(2)]
                        for part in (KS[g], VS[g]):
                            for c in range(2):
                                pe.matmul(bank[part, 3 * g + 1 + c, at], Y1[t[c], g, j, part], BR[t[c], g, j, :], start=True, stop=part == KS[g])
                        for c in range(2):
                            ins = pe.matmul(bank[VS[g], 3 * g + 1 + c, at], V[t[c], g, j, :], KR[t[c], g, j, :], start=False, stop=True)
                    ins.then_inc(s_dm, 1)
                pe.wait_ge(s_init, 4 * hp + 4)
                for c in range(CHUNKS - 1):
                    for h in range(2):
                        if c == 0:
                            pe.wait_ge(s_dd, 18 * hp + 17 + h)
                        else:
                            pe.wait_ge(s_ce, 2 * (CHUNKS - 1) * hp + 2 * c - 1 + h)
                        pe.matmul(bank[KS[h], 0, HD * (c % 2):HD * (c % 2) + HD], gh[:, h, c // 2, HD * (c % 2):HD * (c % 2) + HD],
                                  state[:, c, h, :], start=True, stop=True).then_inc(s_cm, 1)
                    fill(FILL["chain"])
                pe.wait_ge(s_ce, 2 * (CHUNKS - 1) * (hp + 1))
                pe.wait_ge(s_out2, 2 * hp + 2)
                for c in range(CHUNKS):
                    for h in range(2):
                        ins = pe.matmul(bank[HD * h:HD * h + HD, 3, HD * c:HD * c + HD], state[:, c, h, :],
                                        out2[:, h, c // 2, HD * (c % 2):HD * (c % 2) + HD], start=True, stop=True)
                ins.then_inc(s_ymm, 1)
                fill(FILL["y"])
                pe.wait_ge(s_y, hp + 1)
                pe.matmul(bank[:, 5, :], lora_sb[0:LORA_G, 1, ch], gl[0:LORA_G, :], start=True, stop=True)
                pe.matmul(bank[:, 4, :], C("head_ones"), y_, start=True, stop=True).then_inc(s_mu, 1)
                fill(FILL["mean"])
                pe.wait_ge(s_yc, hp + 1)
                pe.matmul(bank[:, 1, :], C("head_ones"), ysq, start=True, stop=True).then_inc(s_var, 1)
                fill(FILL["var"])

            pe.wait_ge(s_out, HP)
            pe.wait_ge(s_wo, 16)
            for m in range(KT):
                if m >= 2:
                    pe.wait_ge(s_m3, m - 1)
                parts = [(0, rwkv_out, 0, 4), (1, sgu_out, 4, 2), (2, conv_out, 6, 2)]
                for n, src, k0, nk in parts:
                    for k in range(nk):
                        ins = pe.matmul(bank[:, 3 * (m % 2) + n, :], wo_sb[:, k0 + k, m * P:(m + 1) * P], src[:, k, :],
                                        start=(k == 0), stop=(k == nk - 1))
                ins.then_inc(s_mm3, 1)
            def mix(c):
                for i in range(2):
                    n = 2 * c + i
                    if n >= 2:
                        pe.wait_ge(s_pre, n - 1)
                    for k in range(KT):
                        if n == 0:
                            pe.wait_ge(s_merged, k + 1)
                        ins = pe.matmul(proj[:, n % 2, :], merged[:, k, c * P:(c + 1) * P], wout_sb[:, k, T * i:T * i + T],
                                        start=(k == 0), stop=(k == KT - 1))
                    ins.then_inc(s_mx, 1)

            def turn_x1(c):
                pe.wait_ge(s_x1, c + 1)
                if c >= 2:
                    pe.wait_ge(s_x1T, c - 1)
                for k in range(KT):
                    ins = pe.transpose(bank[:, 2 * (c % 2) + k // 4, P * (k % 4):P * (k % 4) + P], x1[:, c, k * P:(k + 1) * P], C("ident"))
                ins.then_inc(s_x1Tp, 1)

            def router(c):
                pe.wait_ge(s_x1T, c + 1)
                for k in range(KT):
                    ins = pe.matmul(bank[:, 4, c * N_EXP:(c + 1) * N_EXP], x1T[:, c % 2, k, :], rw_sb[:, k, :],
                                    start=(k == 0), stop=(k == KT - 1))
                if c == TT - 1:
                    ins.then_inc(s_scp, 1)

            pe.wait_ge(s_wout, 16)
            pe.wait_ge(s_projfree, st["phase"])
            mix(0)
            pe.wait_ge(s_m3, KT)
            pe.wait_ge(s_rw, 32)
            for c in range(TT):
                if c + 1 < TT:
                    mix(c + 1)
                turn_x1(c)
                if c:
                    router(c - 1)
            router(TT - 1)
            pe.wait_ge(s_chosen, 1)
            for c in range(TT):
                for n in range(c + 1):
                    pe.matmul(bank[:, 5, c * N_EXP:(c + 1) * N_EXP], C("earlier") if n == c else C("ones"), chosen[:, n, :],
                              start=(n == 0), stop=(n == c))
            for n in range(TT):
                ins = pe.matmul(bank[:, 5, TT * N_EXP:(TT + 1) * N_EXP], C("ones"), chosen[:, n, :], start=(n == 0), stop=(n == TT - 1))
            ins.then_inc(s_rank, 1)
            for n in range(TOPK * TT):
                pe.wait_ge(s_hot, n + 1)
                if n == 0:
                    pe.wait_ge(s_score, 1)
                ins = pe.matmul(bank[:, 4, 0:3 * PASSES], slot_hot[:, n, :], pass_hot[:, n, :, :], start=(n == 0), stop=(n == TOPK * TT - 1))
            ins.then_inc(s_tabp, 1)
            pe.wait_ge(s_tab, 3)

            def turn(p):
                pe.wait_ge(s_xe, p * 16 + 16)
                pe.wait_ge(s_xeT, p)
                for c in range(4):
                    ins = pe.transpose(bank[:, 2, c * P:(c + 1) * P], xe[:, c * P:(c + 1) * P], C("ident"))
                ins.then_inc(s_xeTp, 1)

            def one_pass(p, b, loads):
                pe.wait_ge(s_xeT, p + 1)
                gu = w_set[b][:, 0:GU].rearrange("p (k h i n) -> p k h i n", k=KT, h=2, i=2)
                for k in range(KT):
                    if k % 2 == 0:
                        pe.wait_ge(s_w[b][k // 2], loads)
                    for h in range(2):
                        ins = pe.matmul(bank[SLOTS * h:SLOTS * h + SLOTS, 0, :], xeT[:, k % 4, SLOTS * (k // 4):SLOTS * (k // 4) + SLOTS],
                                        gu[:, k, h, :, :], start=(k == 0), stop=(k == KT - 1))
                    if k == KT - 1:
                        ins.then_inc(s_hp, 1)
                    elif k % 2 == 1:
                        ins.then_inc(s_used, 1)
                turn(p + 1)
                pe.wait_ge(s_h, p + 1)
                for c in range(2):
                    ins = pe.transpose(bank[:, 3, c * P:(c + 1) * P], h_e[:, c * P:(c + 1) * P], C("ident"))
                ins.then_inc(s_hTp, 1)
                pe.sem_inc(s_used, 1)
                pe.wait_ge(s_hT, p + 1)
                pe.wait_ge(s_yfree, p + 1)
                wd = w_set[b][:, GU:].rearrange("p (f h n) -> p f h n", f=4, h=2)
                for f in range(4):
                    if f % 2 == 0:
                        pe.wait_ge(s_w[b][4 + f // 2], loads)
                    for h in range(2):
                        ins = pe.matmul(bank[SLOTS * h:SLOTS * h + SLOTS, 1, :], hT[:, f % 2, SLOTS * (f // 2):SLOTS * (f // 2) + SLOTS],
                                        wd[:, f, h, :], start=(f == 0), stop=(f == 3))
                    if f == 1:
                        ins.then_inc(s_used, 1)
                ins.then_inc(s_yp, 1)
                pe.wait_ge(s_yp, p + 1)
                pe.sem_inc(s_used, 1)

            turn(0)
            with pe.Fori(0, N_EXP // 2) as i:
                for b in range(2):
                    one_pass(i * 2 + b, b, i * 16 + 16)
            more = pe.value_load(more_i[0:1, 0:1], min_val=0, max_val=MORE)
            with pe.If(more > 0):
                with pe.Fori(0, more) as i:
                    one_pass(i + N_EXP, 0, i * 16 + 16 * (N_EXP // 2 + 1))


def tiles_of(v):
    return v.reshape(-1, P).T


def kernel(**inputs):
    import concourse.bacc as bacc
    from concourse.bass_utils import run_bass_kernel_spmd

    a = {k: np.asarray(v) for k, v in inputs.items()}
    mu = a["rwkv_mu"][0]
    cols = [tiles_of(mu[0:3 * RW])]
    for at, n in ((OFF_WL, LORA_W + LORA_A), (OFF_GL, LORA_G)):
        col = np.zeros((P, 1), np.float32)
        col[:n, 0] = mu[at:at + n]
        cols.append(col)
    for name in ("rwkv_w0", "rwkv_a0", "rwkv_k_k", "rwkv_k_a", "rwkv_r_k", "rwkv_gn_g", "rwkv_gn_b", "conv_db", "conv_ln_g", "conv_ln_b"):
        cols.append(tiles_of(a[name][0].reshape(-1)))
    dw = a["conv_dw"][0]
    cols += [dw[:, P * i:P * i + P].T for i in range(2)]
    lora = np.zeros((P, 2, RW), np.float32)
    lora[0:LORA_W, 0] = a["rwkv_w_up"][0]
    lora[LORA_W:LORA_W + LORA_A, 0] = a["rwkv_a_up"][0]
    lora[0:LORA_G, 1] = a["rwkv_g_up"][0]
    arrays = {
        "x_tok": a["x"][0],
        "xT": a["x"][0].T.reshape(KT, P, T).transpose(1, 0, 2),
        "w_in": a["w_in_first"],
        "par": np.concatenate(cols, 1),
        "table": TABLE,
        "lora": lora,
        "rows": np.concatenate([a[n].reshape(-1) for n in ("sgu_ln_g", "sgu_ln_b", "ln1_g", "ln1_b", "ln2_g", "ln2_b", "router_b")])[None],
        "sgu_b": a["sgu_b"][0],
        "sgu_wT": a["sgu_w"][0].transpose(2, 0, 1),
        "w_o": np.concatenate([a["rwkv_w_o"][0], a["sgu_w_o"][0], a["conv_w_o"][0]], 0),
        "w_out": a["w_out"][0],
        "router_w": a["router_w"],
        "zeros": np.zeros((SLOTS, D), np.float32),
        "w_gu": np.stack([a[n][0].reshape(N_EXP, KT, P, 2, FE // 2) for n in ("moe_w_gate", "moe_w_up")], 4)
                  .transpose(0, 2, 1, 3, 4, 5).reshape(N_EXP, P, GU),
        "w_down": a["moe_w_down"][0].reshape(N_EXP, FE // P, P, D).transpose(0, 2, 1, 3).reshape(N_EXP, P, WD),
    }
    nc = bacc.Bacc("TRN2", target_bir_lowering=False, num_devices=1)
    aps = []
    for name, v in arrays.items():
        arrays[name] = v = np.ascontiguousarray(v)
        aps.append(nc.dram_tensor(name, v.shape, mybir.dt.from_np(v.dtype), kind="ExternalInput").ap())
    out = nc.dram_tensor("out", (T, D), F32, kind="ExternalOutput").ap()
    program(nc, *aps, out)
    r = run_bass_kernel_spmd(nc, [arrays], core_ids=[0])
    return r.results[0]["out"].reshape(1, T, D)
```

```python
from contextlib import ExitStack

import numpy as np

import concourse.bass as bass
from concourse import mybir

F32 = mybir.dt.float32
I32 = mybir.dt.int32
U32 = mybir.dt.uint32
ALU = mybir.AluOpType
ACT = mybir.ActivationFunctionType
AX_X = mybir.AxisListType.X
ADD, SUB, MUL, MAX = ALU.add, ALU.subtract, ALU.mult, ALU.max

P = 128
T, D = 512, 1024
KT = D // P
TT = T // P
HD = 64
RW = 512
HP = RW // P
LORA_W, LORA_A, LORA_G = 32, 32, 96
SGU = 256
CONV, TAPS = 256, 31
OFF_WL = 3 * RW
OFF_GL = OFF_WL + LORA_W + LORA_A
OFF_SGU = OFF_GL + LORA_G
OFF_CONV = OFF_SGU + 2 * SGU
OFF_GATE = OFF_CONV + 2 * CONV
ALPHA = 2 ** 0.25
LN_EPS, GN_EPS = 1e-5, 64e-5
DECAY_SCALE = float(np.exp(-0.5))

N_EXP, GROUPS, TOPK, FE = 32, 4, 2, 512
PER_GROUP = N_EXP // GROUPS
SLOTS = 64
MORE = T * TOPK // SLOTS - 1
PASSES = N_EXP + MORE + 1
GU = KT * 2 * FE
WD = FE // P * D
CHUNK = 2 * 2 * FE
NCH = (GU + WD) // CHUNK
BIG = 1e30

MU, W0, A0, KK_, KA_, RK_, GNG, GNB, CDB, CLG, CLB, CDW = 0, 14, 18, 22, 26, 30, 34, 38, 42, 44, 46, 48
N_PAR = CDW + 2 * TAPS

CONSTS = {}


def constant_table():
    i, j = np.arange(P)[:, None], np.arange(P)[None, :]
    same64, same16 = i // 64 == j // 64, i // 16 == j // 16
    ic, jc = i % HD, np.arange(HD)[None, :]
    blocks = {
        "ident": i == j,
        "within16": same16 & (j < i),
        "within16T": same16 & (i < j),
        "across16": same64 & ~same16 & (j < i),
        "beforeT": ic < jc,
        "uptoT": ic <= jc,
        "head_ones": same64,
        "ident_twice": (i % 64) == np.arange(64)[None, :],
        "ones": np.ones((P, P), bool),
        "earlier": i < j,
        "slot_iota": j % SLOTS + 0 * i,
        "iota": np.arange(64)[None, :] + np.zeros((P, 1)),
        "expert_left": N_EXP - np.arange(N_EXP)[None, :] + np.zeros((P, 1)),
        "group_left": GROUPS - np.arange(GROUPS)[None, :] + np.zeros((P, 1)),
        "token": np.arange(P)[:, None] + P * (np.arange(TOPK * TT) % TT)[None, :],
        "multiples": SLOTS * np.arange(1, T // SLOTS)[None, :] + np.zeros((P, 1)),
        "half": np.arange(P)[:, None] // SLOTS,
    }
    at, parts = 0, []
    for name, b in blocks.items():
        CONSTS[name] = (at, b.shape[1])
        at += b.shape[1]
        parts.append(b.astype(np.float32))
    return np.ascontiguousarray(np.concatenate(parts, 1))


TABLE = constant_table()

FILL = {"prep": 13, "turned": 2, "scores": 5, "solve": 1, "chain": 1, "y": 1, "mean": 2, "var": 0}
EARLY_FILL = {"v_norm": 8, "conv_sum": 8, "conv_sq": 4, "conv_norm": 12}
CHUNKS = T // HD
GATE_TILES, EARLY = 3 * D // P, 4
PAIR_GATES = (GATE_TILES - EARLY) // HP
FILL["var"] = PAIR_GATES * KT - sum(v * {"chain": CHUNKS - 1, "solve": 7}.get(k, 1) for k, v in FILL.items())
assert FILL["var"] >= 0 and sum(EARLY_FILL.values()) == EARLY * KT and (GATE_TILES - EARLY) % HP == 0


def column_tiles():
    tiles = [(OFF_CONV + P * i, P) for i in range(4)]
    tiles += [(OFF_SGU + SGU + P * i, P) for i in range(2)]
    tiles += [(OFF_SGU + P * i, P) for i in range(2)]
    tiles += [(OFF_WL, LORA_W + LORA_A), (OFF_GL, LORA_G)]
    tiles += [(OFF_GATE + P * g, P) for g in range(EARLY)]
    g = EARLY
    for hp in range(HP):
        tiles += [(RW * n + P * hp, P) for n in range(3)]
        tiles += [(OFF_GATE + P * (g + i), P) for i in range(PAIR_GATES)]
        g += PAIR_GATES
    return tiles


TILES = column_tiles()
RING = 4
V_TILES = (4, 5)


def phase_after(tile):
    if tile < 4:
        return tile + 1
    if tile < 6:
        return 8
    return tile + 3



class Gates:

    def __init__(self):
        self.done = 0

    def step(self, n):
        first = self.done
        self.done += n
        return range(first, self.done)


def phase_of_gate(g):
    if g < EARLY:
        return 12 + g
    pair, n = divmod(g - EARLY, PAIR_GATES)
    return 12 + EARLY + (3 + PAIR_GATES) * pair + 3 + n


def program(nc, x_tok, xT, w_in, par, table, lora, rows, sgu_b, sgu_wT, w_o, w_out, router_w, zeros, w_gu, w_down, out):
    with ExitStack() as ctx:
        def sb(name, shape, dt=F32):
            return ctx.enter_context(nc.sbuf_tensor(name, shape, dt))

        def sem(name):
            return ctx.enter_context(nc.semaphore(name))

        const = sb("const", [P, TABLE.shape[1]])
        par_sb = sb("par_sb", [P, N_PAR + 8])
        lora_sb = sb("lora_sb", [P, 2, RW])
        xT_sb = sb("xT_sb", [P, KT, T])
        ring = sb("ring", [P, RING, KT, P])
        gates = sb("gates", [P, GATE_TILES, T])
        branches = sb("branches", [P, HP + 4, T])
        rwkv_out, sgu_out, conv_out = branches[:, 0:HP, :], branches[:, HP:HP + 2, :], branches[:, HP + 2:, :]
        raw = sb("raw", [P, 2, T + 1])
        wl_al = sb("wl_al", [P, T])
        gl = sb("gl", [P, T])
        ARENA = 23700
        arena = sb("arena", [P, ARENA])
        proj = ctx.enter_context(nc.psum_tensor("proj", [P, 2, T], F32))
        bank = ctx.enter_context(nc.psum_tensor("bank", [P, 6, T], F32))

        def C(name):
            at, n = CONSTS[name]
            return const[:, at:at + n]

        def par_col(c):
            return par_sb[:, c:c + 1]

        CLG_S, GNG_S, EPS_CONV, EPS_GN = N_PAR, N_PAR + 2, N_PAR + 6, N_PAR + 7

        class Cut:
            def __init__(self, base):
                self.at = base

            def __call__(self, n, **split):
                v = arena[:, self.at:self.at + n]
                self.at += n
                assert self.at <= ARENA, self.at
                return v.rearrange(split["r"], **split["k"]) if split else v

        cut = Cut(0)
        conv_val = cut(2 * T, r="p (i t) -> p i t", k=dict(i=2))
        conv_gate = cut(2 * T, r="p (i t) -> p i t", k=dict(i=2))
        PADDED = T + TAPS - 1
        conv_in = cut(2 * PADDED, r="p (i t) -> p i t", k=dict(i=2))
        conv_acc = cut(2 * T, r="p (i t) -> p i t", k=dict(i=2))
        conv_sq = cut(2 * T, r="p (i t) -> p i t", k=dict(i=2))
        conv_rs = cut(T)
        sgu_u = cut(2 * T, r="p (i t) -> p i t", k=dict(i=2))
        sgu_v = cut(TT * SGU, r="p (c d) -> p c d", k=dict(c=TT))
        sgu_w = cut(4 * P, r="p (g q) -> p g q", k=dict(g=4))
        sgu_ln = cut(2 * SGU, r="p (i d) -> p i d", k=dict(i=2))
        sgu_bias = cut(2 * P, r="p (i q) -> p i q", k=dict(i=2))
        sgu_mix = cut(2 * T, r="p (i t) -> p i t", k=dict(i=2))
        sgu_stat = cut(TT * 6, r="p (c s) -> p c s", k=dict(c=TT))
        sgu_mv = cut(TT * 2, r="p (c s) -> p c s", k=dict(c=TT))
        sgu_rs = cut(TT)

        cut = Cut(0)
        r_, k_ = cut(T), cut(T)
        iclr, decay = cut(T), cut(T)
        kk, sq = cut(T), cut(T)
        v_, cum, kh, inv, norm, kkn = (cut(T) for _ in range(6))
        bT, kT, bH, kH, bonus = (cut(T) for _ in range(5))
        ar = cut(3 * T, r="p (n t) -> p n t", k=dict(n=3))
        diag = [cut(T) for _ in range(2)]
        carry = cut(T)
        KS, VS = (slice(0, HD), slice(HD, P)), (slice(HD, P), slice(0, HD))

        def per_chunk(n):
            return cut(8 * n, r="p (h j n) -> p h j n", k=dict(h=2, j=TT))

        X0, Y0, Y1, Y2 = (per_chunk(P) for _ in range(4))
        V, AK = (per_chunk(HD) for _ in range(2))
        BR, KR = (per_chunk(P) for _ in range(2))
        L16, L16T, LX, ZT = (per_chunk(P) for _ in range(4))
        E, ET = (arena[:, at:at + 2 * T].rearrange("p (h j n) -> p h j n", h=2, j=TT) for at in (8 * T, 10 * T))
        out2 = arena[:, 0:2 * T].rearrange("p (h j n) -> p h j n", h=2, j=TT)
        gh = arena[:, 2 * T:4 * T].rearrange("p (h j n) -> p h j n", h=2, j=TT)
        state = arena[:, 4 * T:6 * T].rearrange("p (c h n) -> p c h n", c=CHUNKS, h=2)
        y_, yc, ysq, yrs, yn = bT, kT, bH, kH, cum

        cut = Cut(0)
        wout_sb = cut(KT * D, r="p (k n) -> p k n", k=dict(k=KT))
        merged = cut(KT * T, r="p (k t) -> p k t", k=dict(k=KT))
        wo_sb = cut(8 * D, r="p (k n) -> p k n", k=dict(k=8))
        mtmp = cut(3 * T, r="p (i t) -> p i t", k=dict(i=3))
        ln_stat = cut(TT * 12, r="p (c s) -> p c s", k=dict(c=TT))
        ln_mv = cut(TT * 2, r="p (c s) -> p c s", k=dict(c=TT))
        ln_rs = cut(TT)
        x1 = ring[:, :, :, :].rearrange("p s k c -> p s (k c)")
        ln_rows = xT_sb[:, :, :].rearrange("p k t -> p (k t)").rearrange("p (i d) -> p i d", i=4)

        small_end = cut.at
        SETS = 3
        flat = [gates[:, :, :].rearrange("p g t -> p (g t)"), arena[:, 0:GU + WD]]
        w_chunk = [[v[:, c * CHUNK:(c + 1) * CHUNK] for c in range(NCH)] for v in flat]
        flat = [ring[:, :, :, :].rearrange("p s k c -> p (s k c)"), xT_sb[:, :, :].rearrange("p k t -> p (k t)"),
                branches[:, :, :].rearrange("p k t -> p (k t)")]
        w_chunk.append([v[:, c * CHUNK:(c + 1) * CHUNK] for v in flat for c in range(2)])
        assert KT * D + KT * T == GU + WD == GATE_TILES * T
        cut = Cut(KT * D + KT * T)
        x1T = cut(2 * KT * P, r="p (b k t) -> p b k t", k=dict(b=2, k=KT))
        slot_hot = cut(8 * P, r="p (n s) -> p n s", k=dict(n=8))
        pass_hot = cut(8 * 3 * PASSES, r="p (n i q) -> p n i q", k=dict(n=8, i=3))
        xe = cut(T)
        xeT = cut(T, r="p (c s) -> p c s", k=dict(c=4))
        h_silu, h_e = cut(FE // 2), cut(FE // 2)
        hT = cut(FE // 2, r="p (c s) -> p c s", k=dict(c=2))
        y_e = cut(T)
        assert cut.at <= KT * D + KT * T + 8 * D
        cut = Cut(small_end)
        rt = [cut(2 * TT * N_EXP) for _ in range(4)]
        assert cut.at <= ARENA
        pair_y = arena[:, 0:8 * D].rearrange("p (n d) -> p n d", n=8)
        lora_flat, raw_flat = lora_sb[:, :, :].rearrange("p i n -> p (i n)"), raw[:, :, :].rearrange("p i n -> p (i n)")
        place = {"lora": 0, "raw": 0}

        def late(where, flat, n):
            at = place[where]
            place[where] += n
            return flat[:, at:at + n]

        rw_sb = late("lora", lora_flat, KT * N_EXP).rearrange("p (k e) -> p k e", k=KT)
        rb_sb = late("lora", lora_flat, N_EXP)
        scores = late("lora", lora_flat, TT * N_EXP).rearrange("p (c e) -> p c e", c=TT)
        sel = late("lora", lora_flat, TT * N_EXP).rearrange("p (c e) -> p c e", c=TT)
        top8 = late("lora", lora_flat, TT * GROUPS * 8).rearrange("p (n e) -> p n e", e=8)
        grp = late("lora", lora_flat, 3 * TT * GROUPS).rearrange("p (i n) -> p i n", i=3)
        hot = late("lora", lora_flat, TOPK * TT * N_EXP).rearrange("p (k c e) -> p k c e", k=TOPK, c=TT)
        assert place["lora"] <= 2 * RW
        chosen = late("raw", raw_flat, (TT + 1) * N_EXP).rearrange("p (c e) -> p c e", c=TT + 1)
        small = late("raw", raw_flat, 12 * TOPK * TT).rearrange("p (i n) -> p i n", i=12)
        count = late("raw", raw_flat, 6 * N_EXP).rearrange("p (i n) -> p i n", i=6)
        gate_tab, idx_f = (late("raw", raw_flat, n) for n in (PASSES, PASSES))
        idx_tab, idx_now, pos_i, more_i, extra_i, first_i = (late("raw", raw_flat, n).bitcast(I32) for n in (PASSES, 1, TOPK * TT, 1, N_EXP, N_EXP))
        warm = late("raw", raw_flat, 2)
        assert place["raw"] <= 2 * (T + 1)
        x1_dram = nc.dram_tensor("x1_rows", (T * 2, D // 2), F32).ap()
        y_dram = nc.dram_tensor("y_rows", (PASSES * SLOTS, D), F32).ap()

        s_x = [sem(f"xT_in{n}") for n in range(KT // 2)]
        s_const, s_par, s_small, s_lnrows, s_sgub = map(sem, ["const_in", "par_in", "sgu_par_in", "ln_rows_in", "sgu_bias_in"])
        s_win = [sem(f"ring_in{i}") for i in range(RING)]
        s_proj = sem("proj_done")
        s_projfree = sem("proj_read")
        s_rawfree = sem("raw_read")
        s_dve = sem("dve_seq")
        s_pool = sem("pool_seq")
        s_masked = sem("sgu_w_masked")
        s_convin, s_pads = sem("conv_in_ready"), sem("pads_zeroed")
        s_scaled = sem("gains_scaled")
        s_convacc, s_convsum, s_convsq, s_convvar, s_convn = map(sem, ["conv_acc", "conv_sum", "conv_sq", "conv_var", "conv_norm"])
        s_convout = sem("conv_out_ready")
        s_vln, s_mix = map(sem, ["v_normed", "mixed_in_psum"])
        s_early = sem("early_done")
        s_vstat, s_vroot, s_convroot = map(sem, ["v_variance", "v_deviation", "conv_deviation"])
        s_norm, s_yroot, s_lnvar, s_lnroot = map(sem, ["kk_norm", "y_deviation", "ln_variance", "ln_deviation"])
        s_lora_in = sem("lora_in")
        s_lora, s_th = sem("lora_shifted"), sem("lora_activated")
        s_z, s_iclr, s_decay = map(sem, ["z_in_psum", "iclr_ready", "decay_ready"])
        s_sq, s_ss, s_pr, s_bs, s_ch = map(sem, ["kk_squared", "kk_norm_psum", "rk_product", "bonus_psum", "channels_ready"])
        s_tr, s_tma, s_tmd = map(sem, ["turned", "turned_out_act", "turned_out_dve"])
        s_sc, s_scev = sem("scores_psum"), sem("scores_out")
        s_dm, s_da, s_dd = sem("solve_psum"), sem("solve_out_act"), sem("solve_out_dve")
        s_init, s_diag, s_out2 = sem("state_init"), sem("chunk_products_ready"), sem("output_maps_ready")
        s_zero, s_cumlog, s_cum = sem("zeros_set"), sem("decay_logs_summed"), sem("decay_products_ready")
        s_cm, s_ce = sem("chain_psum"), sem("chain_out")
        s_ymm, s_y, s_mu, s_yc, s_var, s_out = map(sem, ["y_psum", "y_out", "y_mean", "y_centred", "y_var", "pair_done"])
        s_wo = [sem(f"w_o_in{n}") for n in range(2)]
        s_wout, s_xtok = map(sem, ["w_out_in", "x_tok_in"])
        s_mm3, s_m3, s_merged = map(sem, ["branches_psum", "products_ready", "merged_ready"])
        s_mx, s_pre = sem("mixed_psum"), sem("residual_added")
        s_x1, s_st = sem("x1_ready"), sem("stored")
        s_yfree = sem("ye_bank_free")
        s_begun, s_ypad, s_more = map(sem, ["gathers_begun", "y_rows_zeroed", "further_passes_ready"])
        s_first, s_x1back, s_lnback = map(sem, ["first_passes_ready", "x1_back", "ln2_rows_in"])
        assert (N_EXP - 3) % SETS == SETS - 1
        s_x1st, s_rw = sem("x1_stored"), sem("router_par_in")
        s_x1Tp, s_x1T, s_scp, s_score = map(sem, ["x1T_psum", "x1T_out", "scores_in_psum", "scores_ready"])
        s_chosen, s_rank, s_hot, s_tabp, s_tab = map(sem, ["chosen_ready", "rank_psum", "one_hots_ready", "table_psum", "tables_ready"])
        s_w = [[sem(f"w_in{b}_{c}") for c in range(NCH)] for b in range(3)]
        s_used = sem("w_used")
        s_idx, s_xe, s_xe0 = sem("index_ready"), sem("tokens_in"), sem("tokens_zeroed")
        s_xeTp, s_xeT, s_hp, s_silu, s_h, s_hTp, s_hT, s_yp, s_ye, s_yst = map(
            sem, ["xeT_psum", "xeT_out", "h_psum", "silu_ready", "h_ready", "hT_psum", "hT_out", "ye_psum", "ye_ready", "ye_stored"])
        s_pair, s_x2 = [sem(f"pair_in{n}") for n in range(TOPK * TT)], [sem(f"x2_ready{c}") for c in range(TT)]
        s_norm2, s_gain2, s_scale2 = sem("ln2_normed"), sem("ln2_gained"), sem("ln2_scale")
        s_lnvar2, s_lnroot2 = sem("ln2_variance"), sem("ln2_deviation")

        block = ctx.enter_context(nc.Block())

        @block.sync
        def _(sp):
            wv = w_in.rearrange("(k p) c -> p k c", p=P)
            for k in range(0, KT, 2):
                sp.dma_start(xT_sb[:, k:k + 2, :], xT[:, k:k + 2, :]).then_inc(s_x[k // 2], 16)
                for n in range(2):
                    sp.dma_start(ring[:, n, k:k + 2, :], wv[:, k:k + 2, TILES[n][0]:TILES[n][0] + P]).then_inc(s_x[k // 2], 16)
            for n, (c0, w) in enumerate(TILES):
                if n < 2:
                    continue
                if n >= RING:
                    sp.wait_ge(s_proj, phase_after(n - RING))
                sp.dma_start(ring[:, n % RING, :, 0:w], wv[:, :, c0:c0 + w]).then_inc(s_win[n % RING], 16)
                if n == RING - 1:
                    sp.dma_start(const[:, :], table).then_inc(s_const, 16)
                    sp.dma_start(lora_sb[:, :, :], lora).then_inc(s_lora_in, 16)
            for q in range(N_EXP, PASSES):
                sp.dma_start(y_dram[q * SLOTS:(q + 1) * SLOTS, :], zeros).then_inc(s_ypad, 16)
            sp.wait_ge(s_dm, 20 * HP)
            for i in range(2):
                sp.dma_start(wo_sb[:, :, T * i:T * i + T], w_o.rearrange("(k p) n -> p k n", p=P)[:, :, T * i:T * i + T]).then_inc(s_wo[i], 16)
            sp.wait_ge(s_out, HP)
            sp.dma_start(rw_sb[:, :, :], router_w.rearrange("(k p) e -> p k e", p=P)).then_inc(s_rw, 16)
            sp.dma_start(rb_sb[:, :], rows[:, 2 * SGU + 4 * D:].partition_broadcast(P).rearrange("p a e -> p (a e)")).then_inc(s_rw, 16)
            sp.dma_start(wout_sb, w_out.rearrange("(k p) n -> p k n", p=P)).then_inc(s_wout, 16)
            sp.wait_ge(s_proj, phase_after(len(TILES) - 1))
            sp.dma_start(x1, x_tok.rearrange("(c p) d -> p c d", p=P)).then_inc(s_xtok, 16)
            sp.dma_start(ln_rows, rows[:, 2 * SGU:2 * SGU + 4 * D].partition_broadcast(P).rearrange("p a (i d) -> p (a i) d", i=4)).then_inc(s_lnrows, 16)
            def chunk_src(e, c):
                n = c * CHUNK
                return w_gu[e, :, n:n + CHUNK] if n < GU else w_down[e, :, n - GU:n - GU + CHUNK]

            def load(b, c, e):
                sp.dma_start(w_chunk[b][c], chunk_src(e, c)).then_inc(s_w[b][c], 16)

            for m in (TT, KT):
                sp.wait_ge(s_m3, m)
                for c in range(m // TT - 1, NCH, 2):
                    load(0, c, 0)
            sp.wait_ge(s_mm3, KT)
            for c in (4, 5):
                load(2, c, 2)

            def store_x1(c):
                sp.wait_ge(s_x1, c + 1)
                sp.dma_start(x1_dram.rearrange("(t h) d -> t (h d)", h=2)[c * P:(c + 1) * P, :], x1[:, c, :]).then_inc(s_x1st, 16)

            for c in range(TT - 1):
                store_x1(c)
            sp.wait_ge(s_mx, 2 * TT)
            for c in range(NCH):
                load(1, c, 1)
            store_x1(TT - 1)
            for c in (2, 3):
                load(2, c, 2)
            sp.wait_ge(s_x1st, 16 * TT)
            sp.wait_ge(s_x1Tp, TT)
            for c in (0, 1):
                load(2, c, 2)

            def reload(e, b, used):
                for c in range(NCH):
                    sp.wait_ge(s_used, used + c + 2)
                    n = c * CHUNK
                    src = w_gu[bass.ds(e, 1), :, n:n + CHUNK] if n < GU else w_down[bass.ds(e, 1), :, n - GU:n - GU + CHUNK]
                    sp.dma_start(w_chunk[b][c], src.rearrange("a p n -> (a p) n")).then_inc(s_w[b][c], 16)

            with sp.Fori(1, N_EXP // SETS) as i:
                for b in range(SETS):
                    reload(sp.snap(i * SETS + b, min_val=0, max_val=N_EXP - 1), b, i * (SETS * NCH) + (b - SETS) * NCH)
            for e in range(N_EXP // SETS * SETS, N_EXP):
                for c in range(NCH):
                    sp.wait_ge(s_used, (e - SETS) * NCH + c + 2)
                    load(e % SETS, c, e)
            sp.wait_ge(s_used, (N_EXP - 2) * NCH + 1)
            sp.dma_start(x1, x1_dram.rearrange("(c p h) d -> p c (h d)", p=P, h=2)).then_inc(s_x1back, 16)
            sp.dma_start(ln_rows[:, 2:4, :], rows[:, 2 * SGU + 2 * D:2 * SGU + 4 * D].partition_broadcast(P).rearrange("p a (i d) -> p (a i) d", i=2)).then_inc(s_lnback, 16)
            for c in range(TT):
                sp.wait_ge(s_x2[c], 1)
                sp.dma_start(out[c * P:(c + 1) * P, :], x1[:, c, :]).then_inc(s_st, 16)
            sp.wait_ge(s_st, 16 * TT)

        @block.gpsimd
        def _(pool):
            pool.wait_ge(s_x[KT // 2 - 1], 48)
            pool.dma_start(sgu_w, sgu_wT).then_inc(s_small, 16)
            pool.dma_start(sgu_ln, rows[:, 0:2 * SGU].partition_broadcast(P).rearrange("p a (i d) -> p (a i) d", i=2)).then_inc(s_small, 16)
            for g in range(4):
                pool.dma_start(sgu_bias[HD * (g % 2):HD * (g % 2) + HD, g // 2, :],
                               sgu_b[g:g + 1, :].partition_broadcast(HD).rearrange("p a q -> p (a q)")).then_inc(s_sgub, 16)
            pool.memset(conv_in[:, :, 0:TAPS - 1], 0.0).then_inc(s_pads, 1)
            pool.memset(raw[:, :, 0:1], 0.0).then_inc(s_pads, 1)
            pool.wait_ge(s_small, 32)
            pool.affine_select(out=sgu_w, in_=sgu_w, compare_op=ALU.is_ge, fill=0.0, base=0,
                               pattern=[[0, 4], [1, P]], channel_multiplier=-1).then_inc(s_masked, 1)
            pool.wait_ge(s_early, 1)
            pool.wait_ge(s_convout, 2)
            for n, z in enumerate((ar[VS[0], 1, :], ar[VS[1], 2, :], diag[0][VS[0], :], diag[1][VS[1], :])):
                pool.memset(z, 0.0).then_inc(s_zero, 1)
                pool.wait_ge(s_zero, n + 1)
            for hp in range(HP):
                pool.wait_ge(s_ch, hp + 1)
                if hp:
                    pool.wait_ge(s_out, hp)
                else:
                    pool.wait_ge(s_const, 16)
                for h in range(2):
                    pool.memset(state[KS[h], 0, h, :], 0.0).then_inc(s_init, 1)
                    pool.wait_ge(s_init, 4 * hp + 2 * h + 1)
                    pool.tensor_copy(state[VS[h], :, h, :],
                                     C("ident_twice")[VS[h], :].unsqueeze(1).broadcast_to([HD, CHUNKS, HD])).then_inc(s_init, 1)
                    pool.wait_ge(s_init, 4 * hp + 2 * h + 2)
                for h in range(2):
                    end = cum[KS[h], :].rearrange("p (c n) -> p c n", c=CHUNKS)[:, :, HD - 1:HD].broadcast_to([HD, CHUNKS, HD])
                    pool.tensor_tensor(diag[h][KS[h], :].rearrange("p (c n) -> p c n", c=CHUNKS),
                                       C("ident_twice")[KS[h], :].unsqueeze(1).broadcast_to([HD, CHUNKS, HD]), end, MUL).then_inc(s_diag, 1)
                    pool.wait_ge(s_diag, 2 * hp + h + 1)
            pool.wait_ge(s_init, 4 * HP)
            for m in range(KT):
                pool.wait_ge(s_m3, m + 1)
                pool.tensor_tensor(mtmp[:, 0, :], mtmp[:, 0, :], mtmp[:, 1, :], ADD).then_inc(s_pool, 1)
                pool.wait_ge(s_pool, m + 1)
                pool.tensor_tensor(merged[:, m, :], mtmp[:, 0, :], mtmp[:, 2, :], ADD).then_inc(s_merged, 1)
            pool.wait_ge(s_mm3, KT)
            pool.wait_ge(s_merged, KT)
            pool.memset(xe, 0.0).then_inc(s_xe0, 1)
            pool.wait_ge(s_xe0, 1)
            pool.wait_ge(s_x1st, 16 * TT)
            pool.wait_ge(s_tab, 1)

            last_half_row, last_row = pool.to_reg(2 * T - 1), pool.to_reg(PASSES * SLOTS - 1)

            def gather(p):
                pool.tensor_copy(idx_now[:, 0:1], idx_tab[:, bass.ds(p, 1)]).then_inc(s_idx, 1)
                pool.wait_ge(s_idx, p + 1)
                pool.sem_inc(s_begun, 1)
                pool.indirect_dma_start(xe, None, x1_dram, bass.IndirectOffsetOnAxis(ap=idx_now[:, 0:1], axis=0),
                                        bounds_check=last_half_row, oob_is_err=False).then_inc(s_xe, 16)

            def one_pass(p):
                pool.wait_ge(s_xe, p * 16 + 16)
                pool.wait_ge(s_xeTp, p + 1)
                gather(p + 1)

            gather(0)
            with pool.Fori(0, N_EXP) as i:
                one_pass(i)
            pool.wait_ge(s_more, 1)
            more = pool.value_load(more_i[0:1, 0:1], min_val=0, max_val=MORE)
            with pool.If(more > 0):
                with pool.Fori(0, more) as i:
                    one_pass(i + N_EXP)
            pool.wait_ge(s_xe, more * 16 + 16 * (N_EXP + 1))
            pool.wait_ge(s_yst, more * 32 + 32 * (N_EXP + 1))
            pool.sem_inc(s_begun, 1)
            for c in range(TT):
                for k in range(TOPK):
                    n = TOPK * c + k
                    pool.indirect_dma_start(pair_y[:, n, :], None, y_dram,
                                            bass.IndirectOffsetOnAxis(ap=pos_i[:, k * TT + c:k * TT + c + 1], axis=0),
                                            bounds_check=last_row, oob_is_err=False).then_inc(s_pair[n], 16)
            pool.wait_ge(s_lnback, 16)
            for c in range(TT - 1):
                pool.wait_ge(s_norm2, c + 1)
                pool.tensor_tensor(x1[:, c, :], x1[:, c, :], ln_rows[:, 2, :], MUL).then_inc(s_gain2, 1)
                pool.wait_ge(s_gain2, c + 1)
                pool.tensor_tensor(x1[:, c, :], x1[:, c, :], ln_rows[:, 3, :], ADD).then_inc(s_x2[c], 1)

        @block.scalar
        def _(act):
            act.dma_start(par_sb[:, 0:N_PAR], par).then_inc(s_par, 16)
            state_ = {"phase": 0, "raw": 0, "seq": 0}

            def take(out, func, rows_=P, **kw):
                ph = state_["phase"]
                act.wait_ge(s_proj, ph + 1)
                n = SGU if 4 <= ph < 8 else T
                act.activation(out, proj[0:rows_, ph % 2, 0:n], func, **kw).then_inc(s_projfree, 1)
                state_["phase"] += 1

            def take_raw(rows_=P):
                n = state_["raw"]
                if n == 0:
                    act.wait_ge(s_pads, 2)
                if n >= 2:
                    act.wait_ge(s_rawfree, n - 1)
                ph = state_["phase"]
                act.wait_ge(s_proj, ph + 1)
                act.activation(raw[0:rows_, n % 2, 1:T + 1], proj[0:rows_, ph % 2, :], ACT.Copy).then_inc(s_projfree, 1)
                state_["phase"] += 1
                state_["raw"] += 1

            for i in range(2):
                take(conv_val[:, i, :], ACT.Copy)
            for i in range(2):
                take(conv_gate[:, i, :], ACT.Sigmoid)
            for c in range(TT):
                take(sgu_v[:, c, :], ACT.Gelu)
            for i in range(2):
                take(sgu_u[:, i, :], ACT.Gelu)
            take_raw(LORA_W + LORA_A)
            take_raw(LORA_G)
            gate = Gates()

            def evac_gates(n):
                for mm in gate.step(n):
                    if mm % KT == KT - 1:
                        g = mm // KT
                        assert state_["phase"] == phase_of_gate(g)
                        take(gates[:, g, :], ACT.Sigmoid)

            act.wait_ge(s_vstat, 1)
            act.activation(sgu_rs, sgu_rs, ACT.Sqrt).then_inc(s_vroot, 1)
            evac_gates(EARLY_FILL["v_norm"])
            act.wait_ge(s_lora, 2)
            act.activation(wl_al[0:LORA_W, :], wl_al[0:LORA_W, :], ACT.Tanh).then_inc(s_th, 1)
            act.activation(gl[0:LORA_G, :], gl[0:LORA_G, :], ACT.Sigmoid).then_inc(s_th, 1)
            evac_gates(EARLY_FILL["conv_sum"])
            evac_gates(EARLY_FILL["conv_sq"])
            act.wait_ge(s_scaled, 1)
            act.wait_ge(s_convvar, 1)
            act.activation(conv_rs, bank[:, 1, :], ACT.Sqrt, bias=par_col(EPS_CONV)).then_inc(s_convroot, 1)
            for i in range(2):
                act.wait_ge(s_convn, i + 1)
                act.wait_ge(s_scaled, 1)
                act.activation(conv_out[:, i, :], conv_sq[:, i, :], ACT.Silu, bias=par_col(CLB + i),
                               scale=par_col(CLG_S + i)).then_inc(s_convout, 1)
            evac_gates(EARLY_FILL["conv_norm"])
            act.wait_ge(s_early, 1)

            for hp in range(HP):
                take_raw()
                take_raw()
                act.wait_ge(s_z, hp + 1)
                act.activation(decay, bank[:, 0, :], ACT.Sigmoid, bias=par_col(W0 + hp)).then_inc(s_decay, 1)
                act.activation(iclr, bank[:, 1, :], ACT.Sigmoid, bias=par_col(A0 + hp)).then_inc(s_iclr, 1)
                act.wait_ge(s_cumlog, hp + 1)
                act.activation(cum, inv, ACT.Exp, scale=-DECAY_SCALE)
                act.activation(inv, inv, ACT.Exp, scale=DECAY_SCALE).then_inc(s_cum, 1)
                take_raw()
                act.wait_ge(s_ss, hp + 1)
                act.activation(norm, bank[:, 2, :], ACT.Sqrt).then_inc(s_norm, 1)
                evac_gates(FILL["prep"])
                act.wait_ge(s_tr, 4 * hp + 1)
                for h in range(2):
                    act.activation(X0[:, h, :, KS[h]],
                                   bank[:, 2, :].rearrange("p (j c) -> p j c", j=TT)[:, :, h * HD:(h + 1) * HD],
                                   ACT.Copy).then_inc(s_tma, 1)
                act.wait_ge(s_tr, 4 * hp + 2)
                act.activation(V, bank[:, 5, :].rearrange("p (j h n) -> p h j n", j=TT, h=2), ACT.Copy).then_inc(s_tma, 1)
                evac_gates(FILL["turned"])
                evac_gates(FILL["scores"])

                def out(stage, *copies):
                    for g in range(2):
                        act.wait_ge(s_dm, 20 * hp + 2 * (stage - 1) + g + 1)
                        for dst, b in copies:
                            d = dst(g)
                            n = d.shape[-1]
                            ins = act.activation(d, bank[:, 3 * g + b, 0:TT * n].rearrange("p (j n) -> p j n", j=TT), ACT.Copy)
                        ins.then_inc(s_da, 1)

                out(1, (lambda g: E[:, g], 0))
                out(2, (lambda g: L16[:, g], 0))
                out(3, (lambda g: X0[:, g, :, VS[g]], 1))
                evac_gates(FILL["solve"])
                out(4, (lambda g: E[:, g], 0))
                for n in (4, 5):
                    evac_gates(FILL["solve"])
                out(6, (lambda g: Y0[:, g], 0))
                for n in (6, 7, 8, 9):
                    evac_gates(FILL["solve"])
                evac_gates(FILL["chain"] * (CHUNKS - 1))
                evac_gates(FILL["y"])
                act.wait_ge(s_ymm, hp + 1)
                act.activation(y_, bank[:, 3, :], ACT.Copy).then_inc(s_y, 1)
                evac_gates(FILL["mean"])
                act.wait_ge(s_var, hp + 1)
                act.activation(yrs, bank[:, 1, :], ACT.Sqrt, bias=par_col(EPS_GN)).then_inc(s_yroot, 1)
                evac_gates(FILL["var"])
            for c in range(TT + 1):
                if c < TT:
                    act.wait_ge(s_lnvar, c + 1)
                    act.activation(ln_rs[:, c:c + 1], ln_rs[:, c:c + 1], ACT.Sqrt).then_inc(s_lnroot, 1)
                if c:
                    act.wait_ge(s_x1Tp, c)
                    b = 2 * ((c - 1) % 2)
                    act.activation(x1T[:, (c - 1) % 2, :, :], bank[:, b:b + 2, :].rearrange("p b (k t) -> p (b k) t", k=4), ACT.Copy).then_inc(s_x1T, 1)
            act.wait_ge(s_scp, 1)
            act.activation(scores[:, :, :], bank[:, 4, 0:TT * N_EXP].rearrange("p (c e) -> p c e", c=TT), ACT.Sigmoid).then_inc(s_score, 1)

            act.wait_ge(s_tab, 1)
            act.sem_inc(s_yfree, 1)
            act.sem_inc(s_yst, 32)

            def one_pass(p):
                act.activation(warm[:, 1:2], warm[:, 0:1], ACT.Silu)
                act.wait_ge(s_hp, p + 1)
                act.activation(h_silu, bank[:, 0, 0:FE // 2], ACT.Silu).then_inc(s_silu, 1)
                act.wait_ge(s_yp, p + 2)
                act.wait_ge(s_yst, p * 32 + 32)
                act.activation(y_e, bank[:, 1, :], ACT.Copy, scale=gate_tab[:, bass.ds(p, 1)]).then_inc(s_ye, 1)
                act.wait_ge(s_ye, p + 1)
                act.sem_inc(s_yfree, 1)
                dst = y_dram.rearrange("(q s) (h d) -> q h s d", s=SLOTS, h=2)
                for h in range(2):
                    act.dma_start(dst[bass.ds(p, 1), h, :, :].rearrange("q s d -> (q s) d"), y_e[SLOTS * h:SLOTS * h + SLOTS, :]).then_inc(s_yst, 16)

            with act.Fori(0, N_EXP) as i:
                one_pass(i)
            act.wait_ge(s_more, 1)
            more = act.value_load(more_i[0:1, 0:1], min_val=0, max_val=MORE)
            with act.If(more > 0):
                with act.Fori(0, more) as i:
                    one_pass(i + N_EXP)
            for c in range(TT):
                act.wait_ge(s_lnvar2, c + 1)
                act.activation(ln_rs[:, c:c + 1], ln_rs[:, c:c + 1], ACT.Sqrt).then_inc(s_lnroot2, 1)
                act.wait_ge(s_scale2, c + 1)
                act.activation(x1[:, c, :], x1[:, c, :], ACT.Identity, scale=ln_rs[:, c:c + 1], bias=ln_mv[:, c, 1:2]).then_inc(s_norm2, 1)

        @block.vector
        def _(dve):
            seq = {"n": 0, "raw": 0}

            def then(ins):
                seq["n"] += 1
                ins.then_inc(s_dve, 1)
                dve.wait_ge(s_dve, seq["n"])

            dve.wait_ge(s_par, 16)
            dve.tensor_scalar(par_sb[:, CLG_S:CLG_S + 2], par_sb[:, CLG:CLG + 2], CONV ** 0.5, None, MUL)
            dve.memset(par_sb[:, EPS_CONV:EPS_CONV + 1], CONV * LN_EPS)
            dve.memset(par_sb[:, EPS_GN:EPS_GN + 1], HD * GN_EPS)
            dve.tensor_scalar(par_sb[:, GNG_S:GNG_S + 4], par_sb[:, GNG:GNG + 4], HD ** 0.5, None, MUL).then_inc(s_scaled, 1)
            dve.wait_ge(s_scaled, 1)

            dve.wait_ge(s_projfree, 4)
            dve.wait_ge(s_pads, 2)
            for i in range(2):
                dve.tensor_tensor(conv_in[:, i, TAPS - 1:PADDED], conv_val[:, i, :], conv_gate[:, i, :], MUL).then_inc(s_convin, 1)
            dve.wait_ge(s_convin, 2)
            for tap in range(TAPS):
                for i in range(2):
                    src, w = conv_in[:, i, tap:tap + T], par_col(CDW + TAPS * i + tap)
                    if tap >= 1:
                        dve.wait_ge(s_convacc, 2 * tap + i - 1)
                    if tap == 0:
                        ins = dve.tensor_scalar(conv_acc[:, i, :], src, w, par_col(CDB + i), MUL, ADD)
                    else:
                        ins = dve.scalar_tensor_tensor(conv_acc[:, i, :], src, w, conv_acc[:, i, :], MUL, ADD)
                    ins.then_inc(s_convacc, 1)

            def shift(dst, mu, rows_=P, done=None):
                n = seq["raw"]
                seq["raw"] += 1
                ph = 10 + n if n < 2 else 12 + EARLY + (3 + PAIR_GATES) * ((n - 2) // 3) + (n - 2) % 3
                dve.wait_ge(s_projfree, ph + 1)
                now, before = raw[0:rows_, n % 2, 1:T + 1], raw[0:rows_, n % 2, 0:T]
                then(dve.tensor_tensor(dst, before, now, SUB))
                dve.scalar_tensor_tensor(dst, dst, par_sb[0:rows_, MU + mu:MU + mu + 1], now, MUL, ADD).then_inc(s_rawfree, 1)

            dve.wait_ge(s_projfree, 8)
            for c in range(TT):
                ins = dve.bn_stats(sgu_stat[:, c, :], sgu_v[:, c, :])
            then(ins)
            for c in range(TT):
                ins = dve.bn_aggr(sgu_mv[:, c, :], sgu_stat[:, c, :])
            then(ins)
            dve.tensor_scalar(sgu_rs, sgu_mv[:, :, 1], LN_EPS, None, ADD).then_inc(s_vstat, 1)
            dve.wait_ge(s_vroot, 1)
            then(dve.reciprocal(sgu_rs, sgu_rs))
            for c in range(TT):
                ins = dve.tensor_scalar(sgu_v[:, c, :], sgu_v[:, c, :], sgu_mv[:, c, 0:1], sgu_rs[:, c:c + 1], SUB, MUL)
            then(ins)
            dve.wait_ge(s_small, 32)
            then(dve.tensor_tensor(sgu_v, sgu_v, sgu_ln[:, 0:1, :].broadcast_to([P, TT, SGU]), MUL))
            dve.tensor_tensor(sgu_v, sgu_v, sgu_ln[:, 1:2, :].broadcast_to([P, TT, SGU]), ADD).then_inc(s_vln, 1)

            shift(wl_al[0:LORA_W + LORA_A, :], 12, LORA_W + LORA_A)
            shift(gl[0:LORA_G, :], 13, LORA_G)
            dve.wait_ge(s_rawfree, 2)
            dve.sem_inc(s_lora, 2)

            dve.wait_ge(s_convsum, 1)
            for i in range(2):
                ins = dve.scalar_tensor_tensor(conv_acc[:, i, :], bank[:, 0, :], -1.0 / CONV, conv_acc[:, i, :], MUL, ADD)
            then(ins)
            for i in range(2):
                dve.tensor_tensor(conv_sq[:, i, :], conv_acc[:, i, :], conv_acc[:, i, :], MUL).then_inc(s_convsq, 1)
            dve.wait_ge(s_convroot, 1)
            then(dve.reciprocal(conv_rs, conv_rs))
            for i in range(2):
                dve.tensor_tensor(conv_sq[:, i, :], conv_acc[:, i, :], conv_rs, MUL).then_inc(s_convn, 1)

            dve.wait_ge(s_mix, 1)
            dve.wait_ge(s_sgub, 64)
            dve.wait_ge(s_projfree, 10)
            for i in range(2):
                ins = dve.tensor_tensor(sgu_mix[:, i, :].rearrange("p (c q) -> p c q", c=TT),
                                        bank[:, 2 + i, :].rearrange("p (c q) -> p c q", c=TT),
                                        sgu_bias[:, i:i + 1, :].broadcast_to([P, TT, P]), ADD)
            then(ins)
            dve.tensor_tensor(sgu_out[:, :, :], sgu_mix, sgu_u, MUL).then_inc(s_early, 1)
            dve.wait_ge(s_early, 1)
            dve.wait_ge(s_convout, 2)

            dve.wait_ge(s_const, 16)
            chunked = "p (c n) -> p c n"
            then(dve.memset(carry, 1.0))
            then(dve.memset(carry[:, ::HD], 0.0))
            for hp in range(HP):
                shift(r_, 0 + hp)
                shift(k_, 4 + hp)
                dve.wait_ge(s_rawfree, 2 + 3 * hp + 2)
                then(dve.tensor_scalar(kk, k_, par_col(KK_ + hp), None, MUL))
                dve.tensor_tensor(sq, kk, kk, MUL).then_inc(s_sq, 1)
                dve.wait_ge(s_decay, hp + 1)
                dve.tensor_tensor_scan(inv, carry, decay, 0.0, MUL, ADD).then_inc(s_cumlog, 1)
                dve.wait_ge(s_iclr, hp + 1)
                then(dve.tensor_scalar(kh, iclr, 1.0, par_col(KA_ + hp), SUB, MUL))
                then(dve.scalar_tensor_tensor(kh, kh, 1.0, k_, ADD, MUL))
                dve.scalar_tensor_tensor(kkn, r_, par_col(RK_ + hp), kh, MUL, MUL).then_inc(s_pr, 1)
                shift(v_, 8 + hp)
                dve.wait_ge(s_norm, hp + 1)
                then(dve.tensor_scalar(norm, norm, 1e-12, None, MAX))
                then(dve.reciprocal(norm, norm))
                dve.wait_ge(s_cum, hp + 1)
                dve.wait_ge(s_bs, hp + 1)
                then(dve.scalar_tensor_tensor(kkn, kk, -1.0, norm, MUL, MUL))
                k3, c3, a3 = (v.rearrange(chunked, c=CHUNKS) for v in (kkn, cum, ar[:, 0, :]))
                dve.tensor_tensor(a3[:, :, 1:HD], k3[:, :, 1:HD], c3[:, :, 0:HD - 1], MUL)
                dve.tensor_copy(a3[:, :, 0:1], k3[:, :, 0:1])
                for h in range(2):
                    dve.tensor_tensor(ar[KS[h], 1 + h, :], r_[KS[h], :], cum[KS[h], :], MUL)
                then(dve.tensor_tensor(norm, iclr, inv, MUL))
                dve.scalar_tensor_tensor(bT, kkn, -1.0, norm, MUL, MUL)
                then(dve.tensor_tensor(kT, kh, inv, MUL))
                end = cum.rearrange(chunked, c=CHUNKS)[:, :, HD - 1:HD].broadcast_to([P, CHUNKS, HD])
                dve.tensor_tensor(bH.rearrange(chunked, c=CHUNKS), bT.rearrange(chunked, c=CHUNKS), end, MUL)
                dve.tensor_tensor(kH.rearrange(chunked, c=CHUNKS), kT.rearrange(chunked, c=CHUNKS), end, MUL)
                dve.wait_ge(s_rawfree, 2 + 3 * hp + 3)
                dve.tensor_tensor(bonus, bank[:, 3, :], v_, MUL).then_inc(s_ch, 1)

                for n, dst in enumerate((BR, KR)):
                    dve.wait_ge(s_tr, 4 * hp + 3 + n)
                    dve.tensor_copy(dst[:, :, :, 0:HD], bank[:, 3 + n, :].rearrange("p (j h n) -> p h j n", j=TT, h=2)).then_inc(s_tmd, 1)

                dve.wait_ge(s_sc, hp + 1)

                def mask(name, n=P):
                    at = CONSTS[name][0]
                    return const[:, at:at + n].unsqueeze(1).broadcast_to([P, 2 * TT, n])

                def both(t):
                    return t.rearrange("p h j n -> p (h j) n")

                def spread(src, name, dst):
                    return dve.tensor_tensor(both(dst).rearrange("p u (c n) -> p u c n", c=2), src.unsqueeze(2).broadcast_to([P, 2 * TT, 2, HD]),
                                             mask(name).rearrange("p u (c n) -> p u c n", c=2), MUL)

                ab, back = (bank[:, b:b + 2, :].rearrange("p h (j n) -> p (h j) n", j=TT) for b in (0, 3))
                spread(ab[:, :, 0:HD], "within16T", L16T)
                spread(back[:, :, 0:HD], "within16", L16)
                spread(back[:, :, 0:HD], "across16", LX)
                dve.tensor_tensor(both(BR)[:, :, HD:P], ab[:, :, HD:P], mask("uptoT", HD), MUL).then_inc(s_scev, 1)
                dve.wait_ge(s_scev, 3 * hp + 1)
                dve.tensor_tensor(both(ZT), both(L16T), mask("ident"), ADD).then_inc(s_scev, 1)
                for h in range(2):
                    ak = bank[:, 2 + 3 * h, :].rearrange("p (j n) -> p j n", j=TT)
                    dve.tensor_tensor(AK[:, h], ak[:, :, 0:HD], mask("beforeT", HD)[:, 0:TT, :], MUL)
                    ins = dve.tensor_tensor(KR[:, h, :, HD:P], ak[:, :, HD:P], mask("uptoT", HD)[:, 0:TT, :], MUL)
                ins.then_inc(s_scev, 1)
                dve.wait_ge(s_scev, 3 * hp + 2)

                def stage(n, f):
                    for g in range(2):
                        dve.wait_ge(s_dm, 20 * hp + 2 * (n - 1) + g + 1)
                        f(g, lambda b, n=P: bank[:, 3 * g + b, 0:TT * n].rearrange("p (j n) -> p j n", j=TT)).then_inc(s_dd, 1)

                def grow(g, b):
                    return dve.tensor_tensor(ZT[:, g], ZT[:, g], b(2), ADD)

                stage(1, lambda g, b: dve.tensor_copy(ET[:, g], b(1)))
                stage(2, grow)
                dve.wait_ge(s_dd, 18 * hp + 4)
                stage(3, grow)
                dve.wait_ge(s_dd, 18 * hp + 6)
                stage(5, grow)
                stage(6, lambda g, b: dve.tensor_copy(ET[:, g], b(2)))
                stage(7, lambda g, b: dve.tensor_tensor(Y1[:, g], b(1), Y0[:, g], ADD))
                stage(8, lambda g, b: dve.tensor_tensor(Y2[:, g], b(0), Y0[:, g], ADD))
                stage(9, lambda g, b: dve.tensor_tensor(Y1[:, g], b(1), Y0[:, g], ADD))
                dve.wait_ge(s_diag, 2 * hp + 2)
                def maps(n, g, dst, own):
                    src = bank[:, 3 * g + 1:3 * g + 3, :].rearrange("p c (j w n) -> p w j c n", j=TT, w=2)[:, n]
                    return dve.tensor_tensor(dst[:, g].rearrange("p j (c n) -> p j c n", c=2), src, own.rearrange("p (j c n) -> p j c n", j=TT, c=2), ADD)

                stage(10, lambda g, b: maps(0, g, gh, diag[g]))

                dve.wait_ge(s_init, 4 * hp + 4)
                for c in range(CHUNKS - 1):
                    for h in range(2):
                        dve.wait_ge(s_cm, 2 * (CHUNKS - 1) * hp + 2 * c + h + 1)
                        dve.tensor_copy(state[KS[h], c + 1, h, :], bank[KS[h], 0, HD * (c % 2):HD * (c % 2) + HD]).then_inc(s_ce, 1)
                    if c in (1, 3):
                        g = c // 2
                        maps(1, g, out2, ar[:, 1 + g, :]).then_inc(s_out2, 1)
                dve.wait_ge(s_mu, hp + 1)
                dve.wait_ge(s_y, hp + 1)
                then(dve.scalar_tensor_tensor(yc, bank[:, 4, :], -1.0 / HD, y_, MUL, ADD))
                dve.tensor_tensor(ysq, yc, yc, MUL).then_inc(s_yc, 1)
                dve.wait_ge(s_yroot, hp + 1)
                then(dve.reciprocal(yrs, yrs))
                then(dve.tensor_tensor(yn, yc, yrs, MUL))
                then(dve.tensor_scalar(yn, yn, par_col(GNG_S + hp), par_col(GNB + hp), MUL, ADD))
                then(dve.tensor_tensor(yn, yn, bonus, ADD))
                dve.tensor_tensor(rwkv_out[:, hp, :], yn, bank[:, 5, :], MUL).then_inc(s_out, 1)
                dve.wait_ge(s_out, hp + 1)

            for m in range(KT):
                dve.wait_ge(s_mm3, m + 1)
                if m == 0:
                    dve.wait_ge(s_projfree, phase_of_gate(GATE_TILES - 1) + 1)
                if m:
                    dve.wait_ge(s_merged, m)
                for n in range(3):
                    ins = dve.tensor_tensor(mtmp[:, n, :], bank[:, 3 * (m % 2) + n, :], gates[:, KT * n + m, :], MUL)
                ins.then_inc(s_m3, 1)
            dve.wait_ge(s_xtok, 16)
            for c in range(TT):
                for i in range(2):
                    n = 2 * c + i
                    dve.wait_ge(s_mx, n + 1)
                    part = x1[:, c, T * i:T * i + T]
                    dve.scalar_tensor_tensor(part, part, ALPHA, proj[:, n % 2, :], MUL, ADD).then_inc(s_pre, 1)
                dve.wait_ge(s_pre, 2 * c + 2)
                for i in range(2):
                    ins = dve.bn_stats(ln_stat[:, c, 6 * i:6 * i + 6], x1[:, c, T * i:T * i + T])
                then(ins)
                then(dve.bn_aggr(ln_mv[:, c, :], ln_stat[:, c, :]))
                dve.tensor_scalar(ln_rs[:, c:c + 1], ln_mv[:, c, 1:2], LN_EPS, None, ADD).then_inc(s_lnvar, 1)
                dve.wait_ge(s_lnroot, c + 1)
                then(dve.reciprocal(ln_rs[:, c:c + 1], ln_rs[:, c:c + 1]))
                then(dve.tensor_scalar(x1[:, c, :], x1[:, c, :], ln_mv[:, c, 0:1], ln_rs[:, c:c + 1], SUB, MUL))
                if c == 0:
                    dve.wait_ge(s_lnrows, 16)
                then(dve.tensor_tensor(x1[:, c, :], x1[:, c, :], ln_rows[:, 0, :], MUL))
                dve.tensor_tensor(x1[:, c, :], x1[:, c, :], ln_rows[:, 1, :], ADD).then_inc(s_x1, 1)

            def bc(name, shape, n=None):
                v = C(name) if n is None else C(name)[:, 0:n]
                return v.unsqueeze(1).broadcast_to([P, shape, n or CONSTS[name][1]])

            NG = TT * GROUPS
            dve.memset(warm, 0.0)
            dve.memset(chosen[:, 0, :], 0.0)
            dve.wait_ge(s_score, 1)
            dve.wait_ge(s_rw, 32)
            then(dve.tensor_tensor(sel[:, :, :], scores[:, :, :], rb_sb[:, :].unsqueeze(1).broadcast_to([P, TT, N_EXP]), ADD))
            sel_g = sel[:, :, :].rearrange("p c (g e) -> p (c g) e", g=GROUPS)
            for n in range(NG):
                ins = dve.max(top8[:, n, :], sel_g[:, n, :])
            then(ins)
            then(dve.tensor_tensor(grp[:, 0, :], top8[:, :, 0], top8[:, :, 1], ADD))
            g4 = [grp[:, n, :].rearrange("p (c g) -> p c g", c=TT) for n in range(3)]
            then(dve.tensor_reduce(small[:, 0, 0:TT], g4[0], AX_X, MAX))
            then(dve.tensor_tensor(g4[1], g4[0], small[:, 0, 0:TT].unsqueeze(2).broadcast_to([P, TT, GROUPS]), ALU.is_equal))
            then(dve.tensor_tensor(g4[1], g4[1], bc("group_left", TT), MUL))
            then(dve.tensor_reduce(small[:, 0, 0:TT], g4[1], AX_X, MAX))
            then(dve.tensor_tensor(g4[2], g4[1], small[:, 0, 0:TT].unsqueeze(2).broadcast_to([P, TT, GROUPS]), ALU.is_equal))
            then(dve.tensor_tensor(sel_g, sel_g, grp[:, 2, :].unsqueeze(2).broadcast_to([P, NG, PER_GROUP]), MUL))
            then(dve.tensor_scalar(grp[:, 1, :], grp[:, 2, :], 1.0, BIG, SUB, MUL))
            then(dve.tensor_tensor(sel_g, sel_g, grp[:, 1, :].unsqueeze(2).broadcast_to([P, NG, PER_GROUP]), ADD))
            best = small[:, 1, 0:TT]
            for k in range(TOPK):
                pick = hot[:, k, :, :]
                then(dve.tensor_reduce(best, sel[:, :, :], AX_X, MAX))
                then(dve.tensor_tensor(pick, sel[:, :, :], best.unsqueeze(2).broadcast_to([P, TT, N_EXP]), ALU.is_equal))
                then(dve.tensor_tensor(pick, pick, bc("expert_left", TT), MUL))
                then(dve.tensor_reduce(best, pick, AX_X, MAX))
                then(dve.tensor_tensor(pick, pick, best.unsqueeze(2).broadcast_to([P, TT, N_EXP]), ALU.is_equal))
                if k == 0:
                    then(dve.scalar_tensor_tensor(sel[:, :, :], pick, -3 * BIG, sel[:, :, :], MUL, ADD))
            dve.tensor_tensor(chosen[:, 1:, :], hot[:, 0, :, :], hot[:, 1, :, :], ADD).then_inc(s_chosen, 1)

            KC = TOPK * TT
            hot_f = hot[:, :, :, :].rearrange("p k c e -> p (k c) e")
            work = rt[0].rearrange("p (n e) -> p n e", n=KC)
            GATE_, RANK, QUOT, BASE, PASS_, POS, TMP = range(2, 9)

            def picked(dst, row):
                then(dve.tensor_tensor(work, hot_f, row, MUL))
                then(dve.tensor_reduce(small[:, dst, :], work, AX_X, ADD))

            work4 = work.rearrange("p (k c) e -> p k c e", k=TOPK)
            for k in range(TOPK):
                ins = dve.tensor_tensor(work4[:, k, :, :], hot[:, k, :, :], scores[:, :, :], MUL)
            then(ins)
            then(dve.tensor_reduce(small[:, GATE_, :], work, AX_X, ADD))
            then(dve.tensor_tensor(small[:, TMP, 0:TT], small[:, GATE_, 0:TT], small[:, GATE_, TT:KC], ADD))
            then(dve.reciprocal(small[:, TMP, 0:TT], small[:, TMP, 0:TT]))
            for k in range(TOPK):
                ins = dve.tensor_tensor(small[:, GATE_, k * TT:(k + 1) * TT], small[:, GATE_, k * TT:(k + 1) * TT], small[:, TMP, 0:TT], MUL)
            then(ins)
            dve.wait_ge(s_rank, 1)
            rank_ps = bank[:, 5, 0:TT * N_EXP].rearrange("p (c e) -> p c e", c=TT)
            for k in range(TOPK):
                ins = dve.tensor_tensor(work4[:, k, :, :], hot[:, k, :, :], rank_ps, MUL)
            dve.memset(count[:, 3, :], 0.0)
            then(ins)
            EXTRA, INCL, FIRST, ZERO = range(4)
            NM = T // SLOTS - 1
            over = rt[2][:, 0:N_EXP * NM].rearrange("p (e n) -> p e n", n=NM)
            quot = rt[3][:, 0:KC * NM].rearrange("p (e n) -> p e n", n=NM)
            dve.tensor_reduce(small[:, RANK, :], work, AX_X, ADD)
            then(dve.tensor_tensor(over, bank[:, 5, TT * N_EXP:(TT + 1) * N_EXP].unsqueeze(2).broadcast_to([P, N_EXP, NM]), bc("multiples", N_EXP), ALU.is_gt))
            dve.tensor_tensor(quot, small[:, RANK, :].unsqueeze(2).broadcast_to([P, KC, NM]), bc("multiples", KC), ALU.is_ge)
            then(dve.tensor_reduce(count[:, EXTRA, :], over, AX_X, ADD))
            then(dve.tensor_tensor_scan(count[:, INCL, :], count[:, EXTRA, :], count[:, ZERO, :], 0.0, ADD, ADD))
            dve.tensor_reduce(small[:, QUOT, :], quot, AX_X, ADD)
            then(dve.tensor_tensor(count[:, FIRST, :], count[:, INCL, :], count[:, EXTRA, :], SUB))
            then(dve.tensor_tensor(count[:, FIRST, :], count[:, FIRST, :], C("iota")[:, 0:N_EXP], ADD))
            picked(BASE, count[:, FIRST, :].unsqueeze(1).broadcast_to([P, KC, N_EXP]))
            dve.scalar_tensor_tensor(small[:, RANK, :], small[:, QUOT, :], -float(SLOTS), small[:, RANK, :], MUL, ADD)
            then(dve.tensor_tensor(small[:, PASS_, :], small[:, BASE, :], small[:, QUOT, :], ADD))
            dve.tensor_copy(extra_i[:, :], count[:, EXTRA, :])
            dve.tensor_copy(first_i[:, :], count[:, FIRST, :]).then_inc(s_first, 1)

            def over_passes(v):
                return v.unsqueeze(2).broadcast_to([P, KC, PASSES])

            then(dve.tensor_tensor(pass_hot[:, :, 0, :], bc("iota", KC, PASSES), over_passes(small[:, PASS_, :]), ALU.is_equal))
            dve.tensor_tensor(pass_hot[:, :, 1, :], pass_hot[:, :, 0, :], over_passes(C("token")), MUL)
            dve.tensor_tensor(pass_hot[:, :, 2, :], pass_hot[:, :, 0, :], over_passes(small[:, GATE_, :]), MUL)
            for n in range(0, KC, 2):
                dve.tensor_tensor(slot_hot[:, n:n + 2, :], C("slot_iota").unsqueeze(1).broadcast_to([P, 2, P]),
                                  small[:, RANK, n:n + 2].unsqueeze(2).broadcast_to([P, 2, P]), ALU.is_equal).then_inc(s_hot, 1)
            dve.wait_ge(s_tabp, 1)
            tab = bank[:, 4, 0:3 * PASSES].rearrange("p (i q) -> p i q", i=3)
            then(dve.tensor_scalar(idx_f[:, :], tab[:, 0, :], 1.0, -4.0 * T, SUB, MUL))
            then(dve.scalar_tensor_tensor(idx_f[:, :], tab[:, 1, :], 2.0, idx_f[:, :], MUL, ADD))
            dve.tensor_copy(gate_tab[:, :], tab[:, 2, :])
            dve.tensor_scalar(idx_tab[:, :], idx_f[:, :], C("half"), None, ADD).then_inc(s_tab, 1)
            then(dve.scalar_tensor_tensor(small[:, POS, :], small[:, PASS_, :], float(SLOTS), small[:, RANK, :], MUL, ADD))
            dve.tensor_copy(pos_i[:, :], small[:, POS, :])
            dve.tensor_copy(more_i[:, :], count[:, INCL, N_EXP - 1:N_EXP]).then_inc(s_more, 1)

            def one_pass(p, tokens_only=False):
                dve.wait_ge(s_hp, p + 1)
                dve.wait_ge(s_silu, p + 1)
                dve.tensor_tensor(h_e, h_silu, bank[:, 0, FE // 2:FE], MUL).then_inc(s_h, 1)
                turned(p + 1)
                dve.wait_ge(s_hTp, p + 1)
                dve.tensor_copy(hT, bank[:, 3, 0:FE // 2].rearrange("p (c s) -> p c s", c=2)).then_inc(s_hT, 1)

            def turned(p):
                dve.wait_ge(s_xeTp, p + 1)
                dve.tensor_copy(xeT, bank[:, 2, :].rearrange("p (c s) -> p c s", c=4)).then_inc(s_xeT, 1)

            turned(0)
            with dve.Fori(0, N_EXP) as i:
                one_pass(i)
            dve.wait_ge(s_more, 1)
            more = dve.value_load(more_i[0:1, 0:1], min_val=0, max_val=MORE)
            with dve.If(more > 0):
                with dve.Fori(0, more) as i:
                    one_pass(i + N_EXP)
            for c in range(TT):
                if c == 0:
                    dve.wait_ge(s_x1back, 16)
                dve.wait_ge(s_pair[TOPK * c], 16)
                then(dve.scalar_tensor_tensor(x1[:, c, :], x1[:, c, :], ALPHA, pair_y[:, 2 * c, :], MUL, ADD))
                dve.wait_ge(s_pair[TOPK * c + 1], 16)
                then(dve.tensor_tensor(x1[:, c, :], x1[:, c, :], pair_y[:, 2 * c + 1, :], ADD))
                for i in range(2):
                    ins = dve.bn_stats(ln_stat[:, c, 6 * i:6 * i + 6], x1[:, c, T * i:T * i + T])
                then(ins)
                then(dve.bn_aggr(ln_mv[:, c, :], ln_stat[:, c, :]))
                dve.tensor_scalar(ln_rs[:, c:c + 1], ln_mv[:, c, 1:2], LN_EPS, None, ADD).then_inc(s_lnvar2, 1)
                dve.wait_ge(s_lnroot2, c + 1)
                then(dve.reciprocal(ln_rs[:, c:c + 1], ln_rs[:, c:c + 1]))
                dve.scalar_tensor_tensor(ln_mv[:, c, 1:2], ln_mv[:, c, 0:1], -1.0, ln_rs[:, c:c + 1], MUL, MUL).then_inc(s_scale2, 1)
            dve.wait_ge(s_norm2, TT)
            dve.wait_ge(s_lnback, 16)
            then(dve.tensor_tensor(x1[:, TT - 1, :], x1[:, TT - 1, :], ln_rows[:, 2, :], MUL))
            dve.tensor_tensor(x1[:, TT - 1, :], x1[:, TT - 1, :], ln_rows[:, 3, :], ADD).then_inc(s_x2[TT - 1], 1)

        @block.tensor
        def _(pe):
            st = {"phase": 0, "tile": 0}

            def open_phase():
                ph = st["phase"]
                st["phase"] += 1
                if ph >= 2:
                    pe.wait_ge(s_projfree, ph - 1)
                return ph % 2

            def tile_in():
                n = st["tile"]
                st["tile"] += 1
                pe.wait_ge(s_win[n % RING], 16 * (n // RING + (n % RING >= 2)))
                return n % RING

            def channels(w=P):
                slot, b = tile_in(), open_phase()
                for k in range(KT):
                    ins = pe.matmul(proj[0:w, b, :], ring[:, slot, k, 0:w], xT_sb[:, k, :], start=(k == 0), stop=(k == KT - 1))
                ins.then_inc(s_proj, 1)

            for k in range(KT):
                if k % 2 == 0:
                    pe.wait_ge(s_x[k // 2], 48)
                for b in range(2):
                    ins = pe.matmul(proj[:, b, :], ring[:, b, k, :], xT_sb[:, k, :], start=(k == 0), stop=(k == KT - 1))
                    if k == KT - 1:
                        ins.then_inc(s_proj, 1)
            st["phase"], st["tile"] = 2, 2
            for _ in range(2):
                channels()
            slot = tile_in()
            tile_in()
            for c in range(TT):
                b = open_phase()
                for k in range(KT):
                    ins = pe.matmul(proj[:, b, 0:SGU], xT_sb[:, k, c * P:(c + 1) * P],
                                    ring[:, slot:slot + 2, k, :], start=(k == 0), stop=(k == KT - 1))
                ins.then_inc(s_proj, 1)
            for _ in range(2):
                channels()
            channels(LORA_W + LORA_A)
            channels(LORA_G)

            gate = Gates()
            gate_at = {}

            def fill(n):
                for mm in gate.step(n):
                    k = mm % KT
                    if k == 0:
                        gate_at["slot"], gate_at["bank"] = tile_in(), open_phase()
                    ins = pe.matmul(proj[:, gate_at["bank"], :], ring[:, gate_at["slot"], k, :], xT_sb[:, k, :],
                                    start=(k == 0), stop=(k == KT - 1))
                    if k == KT - 1:
                        ins.then_inc(s_proj, 1)

            fill(EARLY_FILL["v_norm"])
            pe.wait_ge(s_vln, 1)
            pe.wait_ge(s_masked, 1)
            for i in range(2):
                for c in range(TT):
                    for at in range(2):
                        g = 2 * i + at
                        ins = pe.matmul(bank[HD * at:HD * at + HD, 2 + i, c * P:(c + 1) * P], sgu_v[:, c, g * HD:(g + 1) * HD],
                                        sgu_w[:, g, :], start=True, stop=True)
            ins.then_inc(s_mix, 1)
            fill(EARLY_FILL["conv_sum"])
            pe.wait_ge(s_const, 16)
            pe.wait_ge(s_convacc, 2 * TAPS)
            for i in range(2):
                ins = pe.matmul(bank[:, 0, :], C("ones"), conv_acc[:, i, :], start=(i == 0), stop=(i == 1))
            ins.then_inc(s_convsum, 1)
            fill(EARLY_FILL["conv_sq"])
            pe.wait_ge(s_convsq, 2)
            for i in range(2):
                ins = pe.matmul(bank[:, 1, :], C("ones"), conv_sq[:, i, :], start=(i == 0), stop=(i == 1))
            ins.then_inc(s_convvar, 1)
            fill(EARLY_FILL["conv_norm"])

            for hp in range(HP):
                ch = slice(P * hp, P * hp + P)
                channels()
                channels()
                if hp == 0:
                    pe.wait_ge(s_early, 1)
                    pe.wait_ge(s_convn, 2)
                    pe.wait_ge(s_th, 2)
                    pe.wait_ge(s_lora_in, 16)
                else:
                    pe.wait_ge(s_out, hp)
                pe.matmul(bank[:, 0, :], lora_sb[0:LORA_W, 0, ch], wl_al[0:LORA_W, :], start=True, stop=True)
                pe.matmul(bank[:, 1, :], lora_sb[LORA_W:LORA_W + LORA_A, 0, ch], wl_al[LORA_W:LORA_W + LORA_A, :],
                          start=True, stop=True).then_inc(s_z, 1)
                channels()
                pe.wait_ge(s_sq, hp + 1)
                pe.matmul(bank[:, 2, :], C("head_ones"), sq, start=True, stop=True).then_inc(s_ss, 1)
                pe.wait_ge(s_pr, hp + 1)
                pe.matmul(bank[:, 3, :], C("head_ones"), kkn, start=True, stop=True).then_inc(s_bs, 1)
                fill(FILL["prep"])
                pe.wait_ge(s_ch, hp + 1)
                for b, src in ((2, ar[:, 0, :]), (5, v_), (3, bH), (4, kH)):
                    for j in range(TT):
                        ins = pe.transpose(bank[:, b, j * P:(j + 1) * P], src[:, j * P:(j + 1) * P], C("ident"))
                    ins.then_inc(s_tr, 1)
                fill(FILL["turned"])
                pe.wait_ge(s_tma, 3 * hp + 3)
                pe.wait_ge(s_tmd, 2 * hp + 2)
                quarters = [(h, c) for h in range(2) for c in range(2)]
                for j in range(TT):
                    for banks, lhs in (((0, 1), bT), ((2, 5), kT)):
                        for h, c in quarters:
                            t = slice(j * P + HD * c, j * P + HD * c + HD)
                            pe.matmul(bank[HD * c:HD * c + HD, banks[h], j * P:(j + 1) * P], lhs[KS[h], t],
                                      ar[KS[h], 0:2 + h:1 + h, t], start=True, stop=True)
                    for h, c in quarters:
                        t = slice(j * P + HD * c, j * P + HD * c + HD)
                        ins = pe.matmul(bank[HD * c:HD * c + HD, 3 + h, j * P:j * P + HD], ar[KS[h], 0, t], bT[KS[h], t], start=True, stop=True)
                ins.then_inc(s_sc, 1)
                fill(FILL["scores"])

                def stage(acts, dves, products, more=0):
                    for g in range(2):
                        if acts:
                            pe.wait_ge(s_da, 10 * hp + 2 * (acts - 1) + g + 1)
                        if dves:
                            pe.wait_ge(s_dd, 18 * hp + 2 * (dves - 1) + g + 1)
                        for b, lhsT, rhs in products(g):
                            for j in range(TT):
                                ins = pe.matmul(bank[:, 3 * g + b, j * P:j * P + P], lhsT[:, j, :], rhs[:, j, :], start=True, stop=True)
                        ins.then_inc(s_dm, 1)
                    fill(more)

                more = FILL["solve"]
                pe.wait_ge(s_scev, 3 * hp + 1)
                stage(0, 0, lambda g: [(0, L16T[:, g], L16[:, g]), (1, L16[:, g], L16T[:, g])])
                pe.wait_ge(s_scev, 3 * hp + 3)
                stage(1, 1, lambda g: [(0, ET[:, g], E[:, g]), (2, E[:, g], ZT[:, g])])
                for g in range(2):
                    pe.wait_ge(s_da, 10 * hp + 2 + g + 1)
                    pe.wait_ge(s_dd, 18 * hp + 2 + g + 1)
                    for j in range(TT):
                        for c in range(2):
                            t = slice(HD * c, HD * c + HD)
                            pe.matmul(bank[t, 3 * g + 1, j * HD:j * HD + HD], AK[t, g, j, :], V[t, g, j, :], start=True, stop=True)
                    for j in range(TT):
                        ins = pe.matmul(bank[:, 3 * g + 2, j * P:j * P + P], L16[:, g, j, :], ZT[:, g, j, :], start=True, stop=True)
                    ins.then_inc(s_dm, 1)
                fill(more)
                stage(3, 3, lambda g: [(0, L16[:, g], ZT[:, g])], more)
                stage(4, 0, lambda g: [(2, L16[:, g], E[:, g])], more)
                stage(0, 4, lambda g: [(0, ZT[:, g], X0[:, g]), (2, LX[:, g], ZT[:, g])], more)
                stage(5, 5, lambda g: [(1, ET[:, g], Y0[:, g])], more)
                stage(0, 6, lambda g: [(0, ET[:, g], Y1[:, g])], more)
                stage(0, 7, lambda g: [(1, ET[:, g], Y2[:, g])], more)
                for g in range(2):
                    pe.wait_ge(s_dd, 18 * hp + 14 + g + 1)
                    for j in range(TT):
                        at, t = slice(j * P, (j + 1) * P), [slice(HD * c, HD * c + HD) for c in range(2)]
                        for part in (KS[g], VS[g]):
                            for c in range(2):
                                pe.matmul(bank[part, 3 * g + 1 + c, at], Y1[t[c], g, j, part], BR[t[c], g, j, :], start=True, stop=part == KS[g])
                        for c in range(2):
                            ins = pe.matmul(bank[VS[g], 3 * g + 1 + c, at], V[t[c], g, j, :], KR[t[c], g, j, :], start=False, stop=True)
                    ins.then_inc(s_dm, 1)
                pe.wait_ge(s_init, 4 * hp + 4)
                for c in range(CHUNKS - 1):
                    for h in range(2):
                        if c == 0:
                            pe.wait_ge(s_dd, 18 * hp + 17 + h)
                        else:
                            pe.wait_ge(s_ce, 2 * (CHUNKS - 1) * hp + 2 * c - 1 + h)
                        pe.matmul(bank[KS[h], 0, HD * (c % 2):HD * (c % 2) + HD], gh[:, h, c // 2, HD * (c % 2):HD * (c % 2) + HD],
                                  state[:, c, h, :], start=True, stop=True).then_inc(s_cm, 1)
                    fill(FILL["chain"])
                pe.wait_ge(s_ce, 2 * (CHUNKS - 1) * (hp + 1))
                pe.wait_ge(s_out2, 2 * hp + 2)
                for c in range(CHUNKS):
                    for h in range(2):
                        ins = pe.matmul(bank[HD * h:HD * h + HD, 3, HD * c:HD * c + HD], state[:, c, h, :],
                                        out2[:, h, c // 2, HD * (c % 2):HD * (c % 2) + HD], start=True, stop=True)
                ins.then_inc(s_ymm, 1)
                fill(FILL["y"])
                pe.wait_ge(s_y, hp + 1)
                pe.matmul(bank[:, 5, :], lora_sb[0:LORA_G, 1, ch], gl[0:LORA_G, :], start=True, stop=True)
                pe.matmul(bank[:, 4, :], C("head_ones"), y_, start=True, stop=True).then_inc(s_mu, 1)
                fill(FILL["mean"])
                pe.wait_ge(s_yc, hp + 1)
                pe.matmul(bank[:, 1, :], C("head_ones"), ysq, start=True, stop=True).then_inc(s_var, 1)
                fill(FILL["var"])

            for m in range(KT):
                if m % 4 == 0:
                    pe.wait_ge(s_wo[m // 4], 16)
                if m >= 2:
                    pe.wait_ge(s_m3, m - 1)
                parts = [(2, conv_out, 6, 2), (0, rwkv_out, 0, 4), (1, sgu_out, 4, 2)]
                for n, src, k0, nk in parts:
                    if m == 0 and n == 0:
                        pe.wait_ge(s_out, HP)
                    for k in range(nk):
                        ins = pe.matmul(bank[:, 3 * (m % 2) + n, :], wo_sb[:, k0 + k, m * P:(m + 1) * P], src[:, k, :],
                                        start=(k == 0), stop=(k == nk - 1))
                ins.then_inc(s_mm3, 1)
            def mix(c):
                for i in range(2):
                    n = 2 * c + i
                    if n >= 2:
                        pe.wait_ge(s_pre, n - 1)
                    for k in range(KT):
                        if n == 0:
                            pe.wait_ge(s_merged, k + 1)
                        ins = pe.matmul(proj[:, n % 2, :], merged[:, k, c * P:(c + 1) * P], wout_sb[:, k, T * i:T * i + T],
                                        start=(k == 0), stop=(k == KT - 1))
                    ins.then_inc(s_mx, 1)

            def turn_x1(c):
                pe.wait_ge(s_x1, c + 1)
                if c >= 2:
                    pe.wait_ge(s_x1T, c - 1)
                for k in range(KT):
                    ins = pe.transpose(bank[:, 2 * (c % 2) + k // 4, P * (k % 4):P * (k % 4) + P], x1[:, c, k * P:(k + 1) * P], C("ident"))
                ins.then_inc(s_x1Tp, 1)

            def router(c):
                pe.wait_ge(s_x1T, c + 1)
                for k in range(KT):
                    ins = pe.matmul(bank[:, 4, c * N_EXP:(c + 1) * N_EXP], x1T[:, c % 2, k, :], rw_sb[:, k, :],
                                    start=(k == 0), stop=(k == KT - 1))
                if c == TT - 1:
                    ins.then_inc(s_scp, 1)

            pe.wait_ge(s_wout, 16)
            pe.wait_ge(s_projfree, st["phase"])
            mix(0)
            pe.wait_ge(s_m3, KT)
            pe.wait_ge(s_rw, 32)
            for c in range(TT):
                if c + 1 < TT:
                    mix(c + 1)
                if c:
                    router(c - 1)
                turn_x1(c)
            router(TT - 1)
            pe.wait_ge(s_chosen, 1)
            for n in range(TT + 1, 1, -1):
                pe.matmul(bank[:, 5, (TT + 1 - n) * N_EXP:(TT + 1) * N_EXP], C("ones"), chosen[:, 0:n, :], start=(n == TT + 1), stop=False)
            pe.matmul(bank[:, 5, 0:TT * N_EXP], C("earlier"), chosen[:, 1:, :], start=False, stop=True).then_inc(s_rank, 1)
            for n in range(TOPK * TT):
                if n % 2 == 0:
                    pe.wait_ge(s_hot, n // 2 + 1)
                if n == 0:
                    pe.wait_ge(s_score, 1)
                ins = pe.matmul(bank[:, 4, 0:3 * PASSES], slot_hot[:, n, :], pass_hot[:, n, :, :], start=(n == 0), stop=(n == TOPK * TT - 1))
            ins.then_inc(s_tabp, 1)
            pe.wait_ge(s_tab, 1)

            def turn(p):
                pe.wait_ge(s_xe, p * 16 + 16)
                pe.wait_ge(s_xeT, p)
                for c in range(4):
                    ins = pe.transpose(bank[:, 2, c * P:(c + 1) * P], xe[:, c * P:(c + 1) * P], C("ident"))
                ins.then_inc(s_xeTp, 1)

            def one_pass(p, b, loads, last):
                pe.wait_ge(s_xeT, p + 1)
                gu = [v.rearrange("p (k h n) -> p k h n", k=2, h=2) for v in w_chunk[b][0:4]]
                for k in range(KT):
                    if k % 2 == 0:
                        pe.wait_ge(s_w[b][k // 2], loads)
                    for h in range(2):
                        ins = pe.matmul(bank[SLOTS * h:SLOTS * h + SLOTS, 0, :], xeT[:, k % 4, SLOTS * (k // 4):SLOTS * (k // 4) + SLOTS],
                                        gu[k // 2][:, k % 2, h, :], start=(k == 0), stop=(k == KT - 1))
                    if k == KT - 1:
                        ins.then_inc(s_hp, 1)
                    elif k % 2 == 1 and last:
                        ins.then_inc(s_used, 1)
                turn(p + 1)
                pe.wait_ge(s_h, p + 1)
                for c in range(2):
                    ins = pe.transpose(bank[:, 3, c * P:(c + 1) * P], h_e[:, c * P:(c + 1) * P], C("ident"))
                ins.then_inc(s_hTp, 1)
                if last:
                    pe.sem_inc(s_used, 1)
                pe.wait_ge(s_hT, p + 1)
                pe.wait_ge(s_yfree, p + 1)
                wd = [v.rearrange("p (f h n) -> p f h n", f=2, h=2) for v in w_chunk[b][4:6]]
                for f in range(4):
                    if f % 2 == 0:
                        pe.wait_ge(s_w[b][4 + f // 2], loads)
                    for h in range(2):
                        ins = pe.matmul(bank[SLOTS * h:SLOTS * h + SLOTS, 1, :], hT[:, f % 2, SLOTS * (f // 2):SLOTS * (f // 2) + SLOTS],
                                        wd[f // 2][:, f % 2, h, :], start=(f == 0), stop=(f == 3))
                    if f == 1 and last:
                        ins.then_inc(s_used, 1)
                ins.then_inc(s_yp, 1)

            turn(0)
            pe.wait_ge(s_first, 1)
            pe.sem_inc(s_yp, 1)

            def expert(e, b, loads):
                extra = pe.value_load(extra_i[0:1, bass.ds(e, 1)], min_val=0, max_val=MORE)
                first = pe.value_load(first_i[0:1, bass.ds(e, 1)], min_val=0, max_val=PASSES - 2)
                pe.wait_ge(s_yp, first + 1)
                pe.sem_inc(s_used, 1)
                with pe.If(extra > 0):
                    with pe.Fori(0, extra) as n:
                        one_pass(first + n, b, loads, False)
                one_pass(first + extra, b, loads, True)

            with pe.Fori(0, N_EXP // SETS) as i:
                for b in range(SETS):
                    expert(pe.snap(i * SETS + b, min_val=0, max_val=N_EXP - 1), b, i * 16 + 16)
            for e in range(N_EXP // SETS * SETS, N_EXP):
                expert(e, e % SETS, 16 * (e // SETS + 1))


def tiles_of(v):
    return v.reshape(-1, P).T


def kernel(**inputs):
    import concourse.bacc as bacc
    from concourse.bass_utils import run_bass_kernel_spmd

    a = {k: np.asarray(v) for k, v in inputs.items()}
    mu = a["rwkv_mu"][0]
    cols = [tiles_of(mu[0:3 * RW])]
    for at, n in ((OFF_WL, LORA_W + LORA_A), (OFF_GL, LORA_G)):
        col = np.zeros((P, 1), np.float32)
        col[:n, 0] = mu[at:at + n]
        cols.append(col)
    for name in ("rwkv_w0", "rwkv_a0", "rwkv_k_k", "rwkv_k_a", "rwkv_r_k", "rwkv_gn_g", "rwkv_gn_b", "conv_db", "conv_ln_g", "conv_ln_b"):
        cols.append(tiles_of(a[name][0].reshape(-1)))
    dw = a["conv_dw"][0]
    cols += [dw[:, P * i:P * i + P].T for i in range(2)]
    lora = np.zeros((P, 2, RW), np.float32)
    lora[0:LORA_W, 0] = a["rwkv_w_up"][0]
    lora[LORA_W:LORA_W + LORA_A, 0] = a["rwkv_a_up"][0]
    lora[0:LORA_G, 1] = a["rwkv_g_up"][0]
    arrays = {
        "x_tok": a["x"][0],
        "xT": a["x"][0].T.reshape(KT, P, T).transpose(1, 0, 2),
        "w_in": a["w_in_first"],
        "par": np.concatenate(cols, 1),
        "table": TABLE,
        "lora": lora,
        "rows": np.concatenate([a[n].reshape(-1) for n in ("sgu_ln_g", "sgu_ln_b", "ln1_g", "ln1_b", "ln2_g", "ln2_b", "router_b")])[None],
        "sgu_b": a["sgu_b"][0],
        "sgu_wT": a["sgu_w"][0].transpose(2, 0, 1),
        "w_o": np.concatenate([a["rwkv_w_o"][0], a["sgu_w_o"][0], a["conv_w_o"][0]], 0),
        "w_out": a["w_out"][0],
        "router_w": a["router_w"],
        "zeros": np.zeros((SLOTS, D), np.float32),
        "w_gu": np.stack([a[n][0].reshape(N_EXP, KT, P, 2, FE // 2) for n in ("moe_w_gate", "moe_w_up")], 4)
                  .transpose(0, 2, 1, 3, 4, 5).reshape(N_EXP, P, GU),
        "w_down": a["moe_w_down"][0].reshape(N_EXP, FE // P, P, D).transpose(0, 2, 1, 3).reshape(N_EXP, P, WD),
    }
    nc = bacc.Bacc("TRN2", target_bir_lowering=False, num_devices=1)
    aps = []
    for name, v in arrays.items():
        arrays[name] = v = np.ascontiguousarray(v)
        aps.append(nc.dram_tensor(name, v.shape, mybir.dt.from_np(v.dtype), kind="ExternalInput").ap())
    out = nc.dram_tensor("out", (T, D), F32, kind="ExternalOutput").ap()
    program(nc, *aps, out)
    r = run_bass_kernel_spmd(nc, [arrays], core_ids=[0])
    return r.results[0]["out"].reshape(1, T, D)
```
